# Optimizing a Trainium2 kernel written in Bass

```python
import jax, jax.numpy as jnp
from jax import lax
import numpy as np
import math

D_MODEL = 1024
BATCH = 1
SEQ = 256
DEPTH = 1

MIX_WIDTH = D_MODEL
POOL_WIDTH = MIX_WIDTH // 2
POOL_WINDOWS = (2, 4, 8, 16)
N_POOL_GROUPS = len(POOL_WINDOWS)
POOL_GROUP_WIDTH = POOL_WIDTH // N_POOL_GROUPS
ATTN_WIDTH = MIX_WIDTH - POOL_WIDTH
HEAD_DIM = 64
N_HEADS = ATTN_WIDTH // HEAD_DIM
IN_WIDTH = POOL_WIDTH + 3 * ATTN_WIDTH + N_HEADS
D_FF = 4 * D_MODEL
BLOCK_Q = 128
LN_EPS = 1e-5
NEG_INF = -1e30
ALPHA = float((2.0 * DEPTH) ** 0.25)
BETA = float((8.0 * DEPTH) ** -0.25)


def layer_norm(x, g, b):
    xf = x.astype(jnp.float32)
    mu = jnp.mean(xf, axis=-1, keepdims=True)
    var = jnp.mean(jnp.square(xf - mu), axis=-1, keepdims=True)
    y = (xf - mu) * lax.rsqrt(var + LN_EPS)
    return (y * g.astype(jnp.float32) + b.astype(jnp.float32)).astype(x.dtype)

def pool_mixer(u, w, scale):
    B, S, _ = u.shape
    uf = u.astype(jnp.float32)
    c = jnp.cumsum(uf, axis=1)
    pos = jnp.arange(1, S + 1, dtype=jnp.float32)
    diffs = []
    for g, win in enumerate(POOL_WINDOWS):
        sl = slice(g * POOL_GROUP_WIDTH, (g + 1) * POOL_GROUP_WIDTH)
        cg = c[..., sl]
        shifted = jnp.pad(cg, ((0, 0), (win, 0), (0, 0)))[:, :S]
        count = jnp.minimum(pos, float(win))[None, :, None]
        diffs.append((cg - shifted) / count - uf[..., sl])
    d = jnp.concatenate(diffs, axis=-1).astype(u.dtype)
    d = d.reshape(B, S, N_POOL_GROUPS, POOL_GROUP_WIDTH)
    y = jnp.einsum('bsgc,gcd->bsgd', d, w).reshape(B, S, POOL_WIDTH)
    return y * scale

def forgetting_attention(q, k, v, f_logit):
    B, S, _ = q.shape
    to_heads = lambda t: t.reshape(B, S, N_HEADS, HEAD_DIM).transpose(0, 2, 1, 3)
    q, k, v = to_heads(q), to_heads(k), to_heads(v)
    log_f = jax.nn.log_sigmoid(f_logit.astype(jnp.float32)).transpose(0, 2, 1)
    cf = jnp.cumsum(log_f, axis=-1)
    scale = HEAD_DIM ** -0.5
    kpos = jnp.arange(S)
    n_blocks = S // BLOCK_Q

    def one_block(i):
        start = i * BLOCK_Q
        qb = lax.dynamic_slice_in_dim(q, start, BLOCK_Q, axis=2)
        cq = lax.dynamic_slice_in_dim(cf, start, BLOCK_Q, axis=2)
        qpos = start + jnp.arange(BLOCK_Q)
        s = jnp.einsum('bhqd,bhkd->bhqk', qb, k, preferred_element_type=jnp.float32) * scale
        s = s + cq[..., :, None] - cf[..., None, :]
        s = jnp.where(kpos[None, :] <= qpos[:, None], s, NEG_INF)
        p = jax.nn.softmax(s, axis=-1)
        return jnp.einsum('bhqk,bhkd->bhqd', p.astype(v.dtype), v)

    out = lax.map(one_block, jnp.arange(n_blocks))
    out = out.transpose(1, 0, 3, 2, 4).reshape(B, S, ATTN_WIDTH)
    return out

def hybrid_mixer(x, w_in, b_f, pool_w, pool_scale, w_out):
    h = x @ w_in
    o = 0
    u = h[..., o:o + POOL_WIDTH]; o += POOL_WIDTH
    q = h[..., o:o + ATTN_WIDTH]; o += ATTN_WIDTH
    k = h[..., o:o + ATTN_WIDTH]; o += ATTN_WIDTH
    v = h[..., o:o + ATTN_WIDTH]; o += ATTN_WIDTH
    f_logit = h[..., o:o + N_HEADS] + b_f
    pool_out = pool_mixer(u, pool_w, pool_scale)
    attn_out = forgetting_attention(q, k, v, f_logit)
    return jnp.concatenate([pool_out, attn_out], axis=-1) @ w_out

def first_inputs(seed: int = 0) -> dict:
    key = jax.random.key(seed)
    ks = jax.random.split(key, 12)
    f32 = jnp.float32
    x = jax.random.normal(ks[0], (BATCH, SEQ, D_MODEL), f32)
    w_in = jax.random.normal(ks[1], (DEPTH, D_MODEL, IN_WIDTH), f32) * D_MODEL ** -0.5
    col_scale = np.ones((IN_WIDTH,), np.float32)
    col_scale[:POOL_WIDTH] = BETA
    col_scale[POOL_WIDTH + 2 * ATTN_WIDTH:POOL_WIDTH + 3 * ATTN_WIDTH] = BETA
    w_in = w_in * jnp.asarray(col_scale)
    b_f = 3.0 + 0.5 * jax.random.normal(ks[2], (DEPTH, N_HEADS), f32)
    pool_w = jax.random.normal(ks[3], (DEPTH, N_POOL_GROUPS, POOL_GROUP_WIDTH, POOL_GROUP_WIDTH), f32) * POOL_GROUP_WIDTH ** -0.5
    pool_scale = 1.0 + 0.1 * jax.random.normal(ks[4], (DEPTH, POOL_WIDTH), f32)
    w_out = jax.random.normal(ks[5], (DEPTH, MIX_WIDTH, D_MODEL), f32) * (MIX_WIDTH ** -0.5 * BETA)
    ln1_g = 1.0 + 0.05 * jax.random.normal(ks[6], (DEPTH, D_MODEL), f32)
    ln1_b = 0.02 * jax.random.normal(ks[7], (DEPTH, D_MODEL), f32)
    w_mlp1 = jax.random.normal(ks[8], (DEPTH, D_MODEL, D_FF), f32) * D_MODEL ** -0.5
    w_mlp2 = jax.random.normal(ks[9], (DEPTH, D_FF, D_MODEL), f32) * (D_FF ** -0.5 * BETA)
    ln2_g = 1.0 + 0.05 * jax.random.normal(ks[10], (DEPTH, D_MODEL), f32)
    ln2_b = 0.02 * jax.random.normal(ks[11], (DEPTH, D_MODEL), f32)
    return {"x": x, "w_in": w_in, "b_f": b_f, "pool_w": pool_w, "pool_scale": pool_scale,
            "w_out": w_out, "ln1_g": ln1_g, "ln1_b": ln1_b, "w_mlp1": w_mlp1,
            "w_mlp2": w_mlp2, "ln2_g": ln2_g, "ln2_b": ln2_b}

def first_block(x, w_in, b_f, pool_w, pool_scale, w_out, ln1_g, ln1_b, w_mlp1, w_mlp2, ln2_g, ln2_b):
    for l in range(DEPTH):
        mix = hybrid_mixer(x, w_in[l], b_f[l], pool_w[l], pool_scale[l], w_out[l])
        x = layer_norm(ALPHA * x + mix, ln1_g[l], ln1_b[l])
        hid = jnp.square(jax.nn.relu(x @ w_mlp1[l]))
        x = layer_norm(ALPHA * x + hid @ w_mlp2[l], ln2_g[l], ln2_b[l])
    return x


DEPTH_2 = 2

N_MIXERS = 4
EPS = 1e-6
D_FF_2 = 2816
REL_BUCKETS = 32
REL_MAX_DIST = 2048
REL_HEADS = 8
A_HEADS = 8
A_HEAD_DIM = D_MODEL // A_HEADS
IDX_HEADS = 8
IDX_DIM = 64
TOPK_MAX = 256
Q_BLOCK = 128
A_SPLITS = (D_MODEL, 2 * D_MODEL, 3 * D_MODEL,
            3 * D_MODEL + IDX_HEADS * IDX_DIM,
            3 * D_MODEL + IDX_HEADS * IDX_DIM + IDX_DIM)
A_IN = 3 * D_MODEL + IDX_HEADS * IDX_DIM + IDX_DIM + IDX_HEADS
B_CHUNK = 128
B_HALF = 3 * D_MODEL
B_GROUPS = 8
C_KERNEL = 31
D_PAIRS = ((128, 1), (512, 4), (2048, 16))
D_NGROUPS = len(D_PAIRS)
D_HEADS = 8
D_HEAD_DIM = 64
D_BLOCK = 128
D_SPAN = D_BLOCK * max(dil for _, dil in D_PAIRS)
D_IN = 3 * D_NGROUPS * D_HEADS * D_HEAD_DIM
D_OUT = D_HEADS * D_HEAD_DIM

def n_uses(m):
    return (DEPTH_2 - m + N_MIXERS - 1) // N_MIXERS


def rmsnorm(x, g):
    xf = x.astype(jnp.float32)
    y = xf * lax.rsqrt(jnp.mean(xf * xf, axis=-1, keepdims=True) + EPS)
    return (y * g.astype(jnp.float32)).astype(x.dtype)

def layernorm(x, g, b):
    xf = x.astype(jnp.float32)
    mu = jnp.mean(xf, axis=-1, keepdims=True)
    var = jnp.mean(jnp.square(xf - mu), axis=-1, keepdims=True)
    y = (xf - mu) * lax.rsqrt(var + EPS)
    return (y * g.astype(jnp.float32) + b.astype(jnp.float32)).astype(x.dtype)

def swiglu(x, w_in, w_out):
    gate, up = jnp.split(x @ w_in, 2, axis=-1)
    return (jax.nn.silu(gate) * up) @ w_out

def rel_bucket(dist):
    max_exact = REL_BUCKETS // 2
    d = jnp.maximum(dist, 0)
    df = jnp.maximum(d, 1).astype(jnp.float32)
    large = max_exact + (jnp.log(df / max_exact) / math.log(REL_MAX_DIST / max_exact)
                         * (REL_BUCKETS - max_exact)).astype(jnp.int32)
    large = jnp.minimum(large, REL_BUCKETS - 1)
    return jnp.where(d < max_exact, d, large)

def mixer_a(h, w_in, w_out, rel_table):
    B_, S, _ = h.shape
    q, k, v, qi, ki, wi = jnp.split(h @ w_in, A_SPLITS, axis=-1)
    q = q.reshape(B_, S, A_HEADS, A_HEAD_DIM)
    k = k.reshape(B_, S, A_HEADS, A_HEAD_DIM)
    v = v.reshape(B_, S, A_HEADS, A_HEAD_DIM)
    qi = qi.reshape(B_, S, IDX_HEADS, IDX_DIM)
    wi = wi * (IDX_HEADS ** -0.5)
    top_k = min(TOPK_MAX, S // 4)
    nb = S // Q_BLOCK
    key_pos = jnp.arange(S)
    scale = A_HEAD_DIM ** -0.5
    gather = jax.vmap(lambda arr, ix: arr[ix])

    def block(i):
        start = i * Q_BLOCK
        q_pos = start + jnp.arange(Q_BLOCK)
        qb = lax.dynamic_slice_in_dim(q, start, Q_BLOCK, axis=1)
        qib = lax.dynamic_slice_in_dim(qi, start, Q_BLOCK, axis=1)
        wib = lax.dynamic_slice_in_dim(wi, start, Q_BLOCK, axis=1)
        rel = jax.nn.relu(jnp.einsum('bthd,bsd->bths', qib, ki).astype(jnp.float32) * (IDX_DIM ** -0.5))
        score = jnp.einsum('bth,bths->bts', wib.astype(jnp.float32), rel)
        causal = key_pos[None, :] <= q_pos[:, None]
        score = jnp.where(causal[None], score, -jnp.inf)
        _, idx = lax.top_k(score, top_k)
        valid = idx <= q_pos[None, :, None]
        kg = gather(k, idx)
        vg = gather(v, idx)
        bias = rel_table[rel_bucket(q_pos[None, :, None] - idx)]
        logits = (jnp.einsum('bthe,btkhe->bhtk', qb, kg).astype(jnp.float32) * scale
                  + jnp.transpose(bias, (0, 3, 1, 2)).astype(jnp.float32))
        logits = jnp.where(valid[:, None], logits, -jnp.inf)
        p = jax.nn.softmax(logits, axis=-1)
        o = jnp.einsum('bhtk,btkhe->bthe', p, vg)
        return o.reshape(B_, Q_BLOCK, D_MODEL)

    out = lax.map(block, jnp.arange(nb))
    out = jnp.transpose(out, (1, 0, 2, 3)).reshape(B_, S, D_MODEL).astype(h.dtype)
    return out @ w_out

def mixer_b(h, w_in, b_in, ln_g, ln_b, w_sp, b_sp, w_out):
    B_, S, _ = h.shape
    z = jax.nn.gelu(h @ w_in + b_in)
    u, v = jnp.split(z, 2, axis=-1)
    v = layernorm(v, ln_g, ln_b)
    nc = S // B_CHUNK
    v = v.reshape(B_, nc, B_CHUNK, B_GROUPS, B_HALF // B_GROUPS)
    tri = jnp.tril(jnp.ones((B_CHUNK, B_CHUNK), dtype=bool))
    w = jnp.where(tri[None], w_sp, jnp.zeros((), w_sp.dtype))
    sv = jnp.einsum('gts,bcsgd->bctgd', w, v) + jnp.transpose(b_sp)[None, None, :, :, None]
    y = u * sv.reshape(B_, S, B_HALF)
    return y @ w_out

def mixer_c(h, w_pw1, b_pw1, w_dw, b_dw, ln_g, ln_b, w_pw2, b_pw2):
    a, g = jnp.split(h @ w_pw1 + b_pw1, 2, axis=-1)
    y = a * jax.nn.sigmoid(g)
    y = lax.conv_general_dilated(y, w_dw[:, None, :], window_strides=(1,),
                                 padding=((C_KERNEL - 1, 0),),
                                 dimension_numbers=('NWC', 'WIO', 'NWC'),
                                 feature_group_count=D_MODEL) + b_dw
    y = jax.nn.silu(layernorm(y, ln_g, ln_b))
    return y @ w_pw2 + b_pw2

def dilated_group(q, k, v, window, dil, rel_table):
    B_, Sp, H, E = q.shape
    n = Sp // dil
    nb = n // D_BLOCK

    def to_sub(t):
        t = jnp.swapaxes(t.reshape(B_, n, dil, H, E), 1, 2)
        return t.reshape(B_, dil, nb, D_BLOCK, H, E)

    def band(t):
        prev = jnp.pad(t, ((0, 0), (0, 0), (1, 0), (0, 0), (0, 0), (0, 0)))[:, :, :-1]
        return jnp.concatenate([prev, t], axis=3)

    qs = to_sub(q)
    kb = band(to_sub(k))
    vb = band(to_sub(v))
    steps = window // dil
    p_loc = jnp.arange(D_BLOCK)[:, None]
    j_loc = jnp.arange(2 * D_BLOCK)[None, :]
    m = p_loc + D_BLOCK - j_loc
    in_win = (m >= 0) & (m <= steps)
    first = (jnp.arange(nb) == 0)[:, None, None] & (j_loc < D_BLOCK)[None]
    mask = in_win[None] & ~first
    bias = jnp.transpose(rel_table[rel_bucket(m * dil)], (2, 0, 1)).astype(jnp.float32)
    logits = jnp.einsum('brnqhe,brnkhe->brnhqk', qs, kb).astype(jnp.float32) * (E ** -0.5) + bias
    logits = jnp.where(mask[None, None, :, None], logits, -jnp.inf)
    mx = jnp.max(logits, axis=-1, keepdims=True)
    e = jnp.exp(logits - mx)
    l = jnp.sum(e, axis=-1, keepdims=True)
    o = jnp.einsum('brnhqk,brnkhe->brnqhe', e / l, vb)
    lse = jnp.swapaxes((mx + jnp.log(l))[..., 0], -1, -2)

    def from_sub(t):
        rest = t.shape[4:]
        t = t.reshape((B_, dil, n) + rest)
        return jnp.swapaxes(t, 1, 2).reshape((B_, Sp) + rest)

    return from_sub(o), from_sub(lse)

def mixer_d(h, w_in, w_out, rel_table):
    B_, S, _ = h.shape
    Sp = -(-S // D_SPAN) * D_SPAN
    proj = jnp.pad(h @ w_in, ((0, 0), (0, Sp - S), (0, 0)))
    proj = proj.reshape(B_, Sp, 3, D_NGROUPS, D_HEADS, D_HEAD_DIM)
    outs, lses = [], []
    for g, (window, dil) in enumerate(D_PAIRS):
        o, lse = dilated_group(proj[:, :, 0, g], proj[:, :, 1, g], proj[:, :, 2, g],
                               window, dil, rel_table)
        outs.append(o)
        lses.append(lse)
    alpha = jax.nn.softmax(jnp.stack(lses, 0), axis=0)
    y = jnp.sum(alpha[..., None] * jnp.stack(outs, 0), axis=0)
    y = y[:, :S].reshape(B_, S, D_OUT).astype(h.dtype)
    return y @ w_out

def second_inputs(seed: int = 0) -> dict:
    key = jax.random.key(seed)
    ks = jax.random.split(key, 32)
    nrm = lambda k, shape, s: jax.random.normal(k, shape, jnp.float32) * s
    nA, nB, nC, nD = n_uses(0), n_uses(1), n_uses(2), n_uses(3)
    D = D_MODEL
    return {
        "x": nrm(ks[0], (BATCH, SEQ, D), 1.0),
        "norm_g": 1.0 + nrm(ks[1], (DEPTH_2, 3, D), 0.05),
        "final_g": 1.0 + nrm(ks[2], (D,), 0.05),
        "ffn_w_in": nrm(ks[3], (DEPTH_2, 2, D, 2 * D_FF_2), D ** -0.5),
        "ffn_w_out": nrm(ks[4], (DEPTH_2, 2, D_FF_2, D), D_FF_2 ** -0.5),
        "rel_table": nrm(ks[5], (REL_BUCKETS, REL_HEADS), 0.5),
        "a_w_in": nrm(ks[6], (nA, D, A_IN), D ** -0.5),
        "a_w_out": nrm(ks[7], (nA, D, D), D ** -0.5),
        "b_w_in": nrm(ks[8], (nB, D, 2 * B_HALF), D ** -0.5),
        "b_b_in": nrm(ks[9], (nB, 2 * B_HALF), 0.02),
        "b_ln_g": 1.0 + nrm(ks[10], (nB, B_HALF), 0.05),
        "b_ln_b": nrm(ks[11], (nB, B_HALF), 0.02),
        "b_w_sp": nrm(ks[12], (nB, B_GROUPS, B_CHUNK, B_CHUNK), B_CHUNK ** -0.5),
        "b_b_sp": 1.0 + nrm(ks[13], (nB, B_GROUPS, B_CHUNK), 0.05),
        "b_w_out": nrm(ks[14], (nB, B_HALF, D), B_HALF ** -0.5),
        "c_w_pw1": nrm(ks[15], (nC, D, 2 * D), D ** -0.5),
        "c_b_pw1": nrm(ks[16], (nC, 2 * D), 0.02),
        "c_w_dw": nrm(ks[17], (nC, C_KERNEL, D), C_KERNEL ** -0.5),
        "c_b_dw": nrm(ks[18], (nC, D), 0.02),
        "c_ln_g": 1.0 + nrm(ks[19], (nC, D), 0.05),
        "c_ln_b": nrm(ks[20], (nC, D), 0.02),
        "c_w_pw2": nrm(ks[21], (nC, D, D), D ** -0.5),
        "c_b_pw2": nrm(ks[22], (nC, D), 0.02),
        "d_w_in": nrm(ks[23], (nD, D, D_IN), D ** -0.5),
        "d_w_out": nrm(ks[24], (nD, D_OUT, D), D_OUT ** -0.5),
    }

def second_block(x, norm_g, final_g, ffn_w_in, ffn_w_out, rel_table,
              a_w_in, a_w_out,
              b_w_in, b_b_in, b_ln_g, b_ln_b, b_w_sp, b_b_sp, b_w_out,
              c_w_pw1, c_b_pw1, c_w_dw, c_b_dw, c_ln_g, c_ln_b, c_w_pw2, c_b_pw2,
              d_w_in, d_w_out):
    h = x
    for i in range(DEPTH_2):
        kind, j = i % N_MIXERS, i // N_MIXERS
        h = h + 0.5 * swiglu(rmsnorm(h, norm_g[i, 0]), ffn_w_in[i, 0], ffn_w_out[i, 0])
        hn = rmsnorm(h, norm_g[i, 1])
        if kind == 0:
            y = mixer_a(hn, a_w_in[j], a_w_out[j], rel_table)
        elif kind == 1:
            y = mixer_b(hn, b_w_in[j], b_b_in[j], b_ln_g[j], b_ln_b[j], b_w_sp[j], b_b_sp[j], b_w_out[j])
        elif kind == 2:
            y = mixer_c(hn, c_w_pw1[j], c_b_pw1[j], c_w_dw[j], c_b_dw[j], c_ln_g[j], c_ln_b[j],
                        c_w_pw2[j], c_b_pw2[j])
        else:
            y = mixer_d(hn, d_w_in[j], d_w_out[j], rel_table)
        h = h + y
        h = h + 0.5 * swiglu(rmsnorm(h, norm_g[i, 2]), ffn_w_in[i, 1], ffn_w_out[i, 1])
    return rmsnorm(h, final_g)


def setup_inputs(seed=0):
    out = dict(first_inputs(seed))
    for name, value in second_inputs(seed + 1).items():
        if name != "x":
            out[name + "_2"] = value
    return out


def reference(
    x, w_in, b_f, pool_w, pool_scale, w_out, ln1_g, ln1_b, w_mlp1, w_mlp2, ln2_g, ln2_b,
    norm_g_2, final_g_2, ffn_w_in_2, ffn_w_out_2, rel_table_2, a_w_in_2, a_w_out_2, b_w_in_2,
    b_b_in_2, b_ln_g_2, b_ln_b_2, b_w_sp_2, b_b_sp_2, b_w_out_2, c_w_pw1_2, c_b_pw1_2, c_w_dw_2,
    c_b_dw_2, c_ln_g_2, c_ln_b_2, c_w_pw2_2, c_b_pw2_2, d_w_in_2, d_w_out_2,
):
    x = first_block(
        x, w_in, b_f, pool_w, pool_scale, w_out, ln1_g, ln1_b, w_mlp1, w_mlp2, ln2_g, ln2_b,
    )
    return second_block(
        x, norm_g_2, final_g_2, ffn_w_in_2, ffn_w_out_2, rel_table_2, a_w_in_2, a_w_out_2,
        b_w_in_2, b_b_in_2, b_ln_g_2, b_ln_b_2, b_w_sp_2, b_b_sp_2, b_w_out_2, c_w_pw1_2,
        c_b_pw1_2, c_w_dw_2, c_b_dw_2, c_ln_g_2, c_ln_b_2, c_w_pw2_2, c_b_pw2_2, d_w_in_2,
        d_w_out_2,
    )


_drawn_inputs = setup_inputs


def setup_inputs(seed=0):
    import zlib

    import numpy as np

    out = dict(_drawn_inputs(seed))
    spreads = {}
    factors = {'b_b_in_2': 3.995, 'b_ln_g_2': 3.398, 'b_ln_b_2': 8.0, 'b_b_sp_2': 3.303}
    for name, (base, spread) in spreads.items():
        noise = np.random.default_rng([zlib.crc32(name.encode()), seed]).standard_normal(out[name].shape)
        drawn = base * np.exp(spread * noise) if base else spread * noise
        out[name] = __import__('jax').numpy.asarray(drawn.astype(out[name].dtype))
    for name, factor in factors.items():
        out[name] = (out[name] * factor).astype(out[name].dtype)
    return out
```

```python
from collections import namedtuple
from contextlib import ExitStack

import numpy as np

import concourse.bass as bass
from concourse import mybir

F32 = mybir.dt.float32
F32R = mybir.dt.float32r
ACT = mybir.ActivationFunctionType
ALU = mybir.AluOpType
AX_X = mybir.AxisListType.X

P = 128
SEQ = 256
TT = SEQ // P
D = 1024
KD = D // P
N = 512
SLAB = 2048
RAW = 3
RING = 6
VW = 1024
VRING = 3
WIDTH = 512
HEADS = 8
DH1, DH2 = 64, 128
DI = 64
DFF1, DFF2, HALF_B = 4096, 2816, 3072
GROUP_B = HALF_B // 8
TOPK = 64
WINDOWS = (2, 4, 8, 16)
ALPHA = float(2.0 ** 0.25)
LN_EPS, EPS = 1e-5, 1e-6
MASKED, TAKEN = -1e30, -3e38
BUCKETS, MAX_DIST = 32, 2048
DISTS = 384

VECTORS = (["ln1_g", "ln1_b", "ln2_g", "ln2_b"] + [f"norm{i}" for i in range(5)]
           + [f"bias_v{j}" for j in range(3)]
           + [f"{w}{j}" for j in range(3) for w in ("gate_g", "gate_b", "bias_u")]
           + ["norm5", "final"])


def column_slabs(w, cols):
    part = w[:, cols].reshape(2, 4, P, N)
    return part.transpose(0, 2, 1, 3).reshape(2, P, SLAB)


def row_slabs(w):
    return w.reshape(-1, 2, P, D).transpose(0, 2, 1, 3).reshape(-1, P, SLAB)


def wide_slab(w):
    out = np.zeros((KD, P, 256), w.dtype)
    out[:, :, :w.shape[1]] = w.reshape(KD, P, -1)
    return out.transpose(1, 0, 2).reshape(1, P, SLAB)


def fused_slabs(up, down, width, chunks, cols):
    rows = row_slabs(down).reshape(chunks, width // 256, P, SLAB)
    out = []
    for c in range(chunks):
        out.append(column_slabs(up, cols(c)))
        if c:
            out.append(rows[c - 1])
    return np.concatenate(out + [rows[chunks - 1]])


class Splits:

    def __init__(self, one, total):
        self.next, self.one, self.total = 0, one, total

    def upto(self, end):
        while self.next < min(end, self.total):
            self.one(self.next)
            self.next += 1


def spread(ap, dims):
    return bass.AP(tensor=ap.tensor, offset=ap.offset, ap=[ap.ap[0]] + dims)


Fused = namedtuple("Fused", "chunks tiles rows s lead period slabs loads start up down")
Unit = namedtuple("Unit", "kind m i last to factor wait")


def fused_shape(first, end, chunks, tiles):
    rows = tiles // 2
    s = 2 + rows
    period = 2 if s == 3 else 3
    return Fused(
        chunks=chunks, tiles=tiles, rows=rows, s=s, lead=RING - s, period=period,
        slabs=s * period, loads=16 * s * period // RAW,
        start=first + 2 + RING - s,
        up=[first] + [first + 2 + s * c for c in range(chunks)],
        down=[first + 4 + s * c for c in range(chunks - 1)] + [end - rows])


def build(nc, dr):
    with ExitStack() as ctx:
        def sb(name, shape, dt=F32):
            return ctx.enter_context(nc.sbuf_tensor(name, shape, dt))

        def also(name, shape, words):
            return nc.alloc_sbuf_tensor_at(name, shape, F32, offset=nc.sbuf_base - 4 * words)

        def sem(name):
            return ctx.enter_context(nc.semaphore(name))

        def stage(name, signals, first=0, count=0):
            return namedtuple(name, "first end " + signals)(
                first, first + count, *[sem(f"{name}_{s}") for s in signals.split()])

        raw = sb("raw", [P, RAW, SLAB])
        whi = sb("whi", [P, RING, SLAB], F32R)
        wlo = sb("wlo", [P, RING, SLAB], F32R)
        vec = sb("vec", [P, VRING, VW])
        h = sb("h", [P, TT, D])
        xt = sb("xt", [P, 2, KD, SEQ], F32R)
        hid = sb("hid", [P, 2 * N])
        hl = sb("hl", [P, 2, 2, N], F32R)
        hlf = also("hlf", [P, 2, 1024], 2048)
        ht = sb("ht", [P, 2, 2, 4, P], F32R)
        htf = also("htf", [P, 2048], 2048)
        reg = sb("reg", [P, 7168])
        idr = sb("idr", [P, P], F32R)
        idf = sb("idf", [P, P])
        causal = sb("causal", [P, P])
        st = sb("st", [P, 192])
        acc = ctx.enter_context(nc.psum_tensor("acc", [P, 4, N], F32))
        mm = ctx.enter_context(nc.psum_tensor("mm", [P, 2, N], F32))
        tp = ctx.enter_context(nc.psum_tensor("tp", [P, 2, N], F32))

        SQ, RSTD, VAR, MV, BN, WI, BSP, PSC, BF = 0, 2, 4, 6, 10, 82, 98, 106, 110
        CQ, MX, NEG, RS, REC, HALF, TOP = 112, 128, 132, 140, 148, 152, 156
        U1, V1, QT1, KT1, CF, NCF, GZ, GE = 0, 1024, 2048, 3072, 4096, 4352, 4608, 4864
        POOLW, BUCK, TABLE, REL, ONES = 5120, 5632, 6016, 6400, 6656
        QT2, KT2, V2, KI, SCORE, SEL = 0, 2048, 4096, 6144, 6400, 6656
        VB, WSP = 0, 6144

        raw_loaded = [sem(f"raw_loaded{i}") for i in range(RAW)]
        vec_loaded = [sem(f"vec_loaded{i}") for i in range(VRING)]
        hi_done, lo_done, slab_used = sem("hi_done"), sem("lo_done"), sem("slab_used")
        const_loaded, half_set, idr_ready = sem("const_loaded"), sem("half_set"), sem("idr_ready")
        small_loaded, bands_loaded, h_loaded = sem("small_loaded"), sem("bands_loaded"), sem("h_loaded")
        x_loaded, x_hi, x_lo = sem("x_loaded"), sem("x_hi"), sem("x_lo")
        table_ready, table_copied = sem("table_ready"), sem("table_copied")
        table_stored, tables_stored = sem("table_stored"), sem("tables_stored")
        bias_loaded, wsp_loaded, wsp_masked = sem("bias_loaded"), sem("wsp_loaded"), sem("wsp_masked")
        vector_step, stored = sem("vector_step"), sem("stored")
        LAYER = "var_ready eps_added rstd_ready"
        FUSED = "unit_ready gate_ready hid_ready hl_hi hl_ready tp_ready ht_ready acc_ready"
        PROJ = "unit_ready evac"
        ATT = ("sc_ready bias_ready p_ready tp_ready pt_ready pv_ready att_ready "
               "xtp_ready hi_ready xt_ready")
        NORM = "sum_ready sq_ready eps_added rstd_ready xn_ready tp_ready hi_ready xt_ready"
        Norm = namedtuple("Norm", "tiles halves split_to " + NORM)
        norm_sems = [sem(f"norm_{s}") for s in NORM.split()]

        def norm_stage(i, split_to=0):
            return Norm(TT * max(i - 1, 0), 2 * TT * i, split_to, *norm_sems)

        at = [0]

        def slabs(n):
            at[0] += n
            return dict(first=at[0] - n, count=n)

        w_in = stage("w_in", PROJ, **slabs(9))
        gates = stage("gates", "z_ready abs_ready exp_ready ln_ready cf_ready cq_ready cq_copied")
        pool = stage("pool", "d_ready d_copied y_ready y_scaled hi_ready xt_ready")
        att1 = stage("att1", ATT)
        w_out = stage("w_out", "acc_ready", **slabs(4))
        l0 = stage("l0", LAYER)
        mlp = stage("mlp", FUSED, **slabs(4 * (DFF1 // 512)))
        l1 = stage("l1", LAYER)
        ffa = stage("ffa", FUSED, **slabs(3 * (DFF2 // 256)))
        a_in = stage("a_in", PROJ, **slabs(15))
        idx = stage("idx", "rel_ready relu_ready rel_used sel_ready")
        att2 = stage("att2", ATT)
        a_out = stage("a_out", "acc_ready", **slabs(4))
        ffb = stage("ffb", FUSED, **slabs(3 * (DFF2 // 256)))
        ffc = stage("ffc", FUSED, **slabs(3 * (DFF2 // 256)))
        b_in = stage("b_in", PROJ + " gelu_ready", **slabs(12))
        vln = stage("vln", LAYER + " done")
        mixb = stage("mixb", FUSED + " unit_taken mix_ready", **slabs(4 * (HALF_B // 512)))
        ffd = stage("ffd", FUSED, **slabs(3 * (DFF2 // 256)))
        SLABS = at[0]

        f_mlp = fused_shape(mlp.first, mlp.end, DFF1 // 512, 4)
        f_mix = fused_shape(mixb.first, mixb.end, HALF_B // 512, 4)
        f_ffa, f_ffb, f_ffc, f_ffd = (fused_shape(s.first, s.end, DFF2 // 256, 2) for s in (ffa, ffb, ffc, ffd))

        n0, n1, n2, n3, n4, n5, n6, n7 = (norm_stage(i, end) for i, end in enumerate(
            (f_mlp.start, f_ffa.start, ffa.end + RING, f_ffb.start, f_ffc.start, ffc.end + RING,
             f_ffd.start, 0)))

        def unit_list(stg, parts):
            out, m, ready = [], stg.first, 0
            for kind, dest, step, factor in parts:
                for i in range(1 if kind == "wide" else 2):
                    last = kind == "wide" or i == 1
                    ready += not last
                    out.append(Unit(
                        kind=kind, m=m, i=i, last=last, to=dest + i * step, factor=factor,
                        wait=(slab_used, m + (1 if kind == "wide" else 2)) if last
                        else (stg.unit_ready, ready)))
                m += 1 if kind == "wide" else 2
            assert m == stg.end
            return out

        IN_UNITS = unit_list(w_in, [("wide", 0, 0, None), ("tokens", U1, N, None), ("tokens", V1, N, None),
                                    ("turned", QT1, N, DH1 ** -0.5), ("turned", KT1, N, None)])
        A_UNITS = unit_list(a_in, [("tokens", V2, D, None), ("wide", 0, 0, None), ("turned", -1, N, None),
                                   ("tokens", V2 + N, D, None),
                                   ("turned", QT2, N, None), ("turned", QT2 + D, N, None),
                                   ("turned", KT2, N, None), ("turned", KT2 + D, N, None)])
        B_UNITS = unit_list(b_in, [("tokens", VB + c * N, HALF_B, None) for c in range(HALF_B // N)])
        QI_UNIT = 4
        INDEX_AFTER = {6: 0, 8: 1, 10: 2, 12: 3}

        GROUPS = [(t, hh) for t in range(TT) for hh in range(2)]
        ptf, att = hlf[:, 0, :], hlf[:, 1, :]

        def scores_of(g):
            pair = acc[:, 2 * (g % 2):2 * (g % 2) + 2, :].rearrange("p b (i n) -> p (b i) n", i=2)
            return pair[:, :, 0:P * (GROUPS[g][0] + 1)]

        def half_of(head):
            return 64 * (head % 4 // 2), (2 * (head // 4) + head % 2) * SEQ

        def by_head(ap):
            return ap.rearrange("p (i n) -> p i n", i=4)

        def place_of(g):
            return N * g if GROUPS[g][0] == 0 else 0

        def key_blocks(g):
            return sum(t + 1 for t, _ in GROUPS[:g])

        def xn_tile(t):
            return hid[:, :] if t == 0 else hlf[:, 1, :]

        def acc_done(eng, src, t):
            if t == 0:
                eng.wait_ge(src.acc_ready, 1)
            else:
                eng.wait_ge(slab_used, src.end)

        def unit_done(eng, stg, f, c, t, i):
            if t == 0:
                eng.wait_ge(stg.unit_ready, c + 1 + i * f.period)
            else:
                eng.wait_ge(slab_used, f.up[c] + 2 + i * f.slabs)

        def turns(eng, f, first, body):
            c, full = first, (f.chunks - first - (f is f_ffd)) // f.period
            if full > 1:
                with eng.Fori(0, full) as i:
                    for r in range(f.period):
                        body(c + r, i)
                c += full * f.period
            while c < f.chunks:
                body(c, 0)
                c += 1

        block = ctx.enter_context(nc.Block())

        @block.sync
        def _(sp):
            def load(m, i=0):
                if m >= RAW:
                    sp.wait_ge(lo_done, m - RAW + 1 + i * RAW)
                sp.dma_start(raw[:, m % RAW, :], dr["slabs"][m + i * RAW]).then_inc(raw_loaded[m % RAW], 16)

            for m in range(RAW):
                load(m)
            rounds = (SLABS - RAW) // RAW
            with sp.Fori(0, rounds) as i:
                for m in range(RAW, 2 * RAW):
                    load(m, i)
            for m in range(RAW * (rounds + 1), SLABS):
                load(m)
            for t in range(TT):
                sp.wait_ge(n7.xn_ready, n7.halves + 2 * t + 2)
                sp.dma_start(dr["out"][t * P:(t + 1) * P, :], xn_tile(t)).then_inc(stored, 16)
            sp.wait_ge(stored, 16 * TT)

        @block.gpsimd
        def _(pq):
            def load_vec(v, free, count):
                if free is not None:
                    pq.wait_ge(free, count)
                src = dr["vectors"][v]
                pq.dma_start(vec[:, v % VRING, :],
                             bass.AP(tensor=src.tensor, offset=src.offset, ap=[[0, P], [1, VW]]))\
                  .then_inc(vec_loaded[v % VRING], 16)

            def power(n, value, eps, t, ready, base=0):
                pq.wait_ge(ready, base + t + 1)
                nc.gpsimd.tensor_scalar(st[:, VAR + t:VAR + t + 1], st[:, value:value + 1], eps, None,
                                        ALU.add).then_inc(n.eps_added, 1)
                pq.wait_ge(n.eps_added, base + t + 1)
                nc.gpsimd.tensor_tensor(st[:, RSTD + t:RSTD + t + 1], st[:, VAR + t:VAR + t + 1],
                                        st[:, HALF:HALF + 1], ALU.pow).then_inc(n.rstd_ready, 1)

            def rms(n):
                for t in range(TT):
                    power(n, SQ + t, EPS, t, n.sq_ready, n.tiles)

            pq.dma_start(idf[:, :], dr["identity"]).then_inc(const_loaded, 16)
            pq.dma_start(causal[:, :], dr["causal"]).then_inc(const_loaded, 16)
            for place, name in ((reg[0:BUCKETS, BUCK:BUCK + DISTS], "buckets"),
                                (reg[0:BUCKETS, REL:REL + HEADS], "rel_table"),
                                (reg[:, POOLW:POOLW + 4 * P], "pool_w"),
                                (st[:, PSC:PSC + 4], "pool_scale"),
                                (st[0:HEADS, BF:BF + 1], "b_f"),
                                (st[:, BSP:BSP + 8], "b_sp")):
                pq.dma_start(place, dr[name]).then_inc(small_loaded, 16)
            pq.dma_start(h[:, :, :].rearrange("p t d -> p (t d)")[:, 0:12 * P], dr["bands"])\
              .then_inc(bands_loaded, 16)
            nc.gpsimd.memset(st[:, HALF:HALF + 1], -0.5).then_inc(half_set, 1)
            for v in range(VRING):
                load_vec(v, None, 0)
            pq.wait_ge(table_copied, 1)
            pq.dma_start(dr["table"], reg[0:HEADS, TABLE:TABLE + DISTS]).then_inc(table_stored, 16)
            pq.wait_ge(table_stored, 16)
            table, tables = dr["table"], dr["tables"]
            pq.dma_start(tables, bass.AP(tensor=table.tensor, offset=table.offset,
                                         ap=[[0, P], [1, HEADS * DISTS]])).then_inc(tables_stored, 16)
            pq.wait_ge(pool.d_ready, 2)
            for t in range(TT):
                pq.dma_start(h[:, t, :], dr["x"][t * P:(t + 1) * P, :]).then_inc(h_loaded, 16)
            pq.wait_ge(half_set, 1)
            for t in range(TT):
                power(l0, MV + 2 * t + 1, LN_EPS, t, l0.var_ready)
            load_vec(3, n0.xn_ready, n0.halves + 4)
            load_vec(4, n0.xn_ready, n0.halves + 4)
            for t in range(TT):
                power(l1, MV + 2 * t + 1, LN_EPS, t, l1.var_ready)
                power(n1, SQ + t, EPS, t, n1.sq_ready, n1.tiles)
            load_vec(5, n1.sum_ready, n1.tiles + 2)
            load_vec(6, n1.sum_ready, n1.tiles + 2)
            load_vec(7, n1.xn_ready, n1.halves + 4)
            rms(n2)
            load_vec(8, n2.xn_ready, n2.halves + 4)
            pq.wait_ge(tables_stored, 16)
            pq.dma_start(htf[:, :].rearrange("p (i n) -> p i n", i=HEADS),
                         bass.AP(tensor=tables.tensor, offset=tables.offset + P - 1,
                                 ap=[[HEADS * DISTS - 1, P], [DISTS, HEADS], [1, SEQ]]))\
              .then_inc(bias_loaded, 16)
            rms(n3)
            load_vec(9, n3.xn_ready, n3.halves + 4)
            pq.dma_start(reg[:, WSP:WSP + 8 * P], dr["w_sp"]).then_inc(wsp_loaded, 16)
            pq.wait_ge(wsp_loaded, 16)
            w_sp = reg[:, WSP:WSP + 8 * P].rearrange("p (g n) -> p g n", g=8)
            nc.gpsimd.affine_select(out=w_sp, in_=w_sp, compare_op=ALU.is_ge, fill=0.0, base=0,
                                    pattern=[[0, 8], [1, P]], channel_multiplier=-1).then_inc(wsp_masked, 1)
            rms(n4)
            load_vec(10, n4.xn_ready, n4.halves + 4)
            rms(n5)
            load_vec(11, n5.xn_ready, n5.halves + 4)
            for j in range(3):
                load_vec(12 + j, b_in.evac, 4 * j + 4)
            for t in range(TT):
                power(vln, MV + 2 * t + 1, EPS, t, vln.var_ready)
            for j in range(2):
                load_vec(15 + 3 * j, vln.done, j + 1)
                load_vec(16 + 3 * j, vln.done, j + 1)
                load_vec(17 + 3 * j, mixb.unit_taken, 4 * j + 4)
            load_vec(21, vln.done, 3)
            load_vec(22, vln.done, 3)
            rms(n6)
            rms(n7)

        @block.scalar
        def _(act):
            def hi(m, f=None, i=0):
                act.wait_ge(raw_loaded[m % RAW], 16 * (m // RAW + 1) + (i * f.loads if f else 0))
                if m >= RING:
                    act.wait_ge(slab_used, m - RING + 1 + (i * f.slabs if f else 0))
                nc.scalar.activation(whi[:, m % RING, :], raw[:, m % RAW, :], ACT.Copy).then_inc(hi_done, 1)

            splits = Splits(hi, SLABS)

            def tp_to_xt(ready, g, k, t, done):
                act.wait_ge(ready, g + 1)
                nc.scalar.activation(xt[:, 0, k:k + 4, t * P:(t + 1) * P], by_head(tp[:, g % 2, :]),
                                     ACT.Copy).then_inc(done, 1)

            def norm(n, src, squares=True):
                for t in range(TT):
                    if squares:
                        act.wait_ge(n.sum_ready, n.tiles + t + 1)
                        nc.scalar.activation(htf[:, t * D:(t + 1) * D], h[:, t, :], ACT.Square,
                                             scale=D ** -0.5, accum_out=st[:, SQ + t:SQ + t + 1])\
                          .then_inc(n.sq_ready, 1)
                    for j in range(2):
                        tp_to_xt(n.tp_ready, n.halves + 2 * t + j, 4 * j, t, n.hi_ready)
                    if t == 0:
                        splits.upto(n.split_to)

            def fused(stg, f, gate, width):
                def hidden_hi(c, t, i):
                    act.wait_ge(stg.hid_ready, 2 * c + t + 1 + i * 2 * f.period)
                    if c > 0:
                        act.wait_ge(stg.tp_ready, f.rows * (2 * c + t - 1) + i * 2 * f.rows * f.period)
                    nc.scalar.activation(hl[:, t, 0, 0:width], hid[:, t * N:t * N + width], ACT.Copy)\
                      .then_inc(stg.hl_hi, 1)

                def turned(c, t, i):
                    for j in range(f.rows):
                        g = f.rows * (2 * c + t) + j
                        act.wait_ge(stg.tp_ready, g + 1 + i * 2 * f.rows * f.period)
                        nc.scalar.activation(ht[:, t, :, 2 * j:2 * j + 2, :],
                                             tp[:, g % 2, :].rearrange("p (i q n) -> p i q n", i=2, q=2),
                                             ACT.Copy).then_inc(stg.ht_ready, 1)

                def chunk(c, i):
                    m = f.up[c] + f.lead
                    for j in range(min(f.s - 1, SLABS - m)):
                        hi(m + j, f, i)
                    gate(c, 0, i)
                    turned(c - 1, 1, i)
                    hidden_hi(c, 0, i)
                    if m + f.s - 1 < SLABS:
                        hi(m + f.s - 1, f, i)
                    gate(c, 1, i)
                    turned(c, 0, i)
                    hidden_hi(c, 1, i)

                splits.upto(f.start)
                gate(0, 0, 0)
                hidden_hi(0, 0, 0)
                gate(0, 1, 0)
                turned(0, 0, 0)
                hidden_hi(0, 1, 0)
                turns(act, f, 1, chunk)
                splits.next = f.up[f.chunks] + f.lead
                splits.upto(stg.end - f.rows + RING)
                turned(f.chunks - 1, 1, 0)

            def silu_gate(stg, f):
                def gate(c, t, i):
                    unit_done(act, stg, f, c, t, i)
                    nc.scalar.activation(hid[:, t * N:t * N + 256], mm[:, t, 0:256], ACT.Silu)\
                      .then_inc(stg.gate_ready, 1)
                return gate

            def relu_gate(c, t, i):
                unit_done(act, mlp, f_mlp, c, t, i)
                if c > 0:
                    act.wait_ge(mlp.hl_ready, 2 * c + t - 1 + i * 2 * f_mlp.period)
                nc.scalar.activation(hid[:, t * N:(t + 1) * N], mm[:, t, :], ACT.Relu)\
                  .then_inc(mlp.gate_ready, 1)

            def gelu_gate(c, t, i):
                act.wait_ge(mixb.unit_taken, 2 * c + t + 1 + i * 2 * f_mix.period)
                nc.scalar.activation(hid[:, t * N:(t + 1) * N], hid[:, t * N:(t + 1) * N],
                                     ACT.Gelu_apprx_tanh).then_inc(mixb.gate_ready, 1)

            def attention(a, tiles, base, between):
                def exps(g):
                    act.wait_ge(a.bias_ready, g + 1)
                    if g >= 2:
                        act.wait_ge(a.tp_ready, key_blocks(g))
                    keys = P * (GROUPS[g][0] + 1)
                    s = scores_of(g)
                    for i in range(4):
                        r = 4 * (g % 2) + i
                        ins = nc.scalar.activation(
                            hid[:, place_of(g) + i * keys:place_of(g) + (i + 1) * keys],
                            s[:, i, :], ACT.Exp, bias=st[:, NEG + r:NEG + r + 1],
                            accum_out=st[:, RS + r:RS + r + 1])
                    ins.then_inc(a.p_ready, 1)

                def turned(g):
                    if g >= 2:
                        act.wait_ge(a.pv_ready, g)
                    for kb in range(GROUPS[g][0] + 1):
                        n = key_blocks(g) + kb
                        act.wait_ge(a.tp_ready, n + 1)
                        nc.scalar.activation(ptf[:, place_of(g) + kb * N:place_of(g) + (kb + 1) * N],
                                             tp[:, n % 2, :], ACT.Copy).then_inc(a.pt_ready, 1)

                def to_xt(t):
                    for j in range(tiles // 4):
                        tp_to_xt(a.xtp_ready, tiles // 4 * t + j, base + 4 * j, t, a.hi_ready)

                exps(0)
                exps(1)
                between()
                turned(0)
                turned(1)
                exps(2)
                to_xt(0)
                turned(2)
                exps(3)
                turned(3)
                to_xt(1)

            act.dma_start(hlf[:, :, :], dr["x_turned"]).then_inc(x_loaded, 16)
            act.wait_ge(x_loaded, 16)
            nc.scalar.activation(xt[:, 0, :, :].rearrange("p k n -> p (k n)"),
                                 hlf[:, :, :].rearrange("p a n -> p (a n)"), ACT.Copy).then_inc(x_hi, 1)
            act.wait_ge(const_loaded, 32)
            nc.scalar.activation(idr[:, :], idf[:, :], ACT.Copy).then_inc(idr_ready, 1)
            for u in IN_UNITS:
                if u is IN_UNITS[3]:
                    z, e = reg[0:HEADS, GZ:GZ + SEQ], reg[0:HEADS, GE:GE + SEQ]
                    act.wait_ge(gates.z_ready, 1)
                    nc.scalar.activation(e, z, ACT.Abs).then_inc(gates.abs_ready, 1)
                    act.wait_ge(gates.abs_ready, 1)
                    nc.scalar.activation(e, e, ACT.Exp, scale=-1.0).then_inc(gates.exp_ready, 1)
                    act.wait_ge(gates.exp_ready, 1)
                    nc.scalar.activation(e, e, ACT.Ln, bias=1.0).then_inc(gates.ln_ready, 1)
                splits.upto(u.m + RING)

            def pooled():
                act.wait_ge(pool.y_scaled, 4)
                nc.scalar.activation(xt[:, 0, 0:4, :].rearrange("p k n -> p (k n)"), htf[:, 1024:2048],
                                     ACT.Copy).then_inc(pool.hi_ready, 1)
                splits.upto(w_in.end + RING)

            attention(att1, WIDTH // P, WIDTH // P, pooled)
            for j in range(4):
                splits.upto(min(w_out.first + j + RING, f_mlp.start))
            norm(n0, w_out, squares=False)
            fused(mlp, f_mlp, relu_gate, N)
            norm(n1, mlp)
            fused(ffa, f_ffa, silu_gate(ffa, f_ffa), 256)
            norm(n2, ffa)

            def relus(g):
                act.wait_ge(idx.rel_ready, g + 1)
                if g >= 2:
                    act.wait_ge(idx.rel_used, g - 1)
                keys = 4 * P * (GROUPS[g][0] + 1)
                nc.scalar.activation(by_head(hlf[:, g % 2, 0:keys]), scores_of(g), ACT.Relu, scale=DI ** -0.5)\
                  .then_inc(idx.relu_ready, 1)

            for n, u in enumerate(A_UNITS):
                splits.upto(u.m + RING)
                if n in INDEX_AFTER:
                    relus(INDEX_AFTER[n])
            attention(att2, D // P, 0, lambda: splits.upto(a_in.end + RING))
            for j in range(4):
                splits.upto(min(a_out.first + j + RING, f_ffb.start))
            norm(n3, a_out)
            fused(ffb, f_ffb, silu_gate(ffb, f_ffb), 256)
            norm(n4, ffb)
            fused(ffc, f_ffc, silu_gate(ffc, f_ffc), 256)
            norm(n5, ffc)
            for n, u in enumerate(B_UNITS):
                splits.upto(u.m + RING)
                v = reg[:, u.to:u.to + N]
                act.wait_ge(b_in.evac, n + 1)
                nc.scalar.activation(v, v, ACT.Gelu_apprx_tanh).then_inc(b_in.gelu_ready, 1)
            fused(mixb, f_mix, gelu_gate, N)
            norm(n6, mixb)
            fused(ffd, f_ffd, silu_gate(ffd, f_ffd), 256)
            for t in range(TT):
                act.wait_ge(n7.sum_ready, n7.tiles + t + 1)
                nc.scalar.activation(htf[:, t * D:(t + 1) * D], h[:, t, :], ACT.Square, scale=D ** -0.5,
                                     accum_out=st[:, SQ + t:SQ + t + 1]).then_inc(n7.sq_ready, 1)

        @block.vector
        def _(dve):
            steps = [0]

            def step(ins):
                steps[0] += 1
                ins.then_inc(vector_step, 1)
                dve.wait_ge(vector_step, steps[0])

            def lo(m, f=None, i=0):
                dve.wait_ge(hi_done, m + 1 + (i * f.slabs if f else 0))
                nc.vector.tensor_tensor(wlo[:, m % RING, :], raw[:, m % RAW, :], whi[:, m % RING, :],
                                        ALU.subtract).then_inc(lo_done, 1)

            splits = Splits(lo, SLABS)

            def half(t, j):
                return h[:, t, j * N:(j + 1) * N]

            def vec_of(v, width=VW, start=0):
                return vec[:, v % VRING, start:start + width]

            def vec_wait(v):
                dve.wait_ge(vec_loaded[v % VRING], 16 * (v // VRING + 1))

            def tp_to_xt(ready, g, k, t, done):
                dve.wait_ge(ready, g + 1)
                nc.vector.tensor_tensor(xt[:, 1, k:k + 4, t * P:(t + 1) * P], by_head(tp[:, g % 2, :]),
                                        xt[:, 0, k:k + 4, t * P:(t + 1) * P], ALU.subtract).then_inc(done, 1)

            def layer(l, src, t, v):
                acc_done(dve, src, t)
                for j in range(2):
                    step(nc.vector.scalar_tensor_tensor(half(t, j), half(t, j), ALPHA, acc[:, 2 * t + j, :],
                                                        ALU.mult, ALU.add))
                for j in range(2):
                    step(nc.vector.bn_stats(st[:, BN + 6 * j:BN + 6 * j + 6], half(t, j)))
                nc.vector.bn_aggr(st[:, MV + 2 * t:MV + 2 * t + 2],
                                  st[:, BN:BN + 12].rearrange("p (c s) -> p c s", s=6)).then_inc(l.var_ready, 1)
                vec_wait(v)
                dve.wait_ge(l.rstd_ready, t + 1)
                step(nc.vector.tensor_scalar(h[:, t, :], h[:, t, :], st[:, MV + 2 * t:MV + 2 * t + 1],
                                             st[:, RSTD + t:RSTD + t + 1], ALU.subtract, ALU.mult))
                step(nc.vector.tensor_tensor(h[:, t, :], h[:, t, :], vec_of(v), ALU.mult))

            def rms(n, t, v):
                vec_wait(v)
                dve.wait_ge(n.rstd_ready, n.tiles + t + 1)
                for j in range(2):
                    nc.vector.scalar_tensor_tensor(xn_tile(t)[:, j * N:(j + 1) * N], half(t, j),
                                                   st[:, RSTD + t:RSTD + t + 1], vec_of(v, N, j * N),
                                                   ALU.mult, ALU.mult).then_inc(n.xn_ready, 1)

            def add_acc(n, src, t, factor):
                acc_done(dve, src, t)
                for j in range(2):
                    ins = nc.vector.scalar_tensor_tensor(half(t, j), acc[:, 2 * t + j, :], factor, half(t, j),
                                                         ALU.mult, ALU.add)
                ins.then_inc(n.sum_ready, 1)

            def to_xt(n, t):
                for j in range(2):
                    tp_to_xt(n.hi_ready, n.halves + 2 * t + j, 4 * j, t, n.xt_ready)

            def norm(n, src, factor, v):
                for t in range(TT):
                    add_acc(n, src, t, factor)
                    rms(n, t, v)
                    to_xt(n, t)
                    if t == 0:
                        splits.upto(n.split_to)

            def fused(stg, f, unit, width):
                def hidden_lo(c, t, i):
                    dve.wait_ge(stg.hl_hi, 2 * c + t + 1 + i * 2 * f.period)
                    nc.vector.tensor_tensor(hl[:, t, 1, 0:width], hid[:, t * N:t * N + width],
                                            hl[:, t, 0, 0:width], ALU.subtract).then_inc(stg.hl_ready, 1)

                def chunk(c, i):
                    m = f.up[c] + f.lead
                    for j in range(min(f.s - 1, SLABS - m)):
                        lo(m + j, f, i)
                    unit(c, 0, i)
                    hidden_lo(c, 0, i)
                    if m + f.s - 1 < SLABS:
                        lo(m + f.s - 1, f, i)
                    unit(c, 1, i)
                    hidden_lo(c, 1, i)

                splits.upto(f.start)
                for t in range(TT):
                    unit(0, t, 0)
                    hidden_lo(0, t, 0)
                if unit is mixed_unit:
                    for c in range(1, f.chunks):
                        chunk(c, 0)
                else:
                    turns(dve, f, 1, chunk)
                splits.next = f.up[f.chunks] + f.lead
                splits.upto(stg.end - f.rows + RING)

            def gated_unit(stg, f):
                def unit(c, t, i):
                    dve.wait_ge(stg.gate_ready, 2 * c + t + 1 + i * 2 * f.period)
                    x = hid[:, t * N:t * N + 256]
                    nc.vector.tensor_tensor(x, mm[:, t, 256:512], x, ALU.mult).then_inc(stg.hid_ready, 1)
                return unit

            def squared_unit(c, t, i):
                dve.wait_ge(mlp.gate_ready, 2 * c + t + 1 + i * 2 * f_mlp.period)
                x = hid[:, t * N:(t + 1) * N]
                nc.vector.scalar_tensor_tensor(x, mm[:, t, :], 0.0, x, ALU.max, ALU.mult)\
                  .then_inc(mlp.hid_ready, 1)

            def mixed_unit(c, t, i):
                if t == 0 and c % 2 == 0:
                    normalize_v(c // 2)
                v = 14 + 3 * (c // 2)
                vec_wait(v)
                unit_done(dve, mixb, f_mix, c, t, 0)
                if c > 0:
                    dve.wait_ge(mixb.hl_ready, 2 * c + t - 1)
                x = hid[:, t * N:(t + 1) * N]
                nc.vector.tensor_tensor(x, mm[:, 0, :], vec_of(v, N, (c % 2) * N), ALU.add)\
                  .then_inc(mixb.unit_taken, 1)
                dve.wait_ge(mixb.gate_ready, 2 * c + t + 1)
                dve.wait_ge(mixb.mix_ready, 2 * c + t + 1)
                for g, a, b in mix_pieces(c):
                    y = hid[:, t * N + a:t * N + b]
                    ins = nc.vector.scalar_tensor_tensor(y, mm[:, 1, a:b], st[:, BSP + g:BSP + g + 1], y,
                                                         ALU.add, ALU.mult)
                ins.then_inc(mixb.hid_ready, 1)

            def normalize_v(j):
                vec_wait(12 + 3 * j)
                vec_wait(13 + 3 * j)
                for t in range(TT):
                    dve.wait_ge(vln.rstd_ready, t + 1)
                    x = reg[:, VB + t * HALF_B + j * D:VB + t * HALF_B + (j + 1) * D]
                    step(nc.vector.tensor_scalar(x, x, st[:, MV + 2 * t:MV + 2 * t + 1],
                                                 st[:, RSTD + t:RSTD + t + 1], ALU.subtract, ALU.mult))
                    step(nc.vector.tensor_tensor(x, x, vec_of(12 + 3 * j), ALU.mult))
                    ins = nc.vector.tensor_tensor(x, x, vec_of(13 + 3 * j), ALU.add)
                ins.then_inc(vln.done, 1)

            def attention(a, width, tiles, base, post, between):
                def maxima(g):
                    t, hh = GROUPS[g]
                    dve.wait_ge(a.sc_ready, g + 1)
                    s = scores_of(g)
                    post(g, s)
                    if g >= 2:
                        dve.wait_ge(a.p_ready, g - 1)
                    mx, neg = st[:, MX:MX + 4], st[:, NEG + 4 * (g % 2):NEG + 4 * (g % 2) + 4]
                    step(nc.vector.tensor_reduce(mx, s, AX_X, ALU.max))
                    if a is att1:
                        cq = st[:, CQ + 8 * t + 4 * hh:CQ + 8 * t + 4 * hh + 4]
                        step(nc.vector.tensor_tensor(mx, mx, cq, ALU.add))
                        nc.vector.tensor_tensor(neg, cq, mx, ALU.subtract).then_inc(a.bias_ready, 1)
                    else:
                        nc.vector.tensor_scalar(neg, mx, -1.0, None, ALU.mult).then_inc(a.bias_ready, 1)

                def scaled(g):
                    dve.wait_ge(a.pv_ready, g + 1)
                    r = RS + 4 * (g % 2)
                    step(nc.vector.reciprocal(st[:, REC:REC + 4], st[:, r:r + 4]))
                    if g == 2:
                        dve.wait_ge(a.xtp_ready, tiles // 4)
                    hh = GROUPS[g][1]
                    nc.vector.tensor_tensor(by_head(att[:, hh * 4 * width:(hh + 1) * 4 * width]),
                                            by_head(mm[:, g % 2, 0:4 * width]),
                                            spread(st[:, REC:REC + 4], [[1, 4], [0, width]]), ALU.mult)\
                      .then_inc(a.att_ready, 1)
                    dve.wait_ge(a.att_ready, g + 1)

                def turned(t):
                    for j in range(tiles // 4):
                        tp_to_xt(a.hi_ready, tiles // 4 * t + j, base + 4 * j, t, a.xt_ready)

                maxima(0)
                maxima(1)
                between()
                scaled(0)
                maxima(2)
                scaled(1)
                maxima(3)
                turned(0)
                scaled(2)
                scaled(3)
                turned(1)

            def evacuate(stg, n, u):
                dve.wait_ge(*u.wait)
                if u.kind == "wide" and stg is w_in:
                    nc.vector.tensor_scalar(reg[0:HEADS, GZ:GZ + SEQ], mm[0:HEADS, n % 2, 0:SEQ],
                                            st[0:HEADS, BF:BF + 1], None, ALU.add).then_inc(gates.z_ready, 1)
                    return
                if u.kind == "wide":
                    nc.vector.tensor_copy(reg[:, KI:KI + SEQ], mm[:, n % 2, 0:SEQ])
                    nc.vector.tensor_scalar(st[:, WI:WI + 16], mm[:, n % 2, SEQ:SEQ + 16],
                                            HEADS ** -0.5, None, ALU.mult).then_inc(stg.evac, 1)
                    return
                to = hid[:, u.i * N:(u.i + 1) * N] if u.to < N and u.kind == "turned" and u is not None \
                    and stg is a_in and u.m == A_UNITS[QI_UNIT].m else reg[:, u.to:u.to + N]
                if u.factor is None:
                    ins = nc.vector.tensor_copy(to, mm[:, n % 2, :])
                else:
                    ins = nc.vector.tensor_scalar(to, mm[:, n % 2, :], u.factor, None, ALU.mult)
                ins.then_inc(stg.evac, 1)

            dve.wait_ge(x_hi, 1)
            nc.vector.tensor_tensor(xt[:, 1, :, :].rearrange("p k n -> p (k n)"),
                                    hlf[:, :, :].rearrange("p a n -> p (a n)"),
                                    xt[:, 0, :, :].rearrange("p k n -> p (k n)"), ALU.subtract).then_inc(x_lo, 1)
            step(nc.vector.memset(reg[0:HEADS, ONES:ONES + SEQ], 1.0))
            dve.wait_ge(small_loaded, 6 * 16)
            dve.wait_ge(table_ready, 1)
            nc.vector.tensor_copy(reg[0:HEADS, TABLE:TABLE + DISTS], tp[0:HEADS, 1, 0:DISTS])\
              .then_inc(table_copied, 1)
            for n, u in enumerate(IN_UNITS):
                splits.upto(u.m + RING)
                evacuate(w_in, n, u)
                if n == 4:
                    z, e = reg[0:HEADS, GZ:GZ + SEQ], reg[0:HEADS, GE:GE + SEQ]
                    cf = reg[0:HEADS, CF:CF + SEQ]
                    dve.wait_ge(gates.ln_ready, 1)
                    step(nc.vector.scalar_tensor_tensor(z, z, 0.0, e, ALU.min, ALU.subtract))
                    step(nc.vector.tensor_tensor_scan(cf, reg[0:HEADS, ONES:ONES + SEQ], z, 0.0,
                                                      ALU.mult, ALU.add))
                    nc.vector.tensor_scalar(reg[0:HEADS, NCF:NCF + SEQ], cf, -1.0, None, ALU.mult)\
                      .then_inc(gates.cf_ready, 1)
            dve.wait_ge(gates.cq_ready, 1)
            step(nc.vector.tensor_copy(st[:, CQ:CQ + 16], tp[:, 0, 0:16]))
            dve.wait_ge(const_loaded, 32)

            def mask_diagonal(g, s):
                keys = P * (GROUPS[g][0] + 1)
                d = s[:, :, keys - P:keys]
                step(nc.vector.tensor_tensor(d, d, spread(causal[:, :], [[0, 4], [1, P]]), ALU.add))

            def pooled():
                for p in range(2):
                    dve.wait_ge(pool.d_ready, p + 1)
                    nc.vector.tensor_copy(htf[:, p * N:(p + 1) * N], mm[:, p, :]).then_inc(pool.d_copied, 1)
                for p in range(2):
                    dve.wait_ge(pool.y_ready, p + 1)
                    for q in range(2):
                        g = 2 * p + q
                        nc.vector.tensor_scalar(htf[:, D + g * SEQ:D + (g + 1) * SEQ],
                                                mm[:, p, q * SEQ:(q + 1) * SEQ],
                                                st[:, PSC + g:PSC + g + 1], None, ALU.mult)\
                          .then_inc(pool.y_scaled, 1)
                dve.wait_ge(pool.hi_ready, 1)
                nc.vector.tensor_tensor(xt[:, 1, 0:4, :].rearrange("p k n -> p (k n)"), htf[:, D:2 * D],
                                        xt[:, 0, 0:4, :].rearrange("p k n -> p (k n)"), ALU.subtract)\
                  .then_inc(pool.xt_ready, 1)
                splits.upto(w_in.end + RING)

            attention(att1, DH1, WIDTH // P, WIDTH // P, mask_diagonal, pooled)
            for j in range(4):
                splits.upto(min(w_out.first + j + RING, f_mlp.start))
            dve.wait_ge(h_loaded, 16 * TT)
            for t in range(TT):
                layer(l0, w_out, t, 0)
                vec_wait(1)
                for j in range(2):
                    nc.vector.tensor_tensor(half(t, j), half(t, j), vec_of(1, N, j * N), ALU.add)\
                      .then_inc(n0.xn_ready, 1)
                to_xt(n0, t)
                if t == 0:
                    splits.upto(n0.split_to)
            fused(mlp, f_mlp, squared_unit, N)

            for t in range(TT):
                layer(l1, mlp, t, 2)
                vec_wait(3)
                nc.vector.tensor_tensor(h[:, t, :], h[:, t, :], vec_of(3), ALU.add).then_inc(n1.sum_ready, 1)
                rms(n1, t, 4)
                to_xt(n1, t)
                if t == 0:
                    splits.upto(n1.split_to)
            fused(ffa, f_ffa, gated_unit(ffa, f_ffa), 256)
            norm(n2, ffa, 0.5, 5)

            def index(g):
                t, hh = GROUPS[g]
                keys = P * (t + 1)
                score, sel = reg[:, SCORE:SCORE + keys], reg[:, SEL + t * SEQ:SEL + t * SEQ + keys]
                dve.wait_ge(idx.relu_ready, g + 1)
                for i in range(4):
                    rel = hlf[:, g % 2, i * keys:(i + 1) * keys]
                    w = WI + 8 * t + 4 * hh + i
                    if hh == 0 and i == 0:
                        step(nc.vector.tensor_scalar(score, rel, st[:, w:w + 1], 0.0, ALU.mult, ALU.add))
                    elif i < 3:
                        step(nc.vector.scalar_tensor_tensor(score, rel, st[:, w:w + 1], score,
                                                            ALU.mult, ALU.add))
                    else:
                        nc.vector.scalar_tensor_tensor(score, rel, st[:, w:w + 1], score, ALU.mult, ALU.add)\
                          .then_inc(idx.rel_used, 1)
                        dve.wait_ge(idx.rel_used, g + 1)
                if hh == 0:
                    return
                diagonal = reg[:, SCORE + keys - P:SCORE + keys]
                step(nc.vector.tensor_tensor(diagonal, diagonal, causal[:, :], ALU.add))
                for r in range(TOPK // 8):
                    step(nc.vector.max(out=st[:, TOP:TOP + 8], in_=score))
                    step(nc.vector.match_replace(out=score, in_to_replace=st[:, TOP:TOP + 8],
                                                 in_values=score, imm_value=TAKEN))
                step(nc.vector.tensor_scalar(sel, score, TAKEN / 2, MASKED, ALU.is_gt, ALU.mult))
                diagonal = reg[:, SEL + t * SEQ + keys - P:SEL + t * SEQ + keys]
                step(nc.vector.tensor_tensor(diagonal, diagonal, causal[:, :], ALU.add))

            for n, u in enumerate(A_UNITS):
                splits.upto(u.m + RING)
                evacuate(a_in, n, u)
                if n in INDEX_AFTER:
                    index(INDEX_AFTER[n])
            dve.wait_ge(bias_loaded, 16)

            def bias_and_select(g, s):
                t, hh = GROUPS[g]
                keys = P * (t + 1)
                bias = htf[:, :].rearrange("p (i n) -> p i n", i=HEADS)[:, 4 * hh:4 * hh + 4, SEQ - keys:SEQ]
                step(nc.vector.scalar_tensor_tensor(s, s, DH2 ** -0.5, bias, ALU.mult, ALU.add))
                sel = reg[:, SEL + t * SEQ:SEL + t * SEQ + keys]
                step(nc.vector.tensor_tensor(s, s, spread(sel, [[0, 4], [1, keys]]), ALU.add))

            attention(att2, DH2, D // P, 0, bias_and_select, lambda: splits.upto(a_in.end + RING))
            for j in range(4):
                splits.upto(min(a_out.first + j + RING, f_ffb.start))
            norm(n3, a_out, 1.0, 6)
            fused(ffb, f_ffb, gated_unit(ffb, f_ffb), 256)
            norm(n4, ffb, 0.5, 7)
            fused(ffc, f_ffc, gated_unit(ffc, f_ffc), 256)
            norm(n5, ffc, 0.5, 8)

            def stats(n):
                u = B_UNITS[n]
                dve.wait_ge(b_in.gelu_ready, n + 1)
                at = BN + 36 * u.i + 6 * (n // 2)
                return nc.vector.bn_stats(st[:, at:at + 6], reg[:, u.to:u.to + N])

            for n, u in enumerate(B_UNITS):
                splits.upto(u.m + RING)
                vec_wait(9 + n // 4)
                dve.wait_ge(*u.wait)
                nc.vector.tensor_tensor(reg[:, u.to:u.to + N], mm[:, n % 2, :],
                                        vec_of(9 + n // 4, N, (n // 2 % 2) * N), ALU.add).then_inc(b_in.evac, 1)
                if n > 0:
                    stats(n - 1)
            step(stats(len(B_UNITS) - 1))
            for t in range(TT):
                nc.vector.bn_aggr(st[:, MV + 2 * t:MV + 2 * t + 2],
                                  st[:, BN + 36 * t:BN + 36 * t + 36].rearrange("p (c s) -> p c s", s=6))\
                  .then_inc(vln.var_ready, 1)
            fused(mixb, f_mix, mixed_unit, N)
            norm(n6, mixb, 1.0, 21)
            fused(ffd, f_ffd, gated_unit(ffd, f_ffd), 256)
            for t in range(TT):
                add_acc(n7, ffd, t, 0.5)
                rms(n7, t, 22)

        @block.tensor
        def _(pe):
            def product(out, a, b, first, last):
                nc.tensor.matmul(out, a[0], b[0], start=first, stop=False)
                nc.tensor.matmul(out, a[0], b[1], start=False, stop=False)
                return nc.tensor.matmul(out, a[1], b[0], start=False, stop=last)

            def x_tile(k, t):
                return [xt[:, i, k, t * P:(t + 1) * P] for i in range(2)]

            def x_all(k):
                return [xt[:, i, k, :] for i in range(2)]

            def col(m, k, start=0, n=N):
                return [w[:, m % RING, k * N + start:k * N + start + n] for w in (whi, wlo)]

            def row(m, k, half):
                return [w[:, m % RING, k * D + half * N:k * D + (half + 1) * N] for w in (whi, wlo)]

            def wide(m, k, start, n):
                return [w[:, m % RING, k * SEQ + start:k * SEQ + start + n] for w in (whi, wlo)]

            def token_unit(bank, m, t, last, ready, shift=0):
                for k in range(KD):
                    if k % 4 == 0:
                        pe.wait_ge(lo_done, m + k // 4 + 1 + shift)
                    ins = product(mm[:, bank, :], x_tile(k, t), col(m + k // 4, k % 4), k == 0, k == KD - 1)
                    if last and k % 4 == 3:
                        ins.then_inc(slab_used, 1)
                if not last:
                    ins.then_inc(ready, 1)

            def project(stg, n, u):
                if n >= 2:
                    pe.wait_ge(stg.evac, n - 1 - (stg is w_in))
                if n == 2 and stg is w_in:
                    pe.wait_ge(gates.z_ready, 1)
                if u.kind == "tokens":
                    token_unit(n % 2, u.m, u.i, u.last, stg.unit_ready)
                elif u.kind == "turned":
                    for j in range(2):
                        for k in range(KD):
                            if k % 4 == 0:
                                pe.wait_ge(lo_done, u.m + k // 4 + 1)
                            ins = product(mm[:, n % 2, j * SEQ:(j + 1) * SEQ],
                                          col(u.m + k // 4, k % 4, (2 * u.i + j) * P, P), x_all(k),
                                          k == 0, k == KD - 1)
                            if u.last and j == 1 and k % 4 == 3:
                                ins.then_inc(slab_used, 1)
                    if not u.last:
                        ins.then_inc(stg.unit_ready, 1)
                else:
                    pe.wait_ge(lo_done, u.m + 1)
                    for k in range(KD):
                        ins = product(mm[:, n % 2, 0:SEQ], wide(u.m, k, 0, P), x_all(k), k == 0, k == KD - 1)
                    if stg is a_in:
                        for t in range(TT):
                            for k in range(KD):
                                ins = product(mm[:, n % 2, SEQ + 8 * t:SEQ + 8 * t + 8], x_tile(k, t),
                                              wide(u.m, k, P, 8), k == 0, k == KD - 1)
                    ins.then_inc(slab_used, 1)

            def out_slabs(stg):
                n = stg.end - stg.first
                for j in range(n):
                    m = stg.first + j
                    pe.wait_ge(lo_done, m + 1)
                    for t in range(TT):
                        for k in range(2):
                            for half in range(2):
                                ins = product(acc[:, 2 * t + half, :], x_tile(2 * j + k, t), row(m, k, half),
                                              j == 0 and k == 0, j == n - 1 and k == 1)
                        if t == 1:
                            ins.then_inc(slab_used, 1)
                        elif j == n - 1:
                            ins.then_inc(stg.acc_ready, 1)

            def turn_norm(n, t, src=None):
                src = xn_tile(t) if src is None else src
                for j in range(2):
                    g = 2 * t + j
                    pe.wait_ge(n.xn_ready, n.halves + g + 1)
                    if g >= 2:
                        pe.wait_ge(n.xt_ready, n.halves + g - 1)
                    for k in range(4):
                        ins = nc.tensor.transpose(tp[:, g % 2, k * P:(k + 1) * P],
                                                  src[:, (4 * j + k) * P:(4 * j + k + 1) * P], idf[:, :])
                    ins.then_inc(n.tp_ready, 1)

            def fused(stg, f, norm, source=None, spatial=None):
                def up(c, t, i):
                    if c > 0 and spatial is None:
                        pe.wait_ge(stg.hid_ready, 2 * c + t - 1 + i * 2 * f.period)
                    if 2 * c + t > 0 and spatial is not None:
                        pe.wait_ge(stg.unit_taken, 2 * c + t)
                    token_unit(t if spatial is None else 0, f.up[c], t, t == 1, stg.unit_ready, i * f.slabs)
                    if spatial is not None:
                        spatial(c, t)

                def turn(c, t, i):
                    pe.wait_ge(stg.hl_ready, 2 * c + t + 1 + i * 2 * f.period)
                    for j in range(f.rows):
                        g = f.rows * (2 * c + t) + j
                        if g >= 2:
                            pe.wait_ge(stg.ht_ready, g - 1 + i * 2 * f.rows * f.period)
                        for part in range(2):
                            for q in range(2):
                                ins = nc.tensor.transpose(
                                    tp[:, g % 2, (2 * part + q) * P:(2 * part + q + 1) * P].bitcast(F32R),
                                    hl[:, t, part, (2 * j + q) * P:(2 * j + q + 1) * P], idr[:, :])
                        ins.then_inc(stg.tp_ready, 1)

                def down(c, t, i):
                    pe.wait_ge(stg.ht_ready, f.rows * (2 * c + t + 1) + i * 2 * f.rows * f.period)
                    for q in range(f.tiles):
                        m = f.down[c] + q // 2
                        if q % 2 == 0:
                            pe.wait_ge(lo_done, m + 1 + i * f.slabs)
                        for half in range(2):
                            ins = product(acc[:, 2 * t + half, :], [ht[:, t, part, q, :] for part in range(2)],
                                          row(m, q % 2, half), c == 0 and q == 0,
                                          c == f.chunks - 1 and q == f.tiles - 1)
                        if t == 1 and q % 2 == 1:
                            ins.then_inc(slab_used, 1)
                    if c == f.chunks - 1 and t == 0:
                        ins.then_inc(stg.acc_ready, 1)

                def chunk(c, i):
                    up(c, 0, i)
                    turn(c - 1, 1, i)
                    down(c - 1, 0, i)
                    up(c, 1, i)
                    turn(c, 0, i)
                    down(c - 1, 1, i)

                up(0, 0, 0)
                if norm is not None:
                    turn_norm(norm, 1, source)
                    pe.wait_ge(norm.xt_ready, norm.halves + 4)
                up(0, 1, 0)
                turn(0, 0, 0)
                chunk(1, 0)
                if spatial is None:
                    turns(pe, f, 2, chunk)
                else:
                    for c in range(2, f.chunks):
                        chunk(c, 0)
                turn(f.chunks - 1, 1, 0)
                down(f.chunks - 1, 0, 0)
                down(f.chunks - 1, 1, 0)

            def attention(a, score, value, width, between):
                tiles = HEADS * width // P

                def scores(g):
                    t, hh = GROUPS[g]
                    if g >= 2:
                        pe.wait_ge(a.p_ready, g - 1)
                    keys = P * (t + 1)
                    s = scores_of(g)
                    for i in range(4):
                        ins = score(s[:, i, :], t, 4 * hh + i, keys)
                    ins.then_inc(a.sc_ready, 1)

                def values(g):
                    t, hh = GROUPS[g]
                    pe.wait_ge(a.p_ready, g + 1)
                    for kb in range(t + 1):
                        n = key_blocks(g) + kb
                        if n >= 2:
                            pe.wait_ge(a.pt_ready, n - 1)
                        for i in range(4):
                            p = place_of(g) + (i * (t + 1) + kb) * P
                            ins = nc.tensor.transpose(tp[:, n % 2, i * P:(i + 1) * P], hid[:, p:p + P],
                                                      idf[:, :])
                        ins.then_inc(a.tp_ready, 1)
                    pe.wait_ge(a.pt_ready, key_blocks(g + 1) if g < 3 else 6)
                    if g >= 2:
                        pe.wait_ge(a.att_ready, g - 1)
                    for i in range(4):
                        for kb in range(t + 1):
                            p = place_of(g) + kb * N + i * P
                            ins = nc.tensor.matmul(mm[:, g % 2, i * width:(i + 1) * width], ptf[:, p:p + P],
                                                   value(kb, 4 * hh + i), start=kb == 0, stop=kb == t)
                    ins.then_inc(a.pv_ready, 1)

                def turn_att(t):
                    pe.wait_ge(a.att_ready, 2 * t + 2)
                    for j in range(tiles // 4):
                        g = tiles // 4 * t + j
                        if g >= 2:
                            pe.wait_ge(a.xt_ready, g - 1)
                        for k in range(4):
                            ins = nc.tensor.transpose(tp[:, g % 2, k * P:(k + 1) * P],
                                                      att[:, (4 * j + k) * P:(4 * j + k + 1) * P], idf[:, :])
                        ins.then_inc(a.xtp_ready, 1)

                scores(0)
                scores(1)
                between()
                values(0)
                scores(2)
                values(1)
                scores(3)
                turn_att(0)
                pe.wait_ge(a.xt_ready, tiles // 4)
                values(2)
                values(3)
                turn_att(1)
                pe.wait_ge(a.xt_ready, tiles // 2)

            pe.wait_ge(small_loaded, 6 * 16)
            nc.tensor.matmul(tp[0:HEADS, 1, 0:DISTS], reg[0:BUCKETS, REL:REL + HEADS],
                             reg[0:BUCKETS, BUCK:BUCK + DISTS], start=True, stop=True).then_inc(table_ready, 1)
            pe.wait_ge(x_lo, 1)
            for n, u in enumerate(IN_UNITS):
                project(w_in, n, u)
            pe.wait_ge(gates.cf_ready, 1)
            pe.wait_ge(const_loaded, 32)
            for t in range(TT):
                ins = nc.tensor.transpose(tp[:, 0, 8 * t:8 * t + 8], reg[0:HEADS, CF + t * P:CF + (t + 1) * P],
                                          idf[0:HEADS, 0:HEADS])
            ins.then_inc(gates.cq_ready, 1)
            pe.wait_ge(w_in.evac, len(IN_UNITS) - 1)

            def score1(out, t, head, keys):
                r, c = half_of(head)
                nc.tensor.matmul(out, reg[r:r + 64, QT1 + c + t * P:QT1 + c + (t + 1) * P],
                                 reg[r:r + 64, KT1 + c:KT1 + c + keys], start=True, stop=False)
                return nc.tensor.matmul(out, spread(idf[0:HEADS, head:head + 1], [[0, P]]),
                                        reg[0:HEADS, NCF:NCF + keys], start=False, stop=True)

            def pooled():
                pe.wait_ge(bands_loaded, 16)
                band = h[:, :, :].rearrange("p t d -> p (t d)")

                def banded(out, t, kind, g, first, last):
                    b = (4 * kind + g) * P
                    return nc.tensor.matmul(out, reg[:, U1 + t * N + g * P:U1 + t * N + (g + 1) * P],
                                            band[:, b:b + P], start=first, stop=last)

                for p in range(2):
                    for q in range(2):
                        g, o = 2 * p + q, q * SEQ
                        banded(mm[:, p, o:o + P], 0, 0, g, True, True)
                        banded(mm[:, p, o + P:o + SEQ], 1, 1, g, True, False)
                        ins = banded(mm[:, p, o + P:o + SEQ], 0, 2, g, False, True)
                    ins.then_inc(pool.d_ready, 1)
                for p in range(2):
                    pe.wait_ge(pool.d_copied, p + 1)
                    for q in range(2):
                        g = 2 * p + q
                        ins = nc.tensor.matmul(mm[:, p, q * SEQ:(q + 1) * SEQ],
                                               reg[:, POOLW + g * P:POOLW + (g + 1) * P],
                                               htf[:, g * SEQ:(g + 1) * SEQ], start=True, stop=True)
                    ins.then_inc(pool.y_ready, 1)
                pe.wait_ge(pool.y_scaled, 4)

            attention(att1, score1, lambda kb, head: reg[:, V1 + kb * N + head * DH1:
                                                         V1 + kb * N + (head + 1) * DH1], DH1, pooled)
            pe.wait_ge(pool.xt_ready, 1)
            out_slabs(w_out)
            turn_norm(n0, 0, h[:, 0, :])
            pe.wait_ge(n0.xt_ready, n0.halves + 2)
            pe.wait_ge(idr_ready, 1)
            fused(mlp, f_mlp, n0, h[:, 1, :])

            turn_norm(n1, 0)
            pe.wait_ge(n1.xt_ready, n1.halves + 2)
            fused(ffa, f_ffa, n1)
            turn_norm(n2, 0)
            pe.wait_ge(n2.xt_ready, n2.halves + 2)

            def index_scores(g):
                t, hh = GROUPS[g]
                if g == 0:
                    pe.wait_ge(a_in.evac, QI_UNIT + 1)
                if g >= 2:
                    pe.wait_ge(idx.relu_ready, g - 1)
                keys = P * (t + 1)
                for i in range(4):
                    head = 4 * hh + i
                    r, c = half_of(head)
                    ins = nc.tensor.matmul(scores_of(g)[:, i, :],
                                           hid[r:r + 64, c + t * P:c + (t + 1) * P],
                                           reg[r:r + 64, KI:KI + keys], start=True, stop=True)
                ins.then_inc(idx.rel_ready, 1)

            for n, u in enumerate(A_UNITS):
                project(a_in, n, u)
                if n == 0:
                    turn_norm(n2, 1)
                    pe.wait_ge(n2.xt_ready, n2.halves + 4)
                if n in INDEX_AFTER:
                    index_scores(INDEX_AFTER[n])
            pe.wait_ge(a_in.evac, len(A_UNITS))
            pe.wait_ge(idx.relu_ready, 4)

            def score2(out, t, head, keys):
                c = head * SEQ
                return nc.tensor.matmul(out, reg[:, QT2 + c + t * P:QT2 + c + (t + 1) * P],
                                        reg[:, KT2 + c:KT2 + c + keys], start=True, stop=True)

            attention(att2, score2, lambda kb, head: reg[:, V2 + kb * D + head * DH2:
                                                         V2 + kb * D + (head + 1) * DH2], DH2, lambda: None)
            out_slabs(a_out)
            turn_norm(n3, 0)
            pe.wait_ge(n3.xt_ready, n3.halves + 2)
            fused(ffb, f_ffb, n3)
            turn_norm(n4, 0)
            pe.wait_ge(n4.xt_ready, n4.halves + 2)
            fused(ffc, f_ffc, n4)
            turn_norm(n5, 0)
            pe.wait_ge(n5.xt_ready, n5.halves + 2)
            for n, u in enumerate(B_UNITS):
                project(b_in, n, u)
                if n == 0:
                    turn_norm(n5, 1)
                    pe.wait_ge(n5.xt_ready, n5.halves + 4)
            pe.wait_ge(b_in.evac, len(B_UNITS))
            pe.wait_ge(wsp_masked, 1)

            def spatial(c, t):
                pe.wait_ge(vln.done, c // 2 + 1)
                if 2 * c + t > 0:
                    pe.wait_ge(mixb.hid_ready, 2 * c + t)
                for g, a, b in mix_pieces(c):
                    v = VB + t * HALF_B + c * N
                    ins = nc.tensor.matmul(mm[:, 1, a:b], reg[:, WSP + g * P:WSP + (g + 1) * P],
                                           reg[:, v + a:v + b], start=True, stop=True)
                ins.then_inc(mixb.mix_ready, 1)

            fused(mixb, f_mix, None, spatial=spatial)
            turn_norm(n6, 0)
            pe.wait_ge(n6.xt_ready, n6.halves + 2)
            fused(ffd, f_ffd, n6)


def mix_pieces(c):
    out, at = [], c * N
    while at < (c + 1) * N:
        g = at // GROUP_B
        end = min((g + 1) * GROUP_B, (c + 1) * N)
        out.append((g, at - c * N, end - c * N))
        at = end
    return out


def bands():
    s, to = np.arange(P)[:, None], np.arange(P)[None, :]
    out = np.zeros((P, 3, len(WINDOWS), P), np.float32)
    for g, w in enumerate(WINDOWS):
        back = to - s
        near = (back >= 0) & (back < w)
        out[:, 0, g] = near / np.minimum(to + 1, w) - (back == 0)
        out[:, 1, g] = near / w - (back == 0)
        out[:, 2, g] = (back + P < w) / w
    return out.reshape(P, -1)


def bucket_rows():
    d = np.maximum(SEQ - 1 - np.arange(DISTS), 0)
    half = BUCKETS // 2
    far = np.log(np.maximum(d, 1).astype(np.float32) / np.float32(half)) / np.float32(np.log(MAX_DIST / half))
    bucket = np.where(d < half, d, np.minimum(half + (far * np.float32(half)).astype(np.int32), BUCKETS - 1))
    return (np.arange(BUCKETS)[:, None] == bucket[None, :]).astype(np.float32)


def kernel(**inputs):
    import concourse.bacc as bacc
    from concourse.bass_utils import run_bass_kernel_spmd

    a = {k: np.asarray(v) for k, v in inputs.items()}
    x, w_in, w_mix = a["x"][0], a["w_in"][0], a["a_w_in_2"][0]
    q = WIDTH
    fout = 4 * WIDTH
    gate = np.zeros((D, P), w_in.dtype)
    gate[:, :HEADS] = w_in[:, fout:fout + HEADS]
    qi, ki = 3 * D, 3 * D + HEADS * DI
    key = w_mix[:, ki:ki + DI]
    index = np.concatenate([key, key, w_mix[:, ki + DI:ki + DI + HEADS]], 1)

    def ffn(l, i):
        up, down = a["ffn_w_in_2"][l, i], a["ffn_w_out_2"][l, i]
        return fused_slabs(up, down, 256, DFF2 // 256,
                           lambda c: np.r_[256 * c:256 * c + 256, DFF2 + 256 * c:DFF2 + 256 * c + 256])

    b_in = a["b_w_in_2"][0]

    def cols(w, start):
        return column_slabs(w, np.r_[start:start + N])

    def paired(w, start):
        heads = start + np.arange(HEADS * 64).reshape(2, 2, 2, 64)
        return column_slabs(w, heads.transpose(0, 2, 1, 3).reshape(-1))

    slabs = np.concatenate(
        [wide_slab(gate), cols(w_in, 0), cols(w_in, 3 * q), paired(w_in, q), paired(w_in, 2 * q),
         row_slabs(a["w_out"][0]),
         fused_slabs(a["w_mlp1"][0], a["w_mlp2"][0], 512, DFF1 // 512, lambda c: np.r_[512 * c:512 * c + 512]),
         ffn(0, 0),
         cols(w_mix, 2 * D), wide_slab(index), paired(w_mix, qi), cols(w_mix, 2 * D + N),
         cols(w_mix, 0), cols(w_mix, N), cols(w_mix, D), cols(w_mix, D + N),
         row_slabs(a["a_w_out_2"][0]), ffn(0, 1), ffn(1, 0)]
        + [cols(b_in, HALF_B + N * c) for c in range(HALF_B // N)]
        + [fused_slabs(b_in, a["b_w_out_2"][0], 512, HALF_B // 512, lambda c: np.r_[512 * c:512 * c + 512]),
           ffn(1, 1)])

    g2 = a["norm_g_2"]
    rows = {"ln1_g": a["ln1_g"][0], "ln1_b": a["ln1_b"][0], "ln2_g": a["ln2_g"][0], "ln2_b": a["ln2_b"][0],
            "final": a["final_g_2"]}
    for i in range(6):
        rows[f"norm{i}"] = g2[i // 3, i % 3]
    for j in range(3):
        part = slice(j * D, (j + 1) * D)
        rows[f"bias_u{j}"] = a["b_b_in_2"][0][:HALF_B][part]
        rows[f"bias_v{j}"] = a["b_b_in_2"][0][HALF_B:][part]
        rows[f"gate_g{j}"], rows[f"gate_b{j}"] = a["b_ln_g_2"][0][part], a["b_ln_b_2"][0][part]

    s, to = np.arange(P)[None, :], np.arange(P)[:, None]
    arrays = {
        "slabs": slabs,
        "vectors": np.stack([rows[v] for v in VECTORS]),
        "x": x,
        "x_turned": x.T.reshape(KD, P, SEQ).transpose(1, 0, 2).reshape(P, 2, 1024),
        "identity": np.eye(P, dtype=np.float32),
        "causal": np.where(s <= to, 0.0, MASKED).astype(np.float32),
        "bands": bands(),
        "buckets": bucket_rows(),
        "rel_table": a["rel_table_2"],
        "pool_w": a["pool_w"][0].transpose(1, 0, 2).reshape(P, -1),
        "pool_scale": a["pool_scale"][0].reshape(4, P).T,
        "b_f": a["b_f"][0].reshape(HEADS, 1),
        "w_sp": a["b_w_sp_2"][0].transpose(2, 0, 1).reshape(P, -1),
        "b_sp": a["b_b_sp_2"][0].T,
    }
    arrays = {k: np.ascontiguousarray(v) for k, v in arrays.items()}
    nc = bacc.Bacc("TRN2", target_bir_lowering=False, num_devices=1)
    dr = {k: nc.dram_tensor(f"{k}_dram", v.shape, F32, kind="ExternalInput").ap() for k, v in arrays.items()}
    dr["table"] = nc.dram_tensor("table_dram", [HEADS, DISTS], F32, kind="Internal").ap()
    dr["tables"] = nc.dram_tensor("tables_dram", [P, HEADS * DISTS], F32, kind="Internal").ap()
    dr["out"] = nc.dram_tensor("out_dram", [SEQ, D], F32, kind="ExternalOutput").ap()
    build(nc, dr)
    r = run_bass_kernel_spmd(nc, [{f"{k}_dram": v for k, v in arrays.items()}], core_ids=[0])
    return r.results[0]["out_dram"].reshape(1, SEQ, D)
```

```python
from collections import namedtuple
from contextlib import ExitStack

import numpy as np

import concourse.bass as bass
from concourse import mybir

F32 = mybir.dt.float32
F32R = mybir.dt.float32r
ACT = mybir.ActivationFunctionType
ALU = mybir.AluOpType
AX_X = mybir.AxisListType.X

P = 128
SEQ = 256
TT = SEQ // P
D = 1024
KD = D // P
N = 512
SLAB = 2048
RAW = 3
RING = 6
VW = 1024
VRING = 3
WIDTH = 512
HEADS = 8
DH1, DH2 = 64, 128
DI = 64
DFF1, DFF2, HALF_B = 4096, 2816, 3072
GROUP_B = HALF_B // 8
TOPK = 64
WINDOWS = (2, 4, 8, 16)
ALPHA = float(2.0 ** 0.25)
LN_EPS, EPS = 1e-5, 1e-6
MASKED, TAKEN = -1e30, -3e38
BUCKETS, MAX_DIST = 32, 2048
DISTS = 384

VECTORS = (["ln1_g", "ln1_b", "ln2_g", "ln2_b"] + [f"norm{i}" for i in range(5)]
           + [f"bias_v{j}" for j in range(3)]
           + [f"{w}{j}" for j in range(3) for w in ("gate_g", "gate_b", "bias_u")]
           + ["norm5", "final"])


def column_slabs(w, cols):
    part = w[:, cols].reshape(2, 4, P, N)
    return part.transpose(0, 2, 1, 3).reshape(2, P, SLAB)


def row_slabs(w):
    return w.reshape(-1, 2, P, D).transpose(0, 2, 1, 3).reshape(-1, P, SLAB)


def wide_slab(w):
    out = np.zeros((KD, P, 256), w.dtype)
    out[:, :, :w.shape[1]] = w.reshape(KD, P, -1)
    return out.transpose(1, 0, 2).reshape(1, P, SLAB)


def fused_slabs(up, down, width, chunks, cols):
    rows = row_slabs(down).reshape(chunks, width // 256, P, SLAB)
    out = []
    for c in range(chunks):
        out.append(column_slabs(up, cols(c)))
        if c:
            out.append(rows[c - 1])
    return np.concatenate(out + [rows[chunks - 1]])


class Splits:

    def __init__(self, one, total):
        self.next, self.one, self.total = 0, one, total

    def upto(self, end):
        while self.next < min(end, self.total):
            self.one(self.next)
            self.next += 1


def spread(ap, dims):
    return bass.AP(tensor=ap.tensor, offset=ap.offset, ap=[ap.ap[0]] + dims)


Fused = namedtuple("Fused", "chunks tiles rows s lead period slabs loads start up down")
Unit = namedtuple("Unit", "kind m i last to factor wait")


def fused_shape(first, end, chunks, tiles):
    rows = tiles // 2
    s = 2 + rows
    period = 2 if s == 3 else 3
    return Fused(
        chunks=chunks, tiles=tiles, rows=rows, s=s, lead=RING - s, period=period,
        slabs=s * period, loads=16 * s * period // RAW,
        start=first + 2 + RING - s,
        up=[first] + [first + 2 + s * c for c in range(chunks)],
        down=[first + 4 + s * c for c in range(chunks - 1)] + [end - rows])


def build(nc, dr):
    with ExitStack() as ctx:
        def sb(name, shape, dt=F32):
            return ctx.enter_context(nc.sbuf_tensor(name, shape, dt))

        def also(name, shape, words):
            return nc.alloc_sbuf_tensor_at(name, shape, F32, offset=nc.sbuf_base - 4 * words)

        def sem(name):
            return ctx.enter_context(nc.semaphore(name))

        def stage(name, signals, first=0, count=0):
            return namedtuple(name, "first end " + signals)(
                first, first + count, *[sem(f"{name}_{s}") for s in signals.split()])

        raw = sb("raw", [P, RAW, SLAB])
        whi = sb("whi", [P, RING, SLAB], F32R)
        wlo = sb("wlo", [P, RING, SLAB], F32R)
        vec = sb("vec", [P, VRING, VW])
        h = sb("h", [P, TT, D])
        xt = sb("xt", [P, 2, KD, SEQ], F32R)
        hid = sb("hid", [P, 2 * N])
        hl = sb("hl", [P, 2, 2, N], F32R)
        hlf = also("hlf", [P, 2, 1024], 2048)
        ht = sb("ht", [P, 2, 2, 4, P], F32R)
        htf = also("htf", [P, 2048], 2048)
        reg = sb("reg", [P, 7168])
        idr = sb("idr", [P, P], F32R)
        idf = sb("idf", [P, P])
        causal = sb("causal", [P, P])
        st = sb("st", [P, 192])
        acc = ctx.enter_context(nc.psum_tensor("acc", [P, 4, N], F32))
        mm = ctx.enter_context(nc.psum_tensor("mm", [P, 2, N], F32))
        tp = ctx.enter_context(nc.psum_tensor("tp", [P, 2, N], F32))

        SQ, RSTD, VAR, MV, BN, WI, BSP, PSC, BF, LRSTD = 0, 2, 4, 6, 10, 82, 98, 106, 110, 166
        CQ, MX, NEG, RS, REC, HALF, TOP = 112, 128, 132, 140, 148, 152, 156
        U1, V1, QT1, KT1, CF, NCF, GZ, GE = 0, 1024, 2048, 3072, 4096, 4352, 4608, 4864
        POOLW, BUCK, TABLE, REL, ONES = 5120, 5632, 6016, 6400, 6656
        QT2, KT2, V2, KI, SCORE, SEL = 0, 2048, 4096, 6144, 6400, 6656
        VB, WSP = 0, 6144

        raw_loaded = [sem(f"raw_loaded{i}") for i in range(RAW)]
        vec_loaded = [sem(f"vec_loaded{i}") for i in range(VRING)]
        hi_done, lo_done, slab_used = sem("hi_done"), sem("lo_done"), sem("slab_used")
        const_loaded, half_set, idr_ready = sem("const_loaded"), sem("half_set"), sem("idr_ready")
        small_loaded, bands_loaded, h_loaded = sem("small_loaded"), sem("bands_loaded"), sem("h_loaded")
        x_loaded, x_hi, x_lo = [sem("x_loaded0"), sem("x_loaded1")], sem("x_hi"), sem("x_lo")
        table_ready, table_copied = sem("table_ready"), sem("table_copied")
        table_stored, tables_stored = sem("table_stored"), sem("tables_stored")
        bias_loaded, wsp_loaded, wsp_masked = sem("bias_loaded"), sem("wsp_loaded"), sem("wsp_masked")
        vector_step, stored = sem("vector_step"), sem("stored")
        LAYER = "var_ready eps_added rstd_ready"
        FUSED = "unit_ready gate_ready hid_ready hl_hi hl_ready tp_ready ht_ready acc_ready"
        PROJ = "unit_ready evac"
        ATT = ("sc_ready bias_ready p_ready tp_ready pt_ready pv_ready att_ready "
               "xtp_ready hi_ready xt_ready")
        NORM = "sum_ready sq_ready eps_added rstd_ready xn_ready tp_ready hi_ready xt_ready"
        Norm = namedtuple("Norm", "tiles halves split_to " + NORM)
        norm_sems = [sem(f"norm_{s}") for s in NORM.split()]

        def norm_stage(i, split_to=0):
            return Norm(TT * max(i - 1, 0), 2 * TT * i, split_to, *norm_sems)

        at = [0]

        def slabs(n):
            at[0] += n
            return dict(first=at[0] - n, count=n)

        w_in = stage("w_in", PROJ, **slabs(9))
        gates = stage("gates", "z_ready abs_ready exp_ready ln_ready cf_ready cq_ready cq_copied")
        pool = stage("pool", "d_ready d_copied y_ready y_scaled hi_ready xt_ready")
        att1 = stage("att1", ATT)
        w_out = stage("w_out", "acc_ready", **slabs(4))
        l0 = stage("l0", LAYER)
        mlp = stage("mlp", FUSED, **slabs(4 * (DFF1 // 512)))
        l1 = stage("l1", LAYER)
        ffa = stage("ffa", FUSED, **slabs(3 * (DFF2 // 256)))
        a_in = stage("a_in", PROJ, **slabs(15))
        idx = stage("idx", "rel_ready relu_ready rel_used sel_ready")
        att2 = stage("att2", ATT)
        a_out = stage("a_out", "acc_ready", **slabs(4))
        ffb = stage("ffb", FUSED, **slabs(3 * (DFF2 // 256)))
        ffc = stage("ffc", FUSED, **slabs(3 * (DFF2 // 256)))
        b_in = stage("b_in", PROJ + " gelu_ready", **slabs(12))
        vln = stage("vln", LAYER + " done")
        mixb = stage("mixb", FUSED + " unit_taken mix_ready", **slabs(4 * (HALF_B // 512)))
        ffd = stage("ffd", FUSED, **slabs(3 * (DFF2 // 256)))
        SLABS = at[0]

        f_mlp = fused_shape(mlp.first, mlp.end, DFF1 // 512, 4)
        f_mix = fused_shape(mixb.first, mixb.end, HALF_B // 512, 4)
        f_ffa, f_ffb, f_ffc, f_ffd = (fused_shape(s.first, s.end, DFF2 // 256, 2) for s in (ffa, ffb, ffc, ffd))

        n0, n1, n2, n3, n4, n5, n6, n7 = (norm_stage(i, end) for i, end in enumerate(
            (f_mlp.start, f_ffa.start, ffa.end + RING, f_ffb.start, f_ffc.start, ffc.end + RING,
             f_ffd.start, 0)))

        def unit_list(stg, parts):
            out, m, ready = [], stg.first, 0
            for kind, dest, step, factor in parts:
                for i in range(1 if kind == "wide" else 2):
                    last = kind == "wide" or i == 1
                    ready += not last
                    out.append(Unit(
                        kind=kind, m=m, i=i, last=last, to=dest + i * step, factor=factor,
                        wait=(slab_used, m + (1 if kind == "wide" else 2)) if last
                        else (stg.unit_ready, ready)))
                m += 1 if kind == "wide" else 2
            assert m == stg.end
            return out

        IN_UNITS = unit_list(w_in, [("tokens", U1, N, None), ("wide", 0, 0, None), ("tokens", V1, N, None),
                                    ("turned", QT1, N, DH1 ** -0.5), ("turned", KT1, N, None)])
        A_UNITS = unit_list(a_in, [("tokens", V2, D, None), ("wide", 0, 0, None), ("turned", -1, N, None),
                                   ("tokens", V2 + N, D, None),
                                   ("turned", QT2, N, None), ("turned", QT2 + D, N, None),
                                   ("turned", KT2, N, None), ("turned", KT2 + D, N, None)])
        B_UNITS = unit_list(b_in, [("tokens", VB + c * N, HALF_B, None) for c in range(HALF_B // N)])
        GATE_UNIT = 2
        QI_UNIT = 4
        INDEX_AFTER = {6: 0, 8: 1, 10: 2, 12: 3}

        GROUPS = [(t, hh) for t in range(TT) for hh in range(2)]
        ptf, att = hlf[:, 0, :], hlf[:, 1, :]

        def scores_of(g):
            pair = acc[:, 2 * (g % 2):2 * (g % 2) + 2, :].rearrange("p b (i n) -> p (b i) n", i=2)
            return pair[:, :, 0:P * (GROUPS[g][0] + 1)]

        def half_of(head):
            return 64 * (head % 4 // 2), (2 * (head // 4) + head % 2) * SEQ

        def by_head(ap):
            return ap.rearrange("p (i n) -> p i n", i=4)

        def place_of(g):
            return N * g if GROUPS[g][0] == 0 else 0

        def key_blocks(g):
            return sum(t + 1 for t, _ in GROUPS[:g])

        def xn_tile(t):
            return hid[:, :] if t == 0 else hlf[:, 1, :]

        def acc_done(eng, src, t):
            if t == 0:
                eng.wait_ge(src.acc_ready, 1)
            else:
                eng.wait_ge(slab_used, src.end)

        def unit_done(eng, stg, f, c, t, i):
            if t == 0:
                eng.wait_ge(stg.unit_ready, c + 1 + i * f.period)
            else:
                eng.wait_ge(slab_used, f.up[c] + 2 + i * f.slabs)

        def turns(eng, f, first, body):
            c, full = first, (f.chunks - first - (f is f_ffd)) // f.period
            if full > 1:
                with eng.Fori(0, full) as i:
                    for r in range(f.period):
                        body(c + r, i)
                c += full * f.period
            while c < f.chunks:
                body(c, 0)
                c += 1

        block = ctx.enter_context(nc.Block())

        @block.sync
        def _(sp):
            def load(m, i=0):
                if m >= RAW:
                    sp.wait_ge(lo_done, m - RAW + 1 + i * RAW)
                sp.dma_start(raw[:, m % RAW, :], dr["slabs"][m + i * RAW]).then_inc(raw_loaded[m % RAW], 16)

            for m in range(RAW):
                load(m)
            rounds = (SLABS - RAW) // RAW
            with sp.Fori(0, rounds) as i:
                for m in range(RAW, 2 * RAW):
                    load(m, i)
            for m in range(RAW * (rounds + 1), SLABS):
                load(m)
            for t in range(TT):
                sp.wait_ge(n7.xn_ready, n7.halves + 2 * t + 2)
                sp.dma_start(dr["out"][t * P:(t + 1) * P, :], xn_tile(t)).then_inc(stored, 16)
            sp.wait_ge(stored, 16 * TT)

        @block.gpsimd
        def _(pq):
            def load_vec(v, free, count):
                if free is not None:
                    pq.wait_ge(free, count)
                src = dr["vectors"][v]
                pq.dma_start(vec[:, v % VRING, :],
                             bass.AP(tensor=src.tensor, offset=src.offset, ap=[[0, P], [1, VW]]))\
                  .then_inc(vec_loaded[v % VRING], 16)

            def power(n, value, eps, t, ready, base=0, to=LRSTD):
                pq.wait_ge(ready, base + t + 1)
                nc.gpsimd.tensor_scalar(st[:, VAR + t:VAR + t + 1], st[:, value:value + 1], eps, None,
                                        ALU.add).then_inc(n.eps_added, 1)
                pq.wait_ge(n.eps_added, base + t + 1)
                nc.gpsimd.tensor_tensor(st[:, to + t:to + t + 1], st[:, VAR + t:VAR + t + 1],
                                        st[:, HALF:HALF + 1], ALU.pow).then_inc(n.rstd_ready, 1)

            def rms(n):
                for t in range(TT):
                    power(n, SQ + t, EPS, t, n.sq_ready, n.tiles, RSTD)

            pq.dma_start(idf[:, :], dr["identity"]).then_inc(const_loaded, 16)
            pq.dma_start(causal[:, :], dr["causal"]).then_inc(const_loaded, 16)
            for place, name in ((reg[0:BUCKETS, BUCK:BUCK + DISTS], "buckets"),
                                (reg[0:BUCKETS, REL:REL + HEADS], "rel_table"),
                                (reg[:, POOLW:POOLW + 4 * P], "pool_w"),
                                (st[:, PSC:PSC + 4], "pool_scale"),
                                (st[0:HEADS, BF:BF + 1], "b_f"),
                                (st[:, BSP:BSP + 8], "b_sp")):
                pq.dma_start(place, dr[name]).then_inc(small_loaded, 16)
            nc.gpsimd.memset(st[:, HALF:HALF + 1], -0.5).then_inc(half_set, 1)
            pq.wait_ge(gates.z_ready, 1)
            pq.dma_start(h[:, :, :].rearrange("p t d -> p (t d)")[:, 0:12 * P], dr["bands"])\
              .then_inc(bands_loaded, 16)
            for v in range(VRING):
                load_vec(v, None, 0)
            pq.wait_ge(table_copied, 1)
            pq.dma_start(dr["table"], reg[0:HEADS, TABLE:TABLE + DISTS]).then_inc(table_stored, 16)
            pq.wait_ge(pool.d_ready, 2)
            for t in range(TT):
                pq.dma_start(h[:, t, :], dr["x"][t * P:(t + 1) * P, :]).then_inc(h_loaded, 16)
            pq.wait_ge(half_set, 1)
            for t in range(TT):
                power(l0, MV + 2 * t + 1, LN_EPS, t, l0.var_ready)
            load_vec(3, n0.xn_ready, n0.halves + 4)
            load_vec(4, n0.xn_ready, n0.halves + 4)
            pq.wait_ge(table_stored, 16)
            table, tables = dr["table"], dr["tables"]
            pq.dma_start(tables, bass.AP(tensor=table.tensor, offset=table.offset,
                                         ap=[[0, P], [1, HEADS * DISTS]])).then_inc(tables_stored, 16)
            for t in range(TT):
                power(l1, MV + 2 * t + 1, LN_EPS, t, l1.var_ready)
                power(n1, SQ + t, EPS, t, n1.sq_ready, n1.tiles, RSTD)
            load_vec(5, n1.sum_ready, n1.tiles + 2)
            load_vec(6, n1.sum_ready, n1.tiles + 2)
            load_vec(7, n1.xn_ready, n1.halves + 4)
            rms(n2)
            load_vec(8, n2.xn_ready, n2.halves + 4)
            pq.wait_ge(tables_stored, 16)
            pq.dma_start(htf[:, :].rearrange("p (i n) -> p i n", i=HEADS),
                         bass.AP(tensor=tables.tensor, offset=tables.offset + P - 1,
                                 ap=[[HEADS * DISTS - 1, P], [DISTS, HEADS], [1, SEQ]]))\
              .then_inc(bias_loaded, 16)
            rms(n3)
            load_vec(9, n3.xn_ready, n3.halves + 4)
            pq.dma_start(reg[:, WSP:WSP + 8 * P], dr["w_sp"]).then_inc(wsp_loaded, 16)
            pq.wait_ge(wsp_loaded, 16)
            w_sp = reg[:, WSP:WSP + 8 * P].rearrange("p (g n) -> p g n", g=8)
            nc.gpsimd.affine_select(out=w_sp, in_=w_sp, compare_op=ALU.is_ge, fill=0.0, base=0,
                                    pattern=[[0, 8], [1, P]], channel_multiplier=-1).then_inc(wsp_masked, 1)
            rms(n4)
            load_vec(10, n4.xn_ready, n4.halves + 4)
            rms(n5)
            load_vec(11, n5.xn_ready, n5.halves + 4)
            for j in range(3):
                load_vec(12 + j, b_in.evac, 4 * j + 4)
            for t in range(TT):
                power(vln, MV + 2 * t + 1, EPS, t, vln.var_ready)
            for j in range(2):
                load_vec(15 + 3 * j, vln.done, 4 * j + 4)
                load_vec(16 + 3 * j, vln.done, 4 * j + 4)
                load_vec(17 + 3 * j, mixb.unit_taken, 4 * j + 4)
            load_vec(21, vln.done, 12)
            load_vec(22, vln.done, 12)
            rms(n6)
            rms(n7)

        @block.scalar
        def _(act):
            def hi(m, f=None, i=0):
                act.wait_ge(raw_loaded[m % RAW], 16 * (m // RAW + 1) + (i * f.loads if f else 0))
                if m >= RING:
                    act.wait_ge(slab_used, m - RING + 1 + (i * f.slabs if f else 0))
                nc.scalar.activation(whi[:, m % RING, :], raw[:, m % RAW, :], ACT.Copy).then_inc(hi_done, 1)

            splits = Splits(hi, SLABS)

            def tp_to_xt(ready, g, k, t, done):
                act.wait_ge(ready, g + 1)
                nc.scalar.activation(xt[:, 0, k:k + 4, t * P:(t + 1) * P], by_head(tp[:, g % 2, :]),
                                     ACT.Copy).then_inc(done, 1)

            def square(n, t):
                act.wait_ge(n.sum_ready, n.tiles + t + 1)
                nc.scalar.activation(htf[:, t * D:(t + 1) * D], h[:, t, :], ACT.Square,
                                     scale=D ** -0.5, accum_out=st[:, SQ + t:SQ + t + 1])\
                  .then_inc(n.sq_ready, 1)

            def norm(n, squares=True, first=False):
                for t in range(TT):
                    if first:
                        square(n, t)
                    for j in range(2):
                        tp_to_xt(n.tp_ready, n.halves + 2 * t + j, 4 * j, t, n.hi_ready)
                    if squares and not first:
                        square(n, t)
                    if t == 0:
                        splits.upto(min(splits.next + 1, n.split_to))

            def fused(stg, f, gate, width):
                def hidden_hi(c, t, i):
                    act.wait_ge(stg.hid_ready, 2 * c + t + 1 + i * 2 * f.period)
                    if c > 0:
                        act.wait_ge(stg.tp_ready, f.rows * (2 * c + t - 1) + i * 2 * f.rows * f.period)
                    nc.scalar.activation(hl[:, t, 0, 0:width], hid[:, t * N:t * N + width], ACT.Copy)\
                      .then_inc(stg.hl_hi, 1)

                def turned(c, t, i):
                    for j in range(f.rows):
                        g = f.rows * (2 * c + t) + j
                        act.wait_ge(stg.tp_ready, g + 1 + i * 2 * f.rows * f.period)
                        nc.scalar.activation(ht[:, t, :, 2 * j:2 * j + 2, :],
                                             tp[:, g % 2, :].rearrange("p (i q n) -> p i q n", i=2, q=2),
                                             ACT.Copy).then_inc(stg.ht_ready, 1)

                def chunk(c, i):
                    m = f.up[c] + f.lead
                    for j in range(min(f.s - 1, SLABS - m)):
                        hi(m + j, f, i)
                    gate(c, 0, i)
                    turned(c - 1, 1, i)
                    hidden_hi(c, 0, i)
                    if m + f.s - 1 < SLABS:
                        hi(m + f.s - 1, f, i)
                    gate(c, 1, i)
                    turned(c, 0, i)
                    hidden_hi(c, 1, i)

                splits.upto(f.start)
                gate(0, 0, 0)
                hidden_hi(0, 0, 0)
                gate(0, 1, 0)
                turned(0, 0, 0)
                hidden_hi(0, 1, 0)
                turns(act, f, 1, chunk)
                splits.next = f.up[f.chunks] + f.lead
                splits.upto(stg.end + 4 - f.rows)
                turned(f.chunks - 1, 1, 0)

            def silu_gate(stg, f, n):
                def gate(c, t, i):
                    unit_done(act, stg, f, c, t, i)
                    if c == 0:
                        act.wait_ge(n.rstd_ready, n.tiles + t + 1)
                    nc.scalar.activation(hid[:, t * N:t * N + 256], mm[:, t, 0:256], ACT.Silu,
                                         scale=st[:, RSTD + t:RSTD + t + 1])\
                      .then_inc(stg.gate_ready, 1)
                return gate

            def relu_gate(c, t, i):
                unit_done(act, mlp, f_mlp, c, t, i)
                if c > 0:
                    act.wait_ge(mlp.hl_ready, 2 * c + t - 1 + i * 2 * f_mlp.period)
                nc.scalar.activation(hid[:, t * N:(t + 1) * N], mm[:, t, :], ACT.Relu)\
                  .then_inc(mlp.gate_ready, 1)

            def gelu_gate(c, t, i):
                act.wait_ge(mixb.unit_taken, 2 * c + t + 1 + i * 2 * f_mix.period)
                nc.scalar.activation(hid[:, t * N:(t + 1) * N], hid[:, t * N:(t + 1) * N],
                                     ACT.Gelu_apprx_tanh).then_inc(mixb.gate_ready, 1)

            def attention(a, tiles, base, between):
                def exps(g):
                    act.wait_ge(a.bias_ready, g + 1)
                    if g >= 2:
                        act.wait_ge(a.tp_ready, key_blocks(g))
                    keys = P * (GROUPS[g][0] + 1)
                    s = scores_of(g)
                    for i in range(4):
                        r = 4 * (g % 2) + i
                        ins = nc.scalar.activation(
                            hid[:, place_of(g) + i * keys:place_of(g) + (i + 1) * keys],
                            s[:, i, :], ACT.Exp, bias=st[:, NEG + r:NEG + r + 1],
                            accum_out=st[:, RS + r:RS + r + 1])
                    ins.then_inc(a.p_ready, 1)

                def turned(g):
                    if g >= 2:
                        act.wait_ge(a.pv_ready, g)
                    for kb in range(GROUPS[g][0] + 1):
                        n = key_blocks(g) + kb
                        act.wait_ge(a.tp_ready, n + 1)
                        nc.scalar.activation(ptf[:, place_of(g) + kb * N:place_of(g) + (kb + 1) * N],
                                             tp[:, n % 2, :], ACT.Copy).then_inc(a.pt_ready, 1)

                def to_xt(t):
                    for j in range(tiles // 4):
                        tp_to_xt(a.xtp_ready, tiles // 4 * t + j, base + 4 * j, t, a.hi_ready)

                exps(0)
                exps(1)
                between()
                turned(0)
                turned(1)
                exps(2)
                to_xt(0)
                turned(2)
                exps(3)
                turned(3)
                to_xt(1)

            for j in range(2):
                act.dma_start(hlf[:, j, :], dr["x_turned"][:, j, :]).then_inc(x_loaded[j], 16)
            for j in range(2):
                act.wait_ge(x_loaded[j], 16)
                nc.scalar.activation(xt[:, 0, 4 * j:4 * j + 4, :].rearrange("p k n -> p (k n)"),
                                     hlf[:, j, :], ACT.Copy).then_inc(x_hi, 1)
                splits.upto(j + 1)
            splits.upto(4)
            act.wait_ge(const_loaded, 32)
            nc.scalar.activation(idr[:, :], idf[:, :], ACT.Copy).then_inc(idr_ready, 1)
            for u in IN_UNITS:
                if u is IN_UNITS[GATE_UNIT + 2]:
                    z, e = reg[0:HEADS, GZ:GZ + SEQ], reg[0:HEADS, GE:GE + SEQ]
                    act.wait_ge(gates.z_ready, 1)
                    nc.scalar.activation(e, z, ACT.Abs).then_inc(gates.abs_ready, 1)
                    act.wait_ge(gates.abs_ready, 1)
                    nc.scalar.activation(e, e, ACT.Exp, scale=-1.0).then_inc(gates.exp_ready, 1)
                    act.wait_ge(gates.exp_ready, 1)
                    nc.scalar.activation(e, e, ACT.Ln, bias=1.0).then_inc(gates.ln_ready, 1)
                splits.upto(u.m + RING)

            def pooled():
                act.wait_ge(pool.y_scaled, 4)
                nc.scalar.activation(xt[:, 0, 0:4, :].rearrange("p k n -> p (k n)"), htf[:, 1024:2048],
                                     ACT.Copy).then_inc(pool.hi_ready, 1)
                splits.upto(w_in.end + RING)

            attention(att1, WIDTH // P, WIDTH // P, pooled)
            splits.upto(w_out.first + RING)
            norm(n0, squares=False)
            fused(mlp, f_mlp, relu_gate, N)
            norm(n1)
            fused(ffa, f_ffa, silu_gate(ffa, f_ffa, n1), 256)
            norm(n2, first=True)

            def relus(g):
                act.wait_ge(idx.rel_ready, g + 1)
                if g >= 2:
                    act.wait_ge(idx.rel_used, g - 1)
                keys = 4 * P * (GROUPS[g][0] + 1)
                nc.scalar.activation(by_head(hlf[:, g % 2, 0:keys]), scores_of(g), ACT.Relu, scale=DI ** -0.5)\
                  .then_inc(idx.relu_ready, 1)

            for n, u in enumerate(A_UNITS):
                splits.upto(u.m + RING)
                if n in INDEX_AFTER:
                    relus(INDEX_AFTER[n])
            attention(att2, D // P, 0, lambda: splits.upto(a_in.end + RING))
            splits.upto(a_out.first + RING)
            norm(n3)
            fused(ffb, f_ffb, silu_gate(ffb, f_ffb, n3), 256)
            norm(n4)
            fused(ffc, f_ffc, silu_gate(ffc, f_ffc, n4), 256)
            norm(n5)
            for n, u in enumerate(B_UNITS):
                splits.upto(u.m + RING)
                v = reg[:, u.to:u.to + N]
                act.wait_ge(b_in.evac, n + 1)
                nc.scalar.activation(v, v, ACT.Gelu_apprx_tanh).then_inc(b_in.gelu_ready, 1)
            fused(mixb, f_mix, gelu_gate, N)
            norm(n6)
            fused(ffd, f_ffd, silu_gate(ffd, f_ffd, n6), 256)
            for t in range(TT):
                square(n7, t)

        @block.vector
        def _(dve):
            steps = [0]

            def step(ins):
                steps[0] += 1
                ins.then_inc(vector_step, 1)
                dve.wait_ge(vector_step, steps[0])

            def lo(m, f=None, i=0):
                dve.wait_ge(hi_done, m + 1 + (i * f.slabs if f else 0))
                nc.vector.tensor_tensor(wlo[:, m % RING, :], raw[:, m % RAW, :], whi[:, m % RING, :],
                                        ALU.subtract).then_inc(lo_done, 1)

            splits = Splits(lo, SLABS)

            def half(t, j):
                return h[:, t, j * N:(j + 1) * N]

            def vec_of(v, width=VW, start=0):
                return vec[:, v % VRING, start:start + width]

            def vec_wait(v):
                dve.wait_ge(vec_loaded[v % VRING], 16 * (v // VRING + 1))

            def tp_to_xt(ready, g, k, t, done):
                dve.wait_ge(ready, g + 1)
                nc.vector.tensor_tensor(xt[:, 1, k:k + 4, t * P:(t + 1) * P], by_head(tp[:, g % 2, :]),
                                        xt[:, 0, k:k + 4, t * P:(t + 1) * P], ALU.subtract).then_inc(done, 1)

            def layer(l, src, t, v, after=None):
                acc_done(dve, src, t)
                for j in range(2):
                    step(nc.vector.scalar_tensor_tensor(half(t, j), half(t, j), ALPHA, acc[:, 2 * t + j, :],
                                                        ALU.mult, ALU.add))
                for j in range(2):
                    step(nc.vector.bn_stats(st[:, BN + 6 * j:BN + 6 * j + 6], half(t, j)))
                nc.vector.bn_aggr(st[:, MV + 2 * t:MV + 2 * t + 2],
                                  st[:, BN:BN + 12].rearrange("p (c s) -> p c s", s=6)).then_inc(l.var_ready, 1)
                dve.wait_ge(l.var_ready, t + 1)
                vec_wait(v)
                vec_wait(v + 1)
                for j in range(2):
                    step(nc.vector.scalar_tensor_tensor(half(t, j), half(t, j), st[:, MV + 2 * t:MV + 2 * t + 1],
                                                        vec_of(v, N, j * N), ALU.subtract, ALU.mult))
                dve.wait_ge(l.rstd_ready, t + 1)
                for j in range(2):
                    ins = nc.vector.scalar_tensor_tensor(
                        half(t, j), half(t, j), st[:, LRSTD + t:LRSTD + t + 1], vec_of(v + 1, N, j * N),
                        ALU.mult, ALU.add)
                    if after is not None:
                        after(j, ins)
                return ins

            def rms(n, t, v):
                vec_wait(v)
                dve.wait_ge(n.rstd_ready, n.tiles + t + 1)
                for j in range(2):
                    nc.vector.scalar_tensor_tensor(xn_tile(t)[:, j * N:(j + 1) * N], half(t, j),
                                                   st[:, RSTD + t:RSTD + t + 1], vec_of(v, N, j * N),
                                                   ALU.mult, ALU.mult).then_inc(n.xn_ready, 1)

            def gained(n, t, j, v):
                nc.vector.tensor_tensor(xn_tile(t)[:, j * N:(j + 1) * N], half(t, j), vec_of(v, N, j * N),
                                        ALU.mult).then_inc(n.xn_ready, 1)

            def add_acc(n, src, t, factor, v=None):
                acc_done(dve, src, t)
                if v is not None:
                    vec_wait(v)
                for j in range(2):
                    ins = nc.vector.scalar_tensor_tensor(half(t, j), acc[:, 2 * t + j, :], factor, half(t, j),
                                                         ALU.mult, ALU.add)
                    if j == 0 and v is not None:
                        step(ins)
                        gained(n, t, 0, v)
                ins.then_inc(n.sum_ready, 1)
                if v is not None:
                    dve.wait_ge(n.sum_ready, n.tiles + t + 1)
                    gained(n, t, 1, v)

            def to_xt(n, t):
                for j in range(2):
                    tp_to_xt(n.hi_ready, n.halves + 2 * t + j, 4 * j, t, n.xt_ready)

            def norm(n, src, factor, v, first=False):
                for t in range(TT):
                    if first:
                        add_acc(n, src, t, factor)
                        rms(n, t, v)
                    else:
                        add_acc(n, src, t, factor, v)
                    to_xt(n, t)

            def fused(stg, f, unit, width):
                def hidden_lo(c, t, i):
                    dve.wait_ge(stg.hl_hi, 2 * c + t + 1 + i * 2 * f.period)
                    nc.vector.tensor_tensor(hl[:, t, 1, 0:width], hid[:, t * N:t * N + width],
                                            hl[:, t, 0, 0:width], ALU.subtract).then_inc(stg.hl_ready, 1)

                def chunk(c, i):
                    m = f.up[c] + f.lead
                    for j in range(min(f.s - 1, SLABS - m)):
                        lo(m + j, f, i)
                    unit(c, 0, i)
                    hidden_lo(c, 0, i)
                    if m + f.s - 1 < SLABS:
                        lo(m + f.s - 1, f, i)
                    unit(c, 1, i)
                    hidden_lo(c, 1, i)

                splits.upto(f.start)
                for t in range(TT):
                    unit(0, t, 0)
                    hidden_lo(0, t, 0)
                if unit is mixed_unit:
                    for c in range(1, f.chunks):
                        chunk(c, 0)
                else:
                    turns(dve, f, 1, chunk)
                splits.next = f.up[f.chunks] + f.lead
                splits.upto(stg.end + 4 - f.rows)

            def gated_unit(stg, f):
                def unit(c, t, i):
                    dve.wait_ge(stg.gate_ready, 2 * c + t + 1 + i * 2 * f.period)
                    x = hid[:, t * N:t * N + 256]
                    nc.vector.scalar_tensor_tensor(x, mm[:, t, 256:512], st[:, RSTD + t:RSTD + t + 1], x,
                                                   ALU.mult, ALU.mult).then_inc(stg.hid_ready, 1)
                return unit

            def squared_unit(c, t, i):
                dve.wait_ge(mlp.gate_ready, 2 * c + t + 1 + i * 2 * f_mlp.period)
                x = hid[:, t * N:(t + 1) * N]
                nc.vector.scalar_tensor_tensor(x, mm[:, t, :], 0.0, x, ALU.max, ALU.mult)\
                  .then_inc(mlp.hid_ready, 1)

            def mixed_unit(c, t, i):
                if c == 0 and t == 0:
                    normalize_v(0, 0)
                    normalize_v(0, 1)
                v = 14 + 3 * (c // 2)
                vec_wait(v)
                unit_done(dve, mixb, f_mix, c, t, 0)
                if c > 0:
                    dve.wait_ge(mixb.hl_ready, 2 * c + t - 1)
                x = hid[:, t * N:(t + 1) * N]
                nc.vector.scalar_tensor_tensor(x, mm[:, 0, :], st[:, RSTD + t:RSTD + t + 1],
                                               vec_of(v, N, (c % 2) * N), ALU.mult, ALU.add)\
                  .then_inc(mixb.unit_taken, 1)
                dve.wait_ge(mixb.gate_ready, 2 * c + t + 1)
                dve.wait_ge(mixb.mix_ready, 2 * c + t + 1)
                for g, a, b in mix_pieces(c):
                    y = hid[:, t * N + a:t * N + b]
                    ins = nc.vector.scalar_tensor_tensor(y, mm[:, 1, a:b], st[:, BSP + g:BSP + g + 1], y,
                                                         ALU.add, ALU.mult)
                ins.then_inc(mixb.hid_ready, 1)
                if c + 1 < f_mix.chunks:
                    normalize_v(c + 1, t)

            def normalize_v(c, t):
                v = 12 + 3 * (c // 2)
                vec_wait(v)
                vec_wait(v + 1)
                dve.wait_ge(vln.rstd_ready, t + 1)
                x = reg[:, VB + t * HALF_B + c * N:VB + t * HALF_B + (c + 1) * N]
                step(nc.vector.scalar_tensor_tensor(x, x, st[:, MV + 2 * t:MV + 2 * t + 1],
                                                    vec_of(v, N, (c % 2) * N), ALU.subtract, ALU.mult))
                nc.vector.scalar_tensor_tensor(x, x, st[:, LRSTD + t:LRSTD + t + 1],
                                               vec_of(v + 1, N, (c % 2) * N), ALU.mult, ALU.add)\
                  .then_inc(vln.done, 1)

            def attention(a, width, tiles, base, post, between):
                def maxima(g):
                    t, hh = GROUPS[g]
                    dve.wait_ge(a.sc_ready, g + 1)
                    s = scores_of(g)
                    post(g, s)
                    if g >= 2:
                        dve.wait_ge(a.p_ready, g - 1)
                    mx, neg = st[:, MX:MX + 4], st[:, NEG + 4 * (g % 2):NEG + 4 * (g % 2) + 4]
                    step(nc.vector.tensor_reduce(mx, s, AX_X, ALU.max))
                    if a is att1:
                        cq = st[:, CQ + 8 * t + 4 * hh:CQ + 8 * t + 4 * hh + 4]
                        step(nc.vector.tensor_tensor(mx, mx, cq, ALU.add))
                        nc.vector.tensor_tensor(neg, cq, mx, ALU.subtract).then_inc(a.bias_ready, 1)
                    else:
                        nc.vector.tensor_scalar(neg, mx, -1.0, None, ALU.mult).then_inc(a.bias_ready, 1)

                def scaled(g):
                    dve.wait_ge(a.pv_ready, g + 1)
                    r = RS + 4 * (g % 2)
                    step(nc.vector.reciprocal(st[:, REC:REC + 4], st[:, r:r + 4]))
                    if g == 2:
                        dve.wait_ge(a.xtp_ready, tiles // 4)
                    hh = GROUPS[g][1]
                    nc.vector.tensor_tensor(by_head(att[:, hh * 4 * width:(hh + 1) * 4 * width]),
                                            by_head(mm[:, g % 2, 0:4 * width]),
                                            spread(st[:, REC:REC + 4], [[1, 4], [0, width]]), ALU.mult)\
                      .then_inc(a.att_ready, 1)
                    dve.wait_ge(a.att_ready, g + 1)

                def turned(t):
                    for j in range(tiles // 4):
                        tp_to_xt(a.hi_ready, tiles // 4 * t + j, base + 4 * j, t, a.xt_ready)

                maxima(0)
                maxima(1)
                between()
                scaled(0)
                maxima(2)
                scaled(1)
                maxima(3)
                turned(0)
                scaled(2)
                scaled(3)
                turned(1)

            def evacuate(stg, n, u):
                dve.wait_ge(*u.wait)
                if u.kind == "wide" and stg is w_in:
                    nc.vector.tensor_scalar(reg[0:HEADS, GZ:GZ + SEQ], mm[0:HEADS, n % 2, 0:SEQ],
                                            st[0:HEADS, BF:BF + 1], None, ALU.add).then_inc(gates.z_ready, 1)
                    return
                if u.kind == "wide":
                    nc.vector.tensor_copy(reg[:, KI:KI + SEQ], mm[:, n % 2, 0:SEQ])
                    nc.vector.tensor_scalar(st[:, WI:WI + 16], mm[:, n % 2, SEQ:SEQ + 16],
                                            HEADS ** -0.5, None, ALU.mult).then_inc(stg.evac, 1)
                    return
                to = hid[:, u.i * N:(u.i + 1) * N] if u.to < N and u.kind == "turned" and u is not None \
                    and stg is a_in and u.m == A_UNITS[QI_UNIT].m else reg[:, u.to:u.to + N]
                if u.factor is None:
                    ins = nc.vector.tensor_copy(to, mm[:, n % 2, :])
                else:
                    ins = nc.vector.tensor_scalar(to, mm[:, n % 2, :], u.factor, None, ALU.mult)
                ins.then_inc(stg.evac, 1)

            for j in range(2):
                k = slice(4 * j, 4 * j + 4)
                dve.wait_ge(x_hi, j + 1)
                nc.vector.tensor_tensor(xt[:, 1, k, :].rearrange("p k n -> p (k n)"), hlf[:, j, :],
                                        xt[:, 0, k, :].rearrange("p k n -> p (k n)"), ALU.subtract)\
                  .then_inc(x_lo, 1)
                splits.upto(j + 1)
            step(nc.vector.memset(reg[0:HEADS, ONES:ONES + SEQ], 1.0))
            dve.wait_ge(small_loaded, 6 * 16)
            for n, u in enumerate(IN_UNITS):
                splits.upto(u.m + RING)
                evacuate(w_in, n, u)
                if n == GATE_UNIT + 3:
                    z, e = reg[0:HEADS, GZ:GZ + SEQ], reg[0:HEADS, GE:GE + SEQ]
                    cf = reg[0:HEADS, CF:CF + SEQ]
                    dve.wait_ge(gates.ln_ready, 1)
                    step(nc.vector.scalar_tensor_tensor(z, z, 0.0, e, ALU.min, ALU.subtract))
                    step(nc.vector.tensor_tensor_scan(cf, reg[0:HEADS, ONES:ONES + SEQ], z, 0.0,
                                                      ALU.mult, ALU.add))
                    nc.vector.tensor_scalar(reg[0:HEADS, NCF:NCF + SEQ], cf, -1.0, None, ALU.mult)\
                      .then_inc(gates.cf_ready, 1)
            dve.wait_ge(table_ready, 1)
            nc.vector.tensor_copy(reg[0:HEADS, TABLE:TABLE + DISTS], tp[0:HEADS, 1, 0:DISTS])\
              .then_inc(table_copied, 1)
            dve.wait_ge(gates.cq_ready, 1)
            step(nc.vector.tensor_copy(st[:, CQ:CQ + 16], tp[:, 0, 0:16]))
            dve.wait_ge(const_loaded, 32)

            def mask_diagonal(g, s):
                keys = P * (GROUPS[g][0] + 1)
                d = s[:, :, keys - P:keys]
                step(nc.vector.tensor_tensor(d, d, spread(causal[:, :], [[0, 4], [1, P]]), ALU.add))

            def pooled():
                for p in range(2):
                    dve.wait_ge(pool.d_ready, p + 1)
                    nc.vector.tensor_copy(htf[:, p * N:(p + 1) * N], mm[:, p, :]).then_inc(pool.d_copied, 1)
                for p in range(2):
                    dve.wait_ge(pool.y_ready, p + 1)
                    for q in range(2):
                        g = 2 * p + q
                        nc.vector.tensor_scalar(htf[:, D + g * SEQ:D + (g + 1) * SEQ],
                                                mm[:, p, q * SEQ:(q + 1) * SEQ],
                                                st[:, PSC + g:PSC + g + 1], None, ALU.mult)\
                          .then_inc(pool.y_scaled, 1)
                dve.wait_ge(pool.hi_ready, 1)
                nc.vector.tensor_tensor(xt[:, 1, 0:4, :].rearrange("p k n -> p (k n)"), htf[:, D:2 * D],
                                        xt[:, 0, 0:4, :].rearrange("p k n -> p (k n)"), ALU.subtract)\
                  .then_inc(pool.xt_ready, 1)
                splits.upto(w_in.end + RING)

            attention(att1, DH1, WIDTH // P, WIDTH // P, mask_diagonal, pooled)
            splits.upto(w_out.first + RING)
            dve.wait_ge(h_loaded, 16 * TT)
            for t in range(TT):
                layer(l0, w_out, t, 0, lambda j, ins: ins.then_inc(n0.xn_ready, 1))
                to_xt(n0, t)
            fused(mlp, f_mlp, squared_unit, N)

            for t in range(TT):
                layer(l1, mlp, t, 2).then_inc(n1.sum_ready, 1)
                dve.wait_ge(n1.sum_ready, n1.tiles + t + 1)
                vec_wait(4)
                for j in range(2):
                    gained(n1, t, j, 4)
                to_xt(n1, t)
            fused(ffa, f_ffa, gated_unit(ffa, f_ffa), 256)
            norm(n2, ffa, 0.5, 5, first=True)

            def index(g):
                t, hh = GROUPS[g]
                keys = P * (t + 1)
                score, sel = reg[:, SCORE:SCORE + keys], reg[:, SEL + t * SEQ:SEL + t * SEQ + keys]
                dve.wait_ge(idx.relu_ready, g + 1)
                for i in range(4):
                    rel = hlf[:, g % 2, i * keys:(i + 1) * keys]
                    w = WI + 8 * t + 4 * hh + i
                    if hh == 0 and i == 0:
                        step(nc.vector.tensor_scalar(score, rel, st[:, w:w + 1], 0.0, ALU.mult, ALU.add))
                    elif i < 3:
                        step(nc.vector.scalar_tensor_tensor(score, rel, st[:, w:w + 1], score,
                                                            ALU.mult, ALU.add))
                    else:
                        nc.vector.scalar_tensor_tensor(score, rel, st[:, w:w + 1], score, ALU.mult, ALU.add)\
                          .then_inc(idx.rel_used, 1)
                        dve.wait_ge(idx.rel_used, g + 1)
                if hh == 0:
                    return
                diagonal = reg[:, SCORE + keys - P:SCORE + keys]
                step(nc.vector.tensor_tensor(diagonal, diagonal, causal[:, :], ALU.add))
                for r in range(TOPK // 8):
                    step(nc.vector.max(out=st[:, TOP:TOP + 8], in_=score))
                    step(nc.vector.match_replace(out=score, in_to_replace=st[:, TOP:TOP + 8],
                                                 in_values=score, imm_value=TAKEN))
                step(nc.vector.tensor_scalar(sel, score, TAKEN / 2, MASKED, ALU.is_gt, ALU.mult))
                diagonal = reg[:, SEL + t * SEQ + keys - P:SEL + t * SEQ + keys]
                step(nc.vector.tensor_tensor(diagonal, diagonal, causal[:, :], ALU.add))

            for n, u in enumerate(A_UNITS):
                splits.upto(u.m + RING)
                evacuate(a_in, n, u)
                if n in INDEX_AFTER:
                    index(INDEX_AFTER[n])
            dve.wait_ge(bias_loaded, 16)

            def bias_and_select(g, s):
                t, hh = GROUPS[g]
                keys = P * (t + 1)
                bias = htf[:, :].rearrange("p (i n) -> p i n", i=HEADS)[:, 4 * hh:4 * hh + 4, SEQ - keys:SEQ]
                step(nc.vector.scalar_tensor_tensor(s, s, DH2 ** -0.5, bias, ALU.mult, ALU.add))
                sel = reg[:, SEL + t * SEQ:SEL + t * SEQ + keys]
                step(nc.vector.tensor_tensor(s, s, spread(sel, [[0, 4], [1, keys]]), ALU.add))

            attention(att2, DH2, D // P, 0, bias_and_select, lambda: splits.upto(a_in.end + RING))
            splits.upto(a_out.first + RING)
            norm(n3, a_out, 1.0, 6)
            fused(ffb, f_ffb, gated_unit(ffb, f_ffb), 256)
            norm(n4, ffb, 0.5, 7)
            fused(ffc, f_ffc, gated_unit(ffc, f_ffc), 256)
            norm(n5, ffc, 0.5, 8)

            def stats(n):
                u = B_UNITS[n]
                dve.wait_ge(b_in.gelu_ready, n + 1)
                at = BN + 36 * u.i + 6 * (n // 2)
                return nc.vector.bn_stats(st[:, at:at + 6], reg[:, u.to:u.to + N])

            for n, u in enumerate(B_UNITS):
                splits.upto(u.m + RING)
                vec_wait(9 + n // 4)
                dve.wait_ge(*u.wait)
                if n < 2:
                    dve.wait_ge(n5.rstd_ready, n5.tiles + n + 1)
                nc.vector.scalar_tensor_tensor(reg[:, u.to:u.to + N], mm[:, n % 2, :],
                                               st[:, RSTD + u.i:RSTD + u.i + 1],
                                               vec_of(9 + n // 4, N, (n // 2 % 2) * N), ALU.mult, ALU.add)\
                  .then_inc(b_in.evac, 1)
                if n > 0:
                    stats(n - 1)
            step(stats(len(B_UNITS) - 1))
            for t in range(TT):
                nc.vector.bn_aggr(st[:, MV + 2 * t:MV + 2 * t + 2],
                                  st[:, BN + 36 * t:BN + 36 * t + 36].rearrange("p (c s) -> p c s", s=6))\
                  .then_inc(vln.var_ready, 1)
            fused(mixb, f_mix, mixed_unit, N)
            norm(n6, mixb, 1.0, 21)
            fused(ffd, f_ffd, gated_unit(ffd, f_ffd), 256)
            for t in range(TT):
                add_acc(n7, ffd, t, 0.5)
                rms(n7, t, 22)

        @block.tensor
        def _(pe):
            def product(out, a, b, first, last):
                nc.tensor.matmul(out, a[0], b[0], start=first, stop=False)
                nc.tensor.matmul(out, a[0], b[1], start=False, stop=False)
                return nc.tensor.matmul(out, a[1], b[0], start=False, stop=last)

            def x_tile(k, t):
                return [xt[:, i, k, t * P:(t + 1) * P] for i in range(2)]

            def x_all(k):
                return [xt[:, i, k, :] for i in range(2)]

            def col(m, k, start=0, n=N):
                return [w[:, m % RING, k * N + start:k * N + start + n] for w in (whi, wlo)]

            def row(m, k, half):
                return [w[:, m % RING, k * D + half * N:k * D + (half + 1) * N] for w in (whi, wlo)]

            def wide(m, k, start, n):
                return [w[:, m % RING, k * SEQ + start:k * SEQ + start + n] for w in (whi, wlo)]

            def token_unit(bank, m, t, last, ready, shift=0, between=None):
                for k in range(KD):
                    if between is not None and k == between[0]:
                        between[1]()
                    if k % 4 == 0:
                        pe.wait_ge(lo_done, m + k // 4 + 1 + shift)
                    ins = product(mm[:, bank, :], x_tile(k, t), col(m + k // 4, k % 4), k == 0, k == KD - 1)
                    if last and k % 4 == 3:
                        ins.then_inc(slab_used, 1)
                if not last:
                    ins.then_inc(ready, 1)

            def project(stg, n, u, between=None):
                if n >= 2:
                    if stg is not w_in or n - 2 < GATE_UNIT:
                        pe.wait_ge(stg.evac, n - 1)
                    elif n - 2 == GATE_UNIT:
                        pe.wait_ge(gates.z_ready, 1)
                    else:
                        pe.wait_ge(stg.evac, n - 2)
                if u.kind == "tokens":
                    token_unit(n % 2, u.m, u.i, u.last, stg.unit_ready, between=between)
                elif u.kind == "turned":
                    for j in range(2):
                        for k in range(KD):
                            if k % 4 == 0:
                                pe.wait_ge(lo_done, u.m + k // 4 + 1)
                            ins = product(mm[:, n % 2, j * SEQ:(j + 1) * SEQ],
                                          col(u.m + k // 4, k % 4, (2 * u.i + j) * P, P), x_all(k),
                                          k == 0, k == KD - 1)
                            if u.last and j == 1 and k % 4 == 3:
                                ins.then_inc(slab_used, 1)
                    if not u.last:
                        ins.then_inc(stg.unit_ready, 1)
                else:
                    pe.wait_ge(lo_done, u.m + 1)
                    for k in range(KD):
                        ins = product(mm[:, n % 2, 0:SEQ], wide(u.m, k, 0, P), x_all(k), k == 0, k == KD - 1)
                    if stg is a_in:
                        for t in range(TT):
                            for k in range(KD):
                                ins = product(mm[:, n % 2, SEQ + 8 * t:SEQ + 8 * t + 8], x_tile(k, t),
                                              wide(u.m, k, P, 8), k == 0, k == KD - 1)
                    ins.then_inc(slab_used, 1)

            def out_slabs(stg, following=None):
                n = stg.end - stg.first
                for t in range(TT):
                    for j in range(n):
                        m = stg.first + j
                        if t == 0:
                            pe.wait_ge(lo_done, m + 1)
                        elif j == n - 1 and following is not None:
                            following()
                        for k in range(2):
                            for half in range(2):
                                ins = product(acc[:, 2 * t + half, :], x_tile(2 * j + k, t), row(m, k, half),
                                              j == 0 and k == 0, j == n - 1 and k == 1)
                        if t == 1:
                            ins.then_inc(slab_used, 1)
                        elif j == n - 1:
                            ins.then_inc(stg.acc_ready, 1)

            def turn_norm(n, t, src=None):
                src = xn_tile(t) if src is None else src
                for j in range(2):
                    g = 2 * t + j
                    pe.wait_ge(n.xn_ready, n.halves + g + 1)
                    if g >= 2:
                        pe.wait_ge(n.xt_ready, n.halves + g - 1)
                    for k in range(4):
                        ins = nc.tensor.transpose(tp[:, g % 2, k * P:(k + 1) * P],
                                                  src[:, (4 * j + k) * P:(4 * j + k + 1) * P], idf[:, :])
                    ins.then_inc(n.tp_ready, 1)

            def fused(stg, f, norm, following=None, source=None, spatial=None, at=4):
                def up(c, t, i, between=None):
                    if c > 0 and spatial is None:
                        pe.wait_ge(stg.hid_ready, 2 * c + t - 1 + i * 2 * f.period)
                    if 2 * c + t > 0 and spatial is not None:
                        pe.wait_ge(stg.unit_taken, 2 * c + t)
                    token_unit(t if spatial is None else 0, f.up[c], t, t == 1, stg.unit_ready, i * f.slabs,
                               between)
                    if spatial is not None:
                        spatial(c, t)

                def turn(c, t, i):
                    pe.wait_ge(stg.hl_ready, 2 * c + t + 1 + i * 2 * f.period)
                    for j in range(f.rows):
                        g = f.rows * (2 * c + t) + j
                        if g >= 2:
                            pe.wait_ge(stg.ht_ready, g - 1 + i * 2 * f.rows * f.period)
                        for part in range(2):
                            for q in range(2):
                                ins = nc.tensor.transpose(
                                    tp[:, g % 2, (2 * part + q) * P:(2 * part + q + 1) * P].bitcast(F32R),
                                    hl[:, t, part, (2 * j + q) * P:(2 * j + q + 1) * P], idr[:, :])
                        ins.then_inc(stg.tp_ready, 1)

                def down(c, t, i):
                    pe.wait_ge(stg.ht_ready, f.rows * (2 * c + t + 1) + i * 2 * f.rows * f.period)
                    for q in range(f.tiles):
                        if following is not None and (c, t, q) == (f.chunks - 1, 1, f.tiles - 1):
                            following()
                        m = f.down[c] + q // 2
                        if q % 2 == 0:
                            pe.wait_ge(lo_done, m + 1 + i * f.slabs)
                        for half in range(2):
                            ins = product(acc[:, 2 * t + half, :], [ht[:, t, part, q, :] for part in range(2)],
                                          row(m, q % 2, half), c == 0 and q == 0,
                                          c == f.chunks - 1 and q == f.tiles - 1)
                        if t == 1 and q % 2 == 1:
                            ins.then_inc(slab_used, 1)
                    if c == f.chunks - 1 and t == 0:
                        ins.then_inc(stg.acc_ready, 1)

                def chunk(c, i):
                    up(c, 0, i)
                    turn(c - 1, 1, i)
                    down(c - 1, 0, i)
                    up(c, 1, i)
                    turn(c, 0, i)
                    down(c - 1, 1, i)

                def turn_tile():
                    turn_norm(norm, 1, source)

                up(0, 0, 0, (at, turn_tile) if norm is not None else None)
                if norm is not None:
                    if at == KD:
                        turn_tile()
                    pe.wait_ge(norm.xt_ready, norm.halves + 4)
                up(0, 1, 0)
                turn(0, 0, 0)
                chunk(1, 0)
                last = f.chunks - 1
                if spatial is None:
                    turns(pe, f._replace(chunks=last), 2, chunk)
                else:
                    for c in range(2, last):
                        chunk(c, 0)
                up(last, 0, 0)
                turn(last - 1, 1, 0)
                down(last - 1, 0, 0)
                up(last, 1, 0)
                turn(last, 0, 0)
                down(last, 0, 0)
                down(last - 1, 1, 0)
                turn(last, 1, 0)
                down(last, 1, 0)

            def attention(a, score, value, width, between):
                tiles = HEADS * width // P

                def scores(g):
                    t, hh = GROUPS[g]
                    if g >= 2:
                        pe.wait_ge(a.p_ready, g - 1)
                    keys = P * (t + 1)
                    s = scores_of(g)
                    for i in range(4):
                        ins = score(s[:, i, :], t, 4 * hh + i, keys)
                    ins.then_inc(a.sc_ready, 1)

                def values(g):
                    t, hh = GROUPS[g]
                    pe.wait_ge(a.p_ready, g + 1)
                    for kb in range(t + 1):
                        n = key_blocks(g) + kb
                        if n >= 2:
                            pe.wait_ge(a.pt_ready, n - 1)
                        for i in range(4):
                            p = place_of(g) + (i * (t + 1) + kb) * P
                            ins = nc.tensor.transpose(tp[:, n % 2, i * P:(i + 1) * P], hid[:, p:p + P],
                                                      idf[:, :])
                        ins.then_inc(a.tp_ready, 1)
                    pe.wait_ge(a.pt_ready, key_blocks(g + 1) if g < 3 else 6)
                    if g >= 2:
                        pe.wait_ge(a.att_ready, g - 1)
                    for i in range(4):
                        for kb in range(t + 1):
                            p = place_of(g) + kb * N + i * P
                            ins = nc.tensor.matmul(mm[:, g % 2, i * width:(i + 1) * width], ptf[:, p:p + P],
                                                   value(kb, 4 * hh + i), start=kb == 0, stop=kb == t)
                    ins.then_inc(a.pv_ready, 1)

                def turn_att(t):
                    pe.wait_ge(a.att_ready, 2 * t + 2)
                    for j in range(tiles // 4):
                        g = tiles // 4 * t + j
                        if g >= 2:
                            pe.wait_ge(a.xt_ready, g - 1)
                        for k in range(4):
                            ins = nc.tensor.transpose(tp[:, g % 2, k * P:(k + 1) * P],
                                                      att[:, (4 * j + k) * P:(4 * j + k + 1) * P], idf[:, :])
                        ins.then_inc(a.xtp_ready, 1)

                scores(0)
                scores(1)
                between()
                values(0)
                scores(2)
                values(1)
                scores(3)
                turn_att(0)
                pe.wait_ge(a.xt_ready, tiles // 4)
                values(2)
                values(3)
                turn_att(1)
                pe.wait_ge(a.xt_ready, tiles // 2)

            pe.wait_ge(x_lo, 1)
            for n, u in enumerate(IN_UNITS):
                project(w_in, n, u, (4, lambda: pe.wait_ge(x_lo, 2)) if n == 0 else None)
            pe.wait_ge(small_loaded, 6 * 16)
            nc.tensor.matmul(tp[0:HEADS, 1, 0:DISTS], reg[0:BUCKETS, REL:REL + HEADS],
                             reg[0:BUCKETS, BUCK:BUCK + DISTS], start=True, stop=True).then_inc(table_ready, 1)
            pe.wait_ge(gates.cf_ready, 1)
            pe.wait_ge(const_loaded, 32)
            for t in range(TT):
                ins = nc.tensor.transpose(tp[:, 0, 8 * t:8 * t + 8], reg[0:HEADS, CF + t * P:CF + (t + 1) * P],
                                          idf[0:HEADS, 0:HEADS])
            ins.then_inc(gates.cq_ready, 1)
            pe.wait_ge(w_in.evac, len(IN_UNITS) - 1)

            def score1(out, t, head, keys):
                r, c = half_of(head)
                nc.tensor.matmul(out, reg[r:r + 64, QT1 + c + t * P:QT1 + c + (t + 1) * P],
                                 reg[r:r + 64, KT1 + c:KT1 + c + keys], start=True, stop=False)
                return nc.tensor.matmul(out, spread(idf[0:HEADS, head:head + 1], [[0, P]]),
                                        reg[0:HEADS, NCF:NCF + keys], start=False, stop=True)

            def pooled():
                pe.wait_ge(bands_loaded, 16)
                band = h[:, :, :].rearrange("p t d -> p (t d)")

                def banded(out, t, kind, g, first, last):
                    b = (4 * kind + g) * P
                    return nc.tensor.matmul(out, reg[:, U1 + t * N + g * P:U1 + t * N + (g + 1) * P],
                                            band[:, b:b + P], start=first, stop=last)

                for p in range(2):
                    for q in range(2):
                        g, o = 2 * p + q, q * SEQ
                        banded(mm[:, p, o:o + P], 0, 0, g, True, True)
                        banded(mm[:, p, o + P:o + SEQ], 1, 1, g, True, False)
                        ins = banded(mm[:, p, o + P:o + SEQ], 0, 2, g, False, True)
                    ins.then_inc(pool.d_ready, 1)
                for p in range(2):
                    pe.wait_ge(pool.d_copied, p + 1)
                    for q in range(2):
                        g = 2 * p + q
                        ins = nc.tensor.matmul(mm[:, p, q * SEQ:(q + 1) * SEQ],
                                               reg[:, POOLW + g * P:POOLW + (g + 1) * P],
                                               htf[:, g * SEQ:(g + 1) * SEQ], start=True, stop=True)
                    ins.then_inc(pool.y_ready, 1)
                pe.wait_ge(pool.y_scaled, 4)

            attention(att1, score1, lambda kb, head: reg[:, V1 + kb * N + head * DH1:
                                                         V1 + kb * N + (head + 1) * DH1], DH1, pooled)
            pe.wait_ge(pool.xt_ready, 1)
            out_slabs(w_out, lambda: turn_norm(n0, 0, h[:, 0, :]))
            pe.wait_ge(n0.xt_ready, n0.halves + 2)
            pe.wait_ge(idr_ready, 1)
            fused(mlp, f_mlp, n0, lambda: turn_norm(n1, 0), h[:, 1, :], at=KD)

            pe.wait_ge(n1.xt_ready, n1.halves + 2)
            fused(ffa, f_ffa, n1, at=KD)
            turn_norm(n2, 0)
            pe.wait_ge(n2.xt_ready, n2.halves + 2)

            def index_scores(g):
                t, hh = GROUPS[g]
                if g == 0:
                    pe.wait_ge(a_in.evac, QI_UNIT + 1)
                if g >= 2:
                    pe.wait_ge(idx.relu_ready, g - 1)
                keys = P * (t + 1)
                for i in range(4):
                    head = 4 * hh + i
                    r, c = half_of(head)
                    ins = nc.tensor.matmul(scores_of(g)[:, i, :],
                                           hid[r:r + 64, c + t * P:c + (t + 1) * P],
                                           reg[r:r + 64, KI:KI + keys], start=True, stop=True)
                ins.then_inc(idx.rel_ready, 1)

            for n, u in enumerate(A_UNITS):
                project(a_in, n, u, (6, lambda: turn_norm(n2, 1)) if n == 0 else None)
                if n == 0:
                    pe.wait_ge(n2.xt_ready, n2.halves + 4)
                if n in INDEX_AFTER:
                    index_scores(INDEX_AFTER[n])
            pe.wait_ge(a_in.evac, len(A_UNITS))
            pe.wait_ge(idx.relu_ready, 4)

            def score2(out, t, head, keys):
                c = head * SEQ
                return nc.tensor.matmul(out, reg[:, QT2 + c + t * P:QT2 + c + (t + 1) * P],
                                        reg[:, KT2 + c:KT2 + c + keys], start=True, stop=True)

            attention(att2, score2, lambda kb, head: reg[:, V2 + kb * D + head * DH2:
                                                         V2 + kb * D + (head + 1) * DH2], DH2, lambda: None)
            out_slabs(a_out, lambda: turn_norm(n3, 0))
            pe.wait_ge(n3.xt_ready, n3.halves + 2)
            fused(ffb, f_ffb, n3, lambda: turn_norm(n4, 0))
            pe.wait_ge(n4.xt_ready, n4.halves + 2)
            fused(ffc, f_ffc, n4, lambda: turn_norm(n5, 0))
            pe.wait_ge(n5.xt_ready, n5.halves + 2)
            for n, u in enumerate(B_UNITS):
                project(b_in, n, u, (4, lambda: turn_norm(n5, 1)) if n == 0 else None)
                if n == 0:
                    pe.wait_ge(n5.xt_ready, n5.halves + 4)
            pe.wait_ge(b_in.evac, len(B_UNITS))
            pe.wait_ge(wsp_masked, 1)

            def spatial(c, t):
                pe.wait_ge(vln.done, 2 * c + t + 1)
                if 2 * c + t > 0:
                    pe.wait_ge(mixb.hid_ready, 2 * c + t)
                for g, a, b in mix_pieces(c):
                    v = VB + t * HALF_B + c * N
                    ins = nc.tensor.matmul(mm[:, 1, a:b], reg[:, WSP + g * P:WSP + (g + 1) * P],
                                           reg[:, v + a:v + b], start=True, stop=True)
                ins.then_inc(mixb.mix_ready, 1)

            fused(mixb, f_mix, None, lambda: turn_norm(n6, 0), spatial=spatial)
            pe.wait_ge(n6.xt_ready, n6.halves + 2)
            fused(ffd, f_ffd, n6)


def mix_pieces(c):
    out, at = [], c * N
    while at < (c + 1) * N:
        g = at // GROUP_B
        end = min((g + 1) * GROUP_B, (c + 1) * N)
        out.append((g, at - c * N, end - c * N))
        at = end
    return out


def bands():
    s, to = np.arange(P)[:, None], np.arange(P)[None, :]
    out = np.zeros((P, 3, len(WINDOWS), P), np.float32)
    for g, w in enumerate(WINDOWS):
        back = to - s
        near = (back >= 0) & (back < w)
        out[:, 0, g] = near / np.minimum(to + 1, w) - (back == 0)
        out[:, 1, g] = near / w - (back == 0)
        out[:, 2, g] = (back + P < w) / w
    return out.reshape(P, -1)


def bucket_rows():
    d = np.maximum(SEQ - 1 - np.arange(DISTS), 0)
    half = BUCKETS // 2
    far = np.log(np.maximum(d, 1).astype(np.float32) / np.float32(half)) / np.float32(np.log(MAX_DIST / half))
    bucket = np.where(d < half, d, np.minimum(half + (far * np.float32(half)).astype(np.int32), BUCKETS - 1))
    return (np.arange(BUCKETS)[:, None] == bucket[None, :]).astype(np.float32)


def kernel(**inputs):
    import concourse.bacc as bacc
    from concourse.bass_utils import run_bass_kernel_spmd

    a = {k: np.asarray(v) for k, v in inputs.items()}
    x, w_in, w_mix = a["x"][0], a["w_in"][0], a["a_w_in_2"][0]
    q = WIDTH
    fout = 4 * WIDTH
    gate = np.zeros((D, P), w_in.dtype)
    gate[:, :HEADS] = w_in[:, fout:fout + HEADS]
    qi, ki = 3 * D, 3 * D + HEADS * DI
    key = w_mix[:, ki:ki + DI]
    index = np.concatenate([key, key, w_mix[:, ki + DI:ki + DI + HEADS]], 1)

    def ffn(l, i):
        up, down = a["ffn_w_in_2"][l, i], a["ffn_w_out_2"][l, i]
        return fused_slabs(up, down, 256, DFF2 // 256,
                           lambda c: np.r_[256 * c:256 * c + 256, DFF2 + 256 * c:DFF2 + 256 * c + 256])

    b_in = a["b_w_in_2"][0]

    def cols(w, start):
        return column_slabs(w, np.r_[start:start + N])

    def paired(w, start):
        heads = start + np.arange(HEADS * 64).reshape(2, 2, 2, 64)
        return column_slabs(w, heads.transpose(0, 2, 1, 3).reshape(-1))

    slabs = np.concatenate(
        [cols(w_in, 0), wide_slab(gate), cols(w_in, 3 * q), paired(w_in, q), paired(w_in, 2 * q),
         row_slabs(a["w_out"][0]),
         fused_slabs(a["w_mlp1"][0], a["w_mlp2"][0], 512, DFF1 // 512, lambda c: np.r_[512 * c:512 * c + 512]),
         ffn(0, 0),
         cols(w_mix, 2 * D), wide_slab(index), paired(w_mix, qi), cols(w_mix, 2 * D + N),
         cols(w_mix, 0), cols(w_mix, N), cols(w_mix, D), cols(w_mix, D + N),
         row_slabs(a["a_w_out_2"][0]), ffn(0, 1), ffn(1, 0)]
        + [cols(b_in, HALF_B + N * c) for c in range(HALF_B // N)]
        + [fused_slabs(b_in, a["b_w_out_2"][0], 512, HALF_B // 512, lambda c: np.r_[512 * c:512 * c + 512]),
           ffn(1, 1)])

    g2 = a["norm_g_2"]
    rows = {"ln1_g": a["ln1_g"][0], "ln1_b": a["ln1_b"][0], "ln2_g": a["ln2_g"][0], "ln2_b": a["ln2_b"][0],
            "final": a["final_g_2"]}
    for i in range(6):
        rows[f"norm{i}"] = g2[i // 3, i % 3]
    for j in range(3):
        part = slice(j * D, (j + 1) * D)
        rows[f"bias_u{j}"] = a["b_b_in_2"][0][:HALF_B][part]
        rows[f"bias_v{j}"] = a["b_b_in_2"][0][HALF_B:][part]
        rows[f"gate_g{j}"], rows[f"gate_b{j}"] = a["b_ln_g_2"][0][part], a["b_ln_b_2"][0][part]

    s, to = np.arange(P)[None, :], np.arange(P)[:, None]
    arrays = {
        "slabs": slabs,
        "vectors": np.stack([rows[v] for v in VECTORS]),
        "x": x,
        "x_turned": x.T.reshape(KD, P, SEQ).transpose(1, 0, 2).reshape(P, 2, 1024),
        "identity": np.eye(P, dtype=np.float32),
        "causal": np.where(s <= to, 0.0, MASKED).astype(np.float32),
        "bands": bands(),
        "buckets": bucket_rows(),
        "rel_table": a["rel_table_2"],
        "pool_w": a["pool_w"][0].transpose(1, 0, 2).reshape(P, -1),
        "pool_scale": a["pool_scale"][0].reshape(4, P).T,
        "b_f": a["b_f"][0].reshape(HEADS, 1),
        "w_sp": a["b_w_sp_2"][0].transpose(2, 0, 1).reshape(P, -1),
        "b_sp": a["b_b_sp_2"][0].T,
    }
    arrays = {k: np.ascontiguousarray(v) for k, v in arrays.items()}
    nc = bacc.Bacc("TRN2", target_bir_lowering=False, num_devices=1)
    dr = {k: nc.dram_tensor(f"{k}_dram", v.shape, F32, kind="ExternalInput").ap() for k, v in arrays.items()}
    dr["table"] = nc.dram_tensor("table_dram", [HEADS, DISTS], F32, kind="Internal").ap()
    dr["tables"] = nc.dram_tensor("tables_dram", [P, HEADS * DISTS], F32, kind="Internal").ap()
    dr["out"] = nc.dram_tensor("out_dram", [SEQ, D], F32, kind="ExternalOutput").ap()
    build(nc, dr)
    r = run_bass_kernel_spmd(nc, [{f"{k}_dram": v for k, v in arrays.items()}], core_ids=[0])
    return r.results[0]["out_dram"].reshape(1, SEQ, D)
```

```python
from collections import namedtuple
from contextlib import ExitStack

import numpy as np

import concourse.bass as bass
from concourse import mybir

F32 = mybir.dt.float32
F32R = mybir.dt.float32r
ACT = mybir.ActivationFunctionType
ALU = mybir.AluOpType
AX_X = mybir.AxisListType.X

P = 128
SEQ = 256
TT = SEQ // P
D = 1024
KD = D // P
N = 512
SLAB = 2048
RAW = 3
RING = 6
VW = 1024
VRING = 3
WIDTH = 512
HEADS = 8
DH1, DH2 = 64, 128
DI = 64
DFF1, DFF2, HALF_B = 4096, 2816, 3072
GROUP_B = HALF_B // 8
TOPK = 64
WINDOWS = (2, 4, 8, 16)
ALPHA = float(2.0 ** 0.25)
LN_EPS, EPS = 1e-5, 1e-6
MASKED, TAKEN = -1e30, -3e38
BUCKETS, MAX_DIST = 32, 2048
DISTS = 384

VECTORS = (["ln1_g", "ln1_b", "ln2_g", "ln2_b"] + [f"norm{i}" for i in range(5)]
           + [f"bias_v{j}" for j in range(3)]
           + [f"{w}{j}" for j in range(3) for w in ("gate_g", "gate_b", "bias_u")]
           + ["norm5", "final"])


def column_slabs(w, cols):
    part = w[:, cols].reshape(2, 4, P, N)
    return part.transpose(0, 2, 1, 3).reshape(2, P, SLAB)


def row_slabs(w):
    return w.reshape(-1, 2, P, D).transpose(0, 2, 1, 3).reshape(-1, P, SLAB)


def wide_slab(w):
    out = np.zeros((KD, P, 256), w.dtype)
    out[:, :, :w.shape[1]] = w.reshape(KD, P, -1)
    return out.transpose(1, 0, 2).reshape(1, P, SLAB)


def fused_slabs(up, down, width, chunks, cols):
    rows = row_slabs(down).reshape(chunks, width // 256, P, SLAB)
    out = []
    for c in range(chunks):
        out.append(column_slabs(up, cols(c)))
        if c:
            out.append(rows[c - 1])
    return np.concatenate(out + [rows[chunks - 1]])


class Splits:

    def __init__(self, one, total):
        self.next, self.one, self.total = 0, one, total

    def upto(self, end):
        while self.next < min(end, self.total):
            self.one(self.next)
            self.next += 1


def spread(ap, dims):
    return bass.AP(tensor=ap.tensor, offset=ap.offset, ap=[ap.ap[0]] + dims)


Fused = namedtuple("Fused", "chunks tiles rows s lead period slabs loads start up down")
Unit = namedtuple("Unit", "kind m i last to factor wait")


def fused_shape(first, end, chunks, tiles):
    rows = tiles // 2
    s = 2 + rows
    period = 2 if s == 3 else 3
    return Fused(
        chunks=chunks, tiles=tiles, rows=rows, s=s, lead=RING - s, period=period,
        slabs=s * period, loads=16 * s * period // RAW,
        start=first + 2 + RING - s,
        up=[first] + [first + 2 + s * c for c in range(chunks)],
        down=[first + 4 + s * c for c in range(chunks - 1)] + [end - rows])


def build(nc, dr):
    with ExitStack() as ctx:
        def sb(name, shape, dt=F32):
            return ctx.enter_context(nc.sbuf_tensor(name, shape, dt))

        def also(name, shape, words):
            return nc.alloc_sbuf_tensor_at(name, shape, F32, offset=nc.sbuf_base - 4 * words)

        def sem(name):
            return ctx.enter_context(nc.semaphore(name))

        def stage(name, signals, first=0, count=0):
            return namedtuple(name, "first end " + signals)(
                first, first + count, *[sem(f"{name}_{s}") for s in signals.split()])

        raw = sb("raw", [P, RAW, SLAB])
        whi = sb("whi", [P, RING, SLAB], F32R)
        wlo = sb("wlo", [P, RING, SLAB], F32R)
        vec = sb("vec", [P, VRING, VW])
        h = sb("h", [P, TT, D])
        xt = sb("xt", [P, 2, KD, SEQ], F32R)
        hid = sb("hid", [P, 2 * N])
        hl = sb("hl", [P, 2, 2, N], F32R)
        hlf = also("hlf", [P, 2, 1024], 2048)
        ht = sb("ht", [P, 2, 2, 4, P], F32R)
        htf = also("htf", [P, 2048], 2048)
        reg = sb("reg", [P, 7168])
        idr = sb("idr", [P, P], F32R)
        idf = sb("idf", [P, P])
        causal = sb("causal", [P, P])
        st = sb("st", [P, 192])
        acc = ctx.enter_context(nc.psum_tensor("acc", [P, 4, N], F32))
        mm = ctx.enter_context(nc.psum_tensor("mm", [P, 2, N], F32))
        tp = ctx.enter_context(nc.psum_tensor("tp", [P, 2, N], F32))

        SQ, RSTD, VAR, MV, BN, WI, BSP, PSC, BF, LRSTD = 0, 2, 4, 6, 10, 82, 98, 106, 110, 166
        CQ, MX, NEG, RS, REC, HALF, TOP = 112, 128, 132, 168, 148, 152, 156
        U1, V1, QT1, KT1, CF, NCF, GZ, GE = 0, 1024, 2048, 3072, 4096, 4352, 4608, 4864
        POOLW, BUCK, TABLE, REL, ONES = 5120, 5632, 6016, 6400, 6656
        QT2, KT2, V2, KI, SCORE, SEL = 0, 2048, 4096, 6144, 6400, 6656
        VB, WSP = 0, 6144

        raw_loaded = [sem(f"raw_loaded{i}") for i in range(RAW)]
        vec_loaded = [sem(f"vec_loaded{i}") for i in range(VRING)]
        hi_done, lo_done, slab_used = sem("hi_done"), sem("lo_done"), sem("slab_used")
        const_loaded, half_set, idr_ready = sem("const_loaded"), sem("half_set"), sem("idr_ready")
        small_loaded, bands_loaded, h_loaded = sem("small_loaded"), sem("bands_loaded"), sem("h_loaded")
        x_loaded, x_hi, x_lo = [sem("x_loaded0"), sem("x_loaded1")], sem("x_hi"), sem("x_lo")
        table_ready, table_copied = sem("table_ready"), sem("table_copied")
        table_stored, tables_stored = sem("table_stored"), sem("tables_stored")
        bias_loaded, wsp_loaded, wsp_masked = sem("bias_loaded"), sem("wsp_loaded"), sem("wsp_masked")
        vector_step, stored = sem("vector_step"), sem("stored")
        LAYER = "var_ready eps_added rstd_ready"
        FUSED = "unit_ready gate_ready hid_ready hl_hi hl_ready tp_ready ht_ready acc_ready"
        PROJ = "unit_ready evac"
        ATT = ("sc_ready bias_ready p_ready tp_ready pt_ready pv_ready att_ready "
               "xtp_ready hi_ready xt_ready")
        NORM = "sum_ready sq_ready eps_added rstd_ready xn_ready tp_ready hi_ready xt_ready"
        Norm = namedtuple("Norm", "tiles halves split_to " + NORM)
        norm_sems = [sem(f"norm_{s}") for s in NORM.split()]

        def norm_stage(i, split_to=0):
            return Norm(TT * max(i - 1, 0), 2 * TT * i, split_to, *norm_sems)

        at = [0]

        def slabs(n):
            at[0] += n
            return dict(first=at[0] - n, count=n)

        w_in = stage("w_in", PROJ, **slabs(9))
        gates = stage("gates", "z_ready abs_ready exp_ready ln_ready cf_ready nc_hi nc_ready cq_ready")
        pool = stage("pool", "d_ready d_copied y_ready y_scaled hi_ready xt_ready")
        att1 = stage("att1", ATT)
        w_out = stage("w_out", "acc_ready", **slabs(4))
        l0 = stage("l0", LAYER)
        mlp = stage("mlp", FUSED, **slabs(4 * (DFF1 // 512)))
        l1 = stage("l1", LAYER)
        ffa = stage("ffa", FUSED, **slabs(3 * (DFF2 // 256)))
        a_in = stage("a_in", PROJ, **slabs(15))
        idx = stage("idx", "rel_ready relu_ready rel_used sel_ready")
        att2 = stage("att2", ATT)
        a_out = stage("a_out", "acc_ready", **slabs(4))
        ffb = stage("ffb", FUSED, **slabs(3 * (DFF2 // 256)))
        ffc = stage("ffc", FUSED, **slabs(3 * (DFF2 // 256)))
        b_in = stage("b_in", PROJ + " gelu_ready", **slabs(12))
        vln = stage("vln", LAYER + " done")
        mixb = stage("mixb", FUSED + " unit_taken mix_ready", **slabs(4 * (HALF_B // 512)))
        ffd = stage("ffd", FUSED, **slabs(3 * (DFF2 // 256)))
        SLABS = at[0]

        f_mlp = fused_shape(mlp.first, mlp.end, DFF1 // 512, 4)
        f_mix = fused_shape(mixb.first, mixb.end, HALF_B // 512, 4)
        f_ffa, f_ffb, f_ffc, f_ffd = (fused_shape(s.first, s.end, DFF2 // 256, 2) for s in (ffa, ffb, ffc, ffd))

        n0, n1, n2, n3, n4, n5, n6, n7 = (norm_stage(i, end) for i, end in enumerate(
            (f_mlp.start, f_ffa.start, ffa.end + RING, f_ffb.start, f_ffc.start, ffc.end + RING,
             f_ffd.start, 0)))

        def unit_list(stg, parts):
            out, m, ready = [], stg.first, 0
            for kind, dest, step, factor in parts:
                for i in range(1 if kind == "wide" else 2):
                    last = kind == "wide" or i == 1
                    ready += not last
                    out.append(Unit(
                        kind=kind, m=m, i=i, last=last, to=None if dest is None else dest + i * step,
                        factor=factor,
                        wait=(slab_used, m + (1 if kind == "wide" else 2)) if last
                        else (stg.unit_ready, ready)))
                m += 1 if kind == "wide" else 2
            assert m == stg.end
            return out

        IN_UNITS = unit_list(w_in, [("tokens", V1, N, None), ("wide", 0, 0, None), ("turned", QT1, N, DH1 ** -0.5),
                                    ("turned", KT1, N, None), ("tokens", U1, N, None)])
        A_UNITS = unit_list(a_in, [("tokens", V2, D, None), ("wide", 0, 0, None), ("turned", None, 0, None),
                                   ("turned", QT2, N, None), ("turned", QT2 + D, N, None),
                                   ("turned", KT2, N, None), ("turned", KT2 + D, N, None),
                                   ("tokens", V2 + N, D, None)])
        B_UNITS = unit_list(b_in, [("tokens", VB + c * N, HALF_B, None) for c in range(HALF_B // N)])
        LAST_A = len(A_UNITS) - 1
        GATE_UNIT = 2
        QI_UNIT = 4
        INDEX_AFTER = {4: 0, 5: 1, 8: 2, 9: 3}
        SELECT_AFTER = {6: (0, 0), 7: (0, 1), 9: (1, 0), 10: (1, 1)}

        GROUPS = [(t, hh) for t in range(TT) for hh in range(2)]
        ptf, att = hlf[:, 0, :], hlf[:, 1, :]
        nc_hi, nc_lo = hl[0:HEADS, 1, 1, 0:SEQ], hl[0:HEADS, 1, 1, SEQ:2 * SEQ]

        def scores_of(g):
            pair = acc[:, 2 * (g % 2):2 * (g % 2) + 2, :].rearrange("p b (i n) -> p (b i) n", i=2)
            return pair[:, :, 0:P * (GROUPS[g][0] + 1)]

        def half_of(head):
            return 64 * (head % 4 // 2), (2 * (head // 4) + head % 2) * SEQ

        def by_head(ap):
            return ap.rearrange("p (i n) -> p i n", i=4)

        def place_of(g):
            return N * g if GROUPS[g][0] == 0 else 0

        def key_blocks(g):
            return sum(t + 1 for t, _ in GROUPS[:g])

        def xn_tile(t):
            return hid[:, :] if t == 0 else hlf[:, 1, :]

        def acc_done(eng, src, t):
            if t == 0:
                eng.wait_ge(src.acc_ready, 1)
            else:
                eng.wait_ge(slab_used, src.end)

        def unit_done(eng, stg, f, c, t, i):
            if t == 0:
                eng.wait_ge(stg.unit_ready, c + 1 + i * f.period)
            else:
                eng.wait_ge(slab_used, f.up[c] + 2 + i * f.slabs)

        def turns(eng, f, first, body):
            last = f.chunks - 1
            c, full = first, (last - first) // f.period
            if full > 1:
                with eng.Fori(0, full) as i:
                    for r in range(f.period):
                        body(c + r, i)
                c += full * f.period
            while c < last:
                body(c, 0)
                c += 1

        block = ctx.enter_context(nc.Block())

        @block.sync
        def _(sp):
            def load(m, i=0):
                if m >= RAW:
                    sp.wait_ge(lo_done, m - RAW + 1 + i * RAW)
                sp.dma_start(raw[:, m % RAW, :], dr["slabs"][m + i * RAW]).then_inc(raw_loaded[m % RAW], 16)

            for m in range(RAW):
                if m < 2:
                    sp.dma_start(hlf[:, m, :], dr["x_turned"][:, m, :]).then_inc(x_loaded[m], 16)
                load(m)
            rounds = (SLABS - RAW) // RAW
            with sp.Fori(0, rounds) as i:
                for m in range(RAW, 2 * RAW):
                    load(m, i)
            for m in range(RAW * (rounds + 1), SLABS):
                load(m)
            for t in range(TT):
                for j in range(2):
                    sp.wait_ge(n7.xn_ready, n7.halves + 2 * t + j + 1)
                    sp.dma_start(dr["out"][t * P:(t + 1) * P, j * N:(j + 1) * N],
                                 xn_tile(t)[:, j * N:(j + 1) * N]).then_inc(stored, 16)
            sp.wait_ge(stored, 16 * 2 * TT)

        @block.gpsimd
        def _(pq):
            def load_vec(v, free, count):
                if free is not None:
                    pq.wait_ge(free, count)
                src = dr["vectors"][v]
                pq.dma_start(vec[:, v % VRING, :],
                             bass.AP(tensor=src.tensor, offset=src.offset, ap=[[0, P], [1, VW]]))\
                  .then_inc(vec_loaded[v % VRING], 16)

            def power(n, value, eps, t, ready, base=0, to=LRSTD):
                pq.wait_ge(ready, base + t + 1)
                nc.gpsimd.tensor_scalar(st[:, VAR + t:VAR + t + 1], st[:, value:value + 1], eps, None,
                                        ALU.add).then_inc(n.eps_added, 1)
                pq.wait_ge(n.eps_added, base + t + 1)
                nc.gpsimd.tensor_tensor(st[:, to + t:to + t + 1], st[:, VAR + t:VAR + t + 1],
                                        st[:, HALF:HALF + 1], ALU.pow).then_inc(n.rstd_ready, 1)

            def rms(n):
                for t in range(TT):
                    power(n, SQ + t, EPS, t, n.sq_ready, n.tiles, RSTD)

            pq.dma_start(idf[:, :], dr["identity"]).then_inc(const_loaded, 16)
            pq.dma_start(causal[:, :], dr["causal"]).then_inc(const_loaded, 16)
            for place, name in ((reg[0:BUCKETS, BUCK:BUCK + DISTS], "buckets"),
                                (reg[0:BUCKETS, REL:REL + HEADS], "rel_table"),
                                (reg[:, POOLW:POOLW + 4 * P], "pool_w"),
                                (st[:, PSC:PSC + 4], "pool_scale"),
                                (st[0:HEADS, BF:BF + 1], "b_f"),
                                (st[:, BSP:BSP + 8], "b_sp")):
                pq.dma_start(place, dr[name]).then_inc(small_loaded, 16)
            nc.gpsimd.memset(st[:, HALF:HALF + 1], -0.5).then_inc(half_set, 1)
            pq.wait_ge(gates.z_ready, 1)
            pq.dma_start(h[:, :, :].rearrange("p t d -> p (t d)")[:, 0:12 * P], dr["bands"])\
              .then_inc(bands_loaded, 16)
            for v in range(VRING):
                load_vec(v, None, 0)
            pq.wait_ge(table_copied, 1)
            pq.dma_start(dr["table"], reg[0:HEADS, TABLE:TABLE + DISTS]).then_inc(table_stored, 16)
            pq.wait_ge(pool.d_ready, 2)
            for t in range(TT):
                pq.dma_start(h[:, t, :], dr["x"][t * P:(t + 1) * P, :]).then_inc(h_loaded, 16)
            pq.wait_ge(half_set, 1)
            for t in range(TT):
                power(l0, MV + 2 * t + 1, LN_EPS, t, l0.var_ready)
            load_vec(3, n0.xn_ready, n0.halves + 4)
            load_vec(4, n0.xn_ready, n0.halves + 4)
            pq.wait_ge(table_stored, 16)
            table, tables = dr["table"], dr["tables"]
            pq.dma_start(tables, bass.AP(tensor=table.tensor, offset=table.offset,
                                         ap=[[0, P], [1, HEADS * DISTS]])).then_inc(tables_stored, 16)
            for t in range(TT):
                power(l1, MV + 2 * t + 1, LN_EPS, t, l1.var_ready)
                power(n1, SQ + t, EPS, t, n1.sq_ready, n1.tiles, RSTD)
            load_vec(5, n1.sum_ready, n1.tiles + 2)
            load_vec(6, n1.sum_ready, n1.tiles + 2)
            load_vec(7, n1.xn_ready, n1.halves + 4)
            rms(n2)
            load_vec(8, n2.xn_ready, n2.halves + 4)
            pq.wait_ge(tables_stored, 16)
            pq.dma_start(htf[:, :].rearrange("p (i n) -> p i n", i=HEADS),
                         bass.AP(tensor=tables.tensor, offset=tables.offset + P - 1,
                                 ap=[[HEADS * DISTS - 1, P], [DISTS, HEADS], [1, SEQ]]))\
              .then_inc(bias_loaded, 16)
            rms(n3)
            load_vec(9, n3.xn_ready, n3.halves + 4)
            pq.dma_start(reg[:, WSP:WSP + 8 * P], dr["w_sp"]).then_inc(wsp_loaded, 16)
            pq.wait_ge(wsp_loaded, 16)
            w_sp = reg[:, WSP:WSP + 8 * P].rearrange("p (g n) -> p g n", g=8)
            nc.gpsimd.affine_select(out=w_sp, in_=w_sp, compare_op=ALU.is_ge, fill=0.0, base=0,
                                    pattern=[[0, 8], [1, P]], channel_multiplier=-1).then_inc(wsp_masked, 1)
            rms(n4)
            load_vec(10, n4.xn_ready, n4.halves + 4)
            rms(n5)
            load_vec(11, n5.xn_ready, n5.halves + 4)
            for j in range(3):
                load_vec(12 + j, b_in.evac, 4 * j + 4)
            for t in range(TT):
                power(vln, MV + 2 * t + 1, EPS, t, vln.var_ready)
            for j in range(2):
                load_vec(15 + 3 * j, vln.done, 4 * j + 4)
                load_vec(16 + 3 * j, vln.done, 4 * j + 4)
                load_vec(17 + 3 * j, mixb.unit_taken, 4 * j + 4)
            load_vec(21, vln.done, 12)
            load_vec(22, vln.done, 12)
            rms(n6)
            rms(n7)

        @block.scalar
        def _(act):
            def hi(m, f=None, i=0):
                act.wait_ge(raw_loaded[m % RAW], 16 * (m // RAW + 1) + (i * f.loads if f else 0))
                if m >= RING:
                    act.wait_ge(slab_used, m - RING + 1 + (i * f.slabs if f else 0))
                nc.scalar.activation(whi[:, m % RING, :], raw[:, m % RAW, :], ACT.Copy).then_inc(hi_done, 1)

            splits = Splits(hi, SLABS)

            def tp_to_xt(ready, g, k, t, done):
                act.wait_ge(ready, g + 1)
                nc.scalar.activation(xt[:, 0, k:k + 4, t * P:(t + 1) * P], by_head(tp[:, g % 2, :]),
                                     ACT.Copy).then_inc(done, 1)

            def square(n, t):
                act.wait_ge(n.sum_ready, n.tiles + t + 1)
                if t > 0:
                    act.wait_ge(n.sq_ready, n.tiles + t)
                nc.scalar.activation(hlf[:, 0, :], h[:, t, :], ACT.Square,
                                     scale=D ** -0.5, accum_out=st[:, SQ + t:SQ + t + 1])\
                  .then_inc(n.sq_ready, 1)

            def norm(n, squares=True, first=False):
                for t in range(TT):
                    if first:
                        square(n, t)
                    for j in range(2):
                        tp_to_xt(n.tp_ready, n.halves + 2 * t + j, 4 * j, t, n.hi_ready)
                    if squares and not first:
                        square(n, t)
                    if t == 0:
                        splits.upto(min(splits.next + 1, n.split_to))

            def fused(stg, f, gate, width):
                def hidden_hi(c, t, i):
                    act.wait_ge(stg.hid_ready, 2 * c + t + 1 + i * 2 * f.period)
                    if c > 0:
                        act.wait_ge(stg.tp_ready, f.rows * (2 * c + t - 1) + i * 2 * f.rows * f.period)
                    nc.scalar.activation(hl[:, t, 0, 0:width], hid[:, t * N:t * N + width], ACT.Copy)\
                      .then_inc(stg.hl_hi, 1)

                def turned(c, t, i, place=None):
                    place = t if place is None else place
                    for j in range(f.rows):
                        g = f.rows * (2 * c + t) + j
                        act.wait_ge(stg.tp_ready, g + 1 + i * 2 * f.rows * f.period)
                        nc.scalar.activation(ht[:, place, :, 2 * j:2 * j + 2, :],
                                             tp[:, g % 2, :].rearrange("p (i q n) -> p i q n", i=2, q=2),
                                             ACT.Copy).then_inc(stg.ht_ready, 1)

                def chunk(c, i):
                    m = f.up[c] + f.lead
                    for j in range(f.s - 1):
                        hi(m + j, f, i)
                    gate(c, 0, i)
                    turned(c - 1, 1, i)
                    hidden_hi(c, 0, i)
                    hi(m + f.s - 1, f, i)
                    gate(c, 1, i)
                    turned(c, 0, i)
                    hidden_hi(c, 1, i)

                splits.upto(f.start - 1)
                gate(0, 0, 0)
                hidden_hi(0, 0, 0)
                splits.upto(f.start)
                gate(0, 1, 0)
                turned(0, 0, 0)
                hidden_hi(0, 1, 0)
                turns(act, f, 1, chunk)
                last = f.chunks - 1
                splits.next = f.up[last] + f.lead
                splits.upto(f.up[last] + f.lead + f.s - 1)
                gate(last, 0, 0)
                turned(last - 1, 1, 0)
                hidden_hi(last, 0, 0)
                turned(last, 0, 0)
                splits.upto(f.up[last] + f.lead + f.s)
                gate(last, 1, 0)
                hidden_hi(last, 1, 0)
                splits.upto(stg.end + 4 - f.rows)
                turned(last, 1, 0, place=0)

            def silu_gate(stg, f, n):
                def gate(c, t, i):
                    unit_done(act, stg, f, c, t, i)
                    if c == 0:
                        act.wait_ge(n.rstd_ready, n.tiles + t + 1)
                    nc.scalar.activation(hid[:, t * N:t * N + 256], mm[:, t, 0:256], ACT.Silu,
                                         scale=st[:, RSTD + t:RSTD + t + 1])\
                      .then_inc(stg.gate_ready, 1)
                return gate

            def relu_gate(c, t, i):
                unit_done(act, mlp, f_mlp, c, t, i)
                if c > 0:
                    act.wait_ge(mlp.hl_ready, 2 * c + t - 1 + i * 2 * f_mlp.period)
                nc.scalar.activation(hid[:, t * N:(t + 1) * N], mm[:, t, :], ACT.Relu)\
                  .then_inc(mlp.gate_ready, 1)

            def gelu_gate(c, t, i):
                act.wait_ge(mixb.unit_taken, 2 * c + t + 1 + i * 2 * f_mix.period)
                nc.scalar.activation(hid[:, t * N:(t + 1) * N], hid[:, t * N:(t + 1) * N],
                                     ACT.Gelu_apprx_tanh).then_inc(mixb.gate_ready, 1)

            def attention(a, tiles, base, end, between):
                def exps(g):
                    act.wait_ge(a.bias_ready, g + 1)
                    if g >= 2:
                        act.wait_ge(a.tp_ready, key_blocks(g))
                    keys = P * (GROUPS[g][0] + 1)
                    s = scores_of(g)
                    for i in range(4):
                        n, r = NEG + 4 * (g % 2) + i, RS + 4 * g + i
                        ins = nc.scalar.activation(
                            hid[:, place_of(g) + i * keys:place_of(g) + (i + 1) * keys],
                            s[:, i, :], ACT.Exp, bias=st[:, n:n + 1],
                            accum_out=st[:, r:r + 1])
                    ins.then_inc(a.p_ready, 1)

                def turned(g):
                    if g >= 2:
                        act.wait_ge(a.pv_ready, g)
                    for kb in range(GROUPS[g][0] + 1):
                        n = key_blocks(g) + kb
                        act.wait_ge(a.tp_ready, n + 1)
                        nc.scalar.activation(ptf[:, place_of(g) + kb * N:place_of(g) + (kb + 1) * N],
                                             tp[:, n % 2, :], ACT.Copy).then_inc(a.pt_ready, 1)

                def to_xt(t):
                    for j in range(tiles // 4):
                        tp_to_xt(a.xtp_ready, tiles // 4 * t + j, base + 4 * j, t, a.hi_ready)

                exps(0)
                exps(1)
                splits.upto(end + 1)
                between()
                turned(0)
                turned(1)
                splits.upto(end + 4)
                exps(2)
                to_xt(0)
                turned(2)
                exps(3)
                turned(3)
                splits.upto(end + RING - 1)
                to_xt(1)
                splits.upto(end + RING)

            for j in range(2):
                act.wait_ge(x_loaded[j], 16)
                nc.scalar.activation(xt[:, 0, 4 * j:4 * j + 4, :].rearrange("p k n -> p (k n)"),
                                     hlf[:, j, :], ACT.Copy).then_inc(x_hi, 1)
                splits.upto(j + 1)
            splits.upto(4)
            act.wait_ge(const_loaded, 32)
            nc.scalar.activation(idr[:, :], idf[:, :], ACT.Copy).then_inc(idr_ready, 1)
            for n, u in enumerate(IN_UNITS):
                if n == GATE_UNIT + 2:
                    z, e = reg[0:HEADS, GZ:GZ + SEQ], reg[0:HEADS, GE:GE + SEQ]
                    act.wait_ge(gates.z_ready, 1)
                    nc.scalar.activation(e, z, ACT.Abs).then_inc(gates.abs_ready, 1)
                    act.wait_ge(gates.abs_ready, 1)
                    nc.scalar.activation(e, e, ACT.Exp, scale=-1.0).then_inc(gates.exp_ready, 1)
                    act.wait_ge(gates.exp_ready, 1)
                    nc.scalar.activation(e, e, ACT.Ln, bias=1.0).then_inc(gates.ln_ready, 1)
                if n == GATE_UNIT + 4:
                    act.wait_ge(gates.cf_ready, 1)
                    nc.scalar.activation(nc_hi, reg[0:HEADS, NCF:NCF + SEQ], ACT.Copy).then_inc(gates.nc_hi, 1)
                splits.upto(u.m + RING)

            def pooled():
                splits.upto(w_in.end + RING)
                act.wait_ge(pool.y_scaled, 4)
                nc.scalar.activation(xt[:, 0, 0:4, :].rearrange("p k n -> p (k n)"), htf[:, 1024:2048],
                                     ACT.Copy).then_inc(pool.hi_ready, 1)

            attention(att1, WIDTH // P, WIDTH // P, w_in.end, pooled)
            norm(n0, squares=False)
            fused(mlp, f_mlp, relu_gate, N)
            norm(n1)
            fused(ffa, f_ffa, silu_gate(ffa, f_ffa, n1), 256)
            norm(n2, first=True)

            def relus(g):
                act.wait_ge(idx.rel_ready, g + 1)
                if g >= 2:
                    act.wait_ge(idx.rel_used, g - 1)
                keys = 4 * P * (GROUPS[g][0] + 1)
                nc.scalar.activation(by_head(hlf[:, g % 2, 0:keys]), scores_of(g), ACT.Relu, scale=DI ** -0.5)\
                  .then_inc(idx.relu_ready, 1)

            for n, u in enumerate(A_UNITS[:-2]):
                splits.upto(u.m + (RING if n < LAST_A - 3 else 2))
                if n in INDEX_AFTER:
                    relus(INDEX_AFTER[n])
            attention(att2, D // P, 0, a_in.end, lambda: None)
            norm(n3)
            fused(ffb, f_ffb, silu_gate(ffb, f_ffb, n3), 256)
            norm(n4)
            fused(ffc, f_ffc, silu_gate(ffc, f_ffc, n4), 256)
            norm(n5)
            for n, u in enumerate(B_UNITS):
                splits.upto(u.m + RING)
                v = reg[:, u.to:u.to + N]
                act.wait_ge(b_in.evac, n + 1)
                nc.scalar.activation(v, v, ACT.Gelu_apprx_tanh).then_inc(b_in.gelu_ready, 1)
            fused(mixb, f_mix, gelu_gate, N)
            norm(n6)
            fused(ffd, f_ffd, silu_gate(ffd, f_ffd, n6), 256)
            for t in range(TT):
                square(n7, t)

        @block.vector
        def _(dve):
            steps = [0]

            def step(ins):
                steps[0] += 1
                ins.then_inc(vector_step, 1)
                dve.wait_ge(vector_step, steps[0])

            def lo(m, f=None, i=0):
                dve.wait_ge(hi_done, m + 1 + (i * f.slabs if f else 0))
                nc.vector.tensor_tensor(wlo[:, m % RING, :], raw[:, m % RAW, :], whi[:, m % RING, :],
                                        ALU.subtract).then_inc(lo_done, 1)

            splits = Splits(lo, SLABS)

            def half(t, j):
                return h[:, t, j * N:(j + 1) * N]

            def vec_of(v, width=VW, start=0):
                return vec[:, v % VRING, start:start + width]

            def vec_wait(v):
                dve.wait_ge(vec_loaded[v % VRING], 16 * (v // VRING + 1))

            def tp_to_xt(ready, g, k, t, done):
                dve.wait_ge(ready, g + 1)
                nc.vector.tensor_tensor(xt[:, 1, k:k + 4, t * P:(t + 1) * P], by_head(tp[:, g % 2, :]),
                                        xt[:, 0, k:k + 4, t * P:(t + 1) * P], ALU.subtract).then_inc(done, 1)

            def layer(l, src, t, v, after=None):
                acc_done(dve, src, t)
                for j in range(2):
                    step(nc.vector.scalar_tensor_tensor(half(t, j), half(t, j), ALPHA, acc[:, 2 * t + j, :],
                                                        ALU.mult, ALU.add))
                for j in range(2):
                    step(nc.vector.bn_stats(st[:, BN + 6 * j:BN + 6 * j + 6], half(t, j)))
                nc.vector.bn_aggr(st[:, MV + 2 * t:MV + 2 * t + 2],
                                  st[:, BN:BN + 12].rearrange("p (c s) -> p c s", s=6)).then_inc(l.var_ready, 1)
                dve.wait_ge(l.var_ready, t + 1)
                vec_wait(v)
                vec_wait(v + 1)
                for j in range(2):
                    step(nc.vector.scalar_tensor_tensor(half(t, j), half(t, j), st[:, MV + 2 * t:MV + 2 * t + 1],
                                                        vec_of(v, N, j * N), ALU.subtract, ALU.mult))
                dve.wait_ge(l.rstd_ready, t + 1)
                for j in range(2):
                    ins = nc.vector.scalar_tensor_tensor(
                        half(t, j), half(t, j), st[:, LRSTD + t:LRSTD + t + 1], vec_of(v + 1, N, j * N),
                        ALU.mult, ALU.add)
                    if after is not None:
                        after(j, ins)
                return ins

            def rms(n, t, v):
                vec_wait(v)
                dve.wait_ge(n.rstd_ready, n.tiles + t + 1)
                for j in range(2):
                    nc.vector.scalar_tensor_tensor(xn_tile(t)[:, j * N:(j + 1) * N], half(t, j),
                                                   st[:, RSTD + t:RSTD + t + 1], vec_of(v, N, j * N),
                                                   ALU.mult, ALU.mult).then_inc(n.xn_ready, 1)

            def gained(n, t, j, v):
                nc.vector.tensor_tensor(xn_tile(t)[:, j * N:(j + 1) * N], half(t, j), vec_of(v, N, j * N),
                                        ALU.mult).then_inc(n.xn_ready, 1)

            def add_acc(n, src, t, factor, v=None):
                acc_done(dve, src, t)
                if v is not None:
                    vec_wait(v)
                for j in range(2):
                    ins = nc.vector.scalar_tensor_tensor(half(t, j), acc[:, 2 * t + j, :], factor, half(t, j),
                                                         ALU.mult, ALU.add)
                    if j == 0 and v is not None:
                        step(ins)
                        gained(n, t, 0, v)
                ins.then_inc(n.sum_ready, 1)
                if v is not None:
                    dve.wait_ge(n.sum_ready, n.tiles + t + 1)
                    gained(n, t, 1, v)

            def to_xt(n, t):
                for j in range(2):
                    tp_to_xt(n.hi_ready, n.halves + 2 * t + j, 4 * j, t, n.xt_ready)

            def norm(n, src, factor, v, first=False):
                for t in range(TT):
                    if first:
                        add_acc(n, src, t, factor)
                        rms(n, t, v)
                    else:
                        add_acc(n, src, t, factor, v)
                    to_xt(n, t)

            def fused(stg, f, unit, width):
                def hidden_lo(c, t, i):
                    dve.wait_ge(stg.hl_hi, 2 * c + t + 1 + i * 2 * f.period)
                    nc.vector.tensor_tensor(hl[:, t, 1, 0:width], hid[:, t * N:t * N + width],
                                            hl[:, t, 0, 0:width], ALU.subtract).then_inc(stg.hl_ready, 1)

                def chunk(c, i):
                    m = f.up[c] + f.lead
                    for j in range(f.s - 1):
                        lo(m + j, f, i)
                    unit(c, 0, i)
                    hidden_lo(c, 0, i)
                    lo(m + f.s - 1, f, i)
                    unit(c, 1, i)
                    hidden_lo(c, 1, i)

                splits.upto(f.start - 1)
                unit(0, 0, 0)
                hidden_lo(0, 0, 0)
                splits.upto(f.start)
                unit(0, 1, 0)
                hidden_lo(0, 1, 0)
                last = f.chunks - 1
                if unit is mixed_unit:
                    for c in range(1, last):
                        chunk(c, 0)
                else:
                    turns(dve, f, 1, chunk)
                splits.next = f.up[last] + f.lead
                splits.upto(f.up[last] + f.lead + f.s - 1)
                unit(last, 0, 0)
                hidden_lo(last, 0, 0)
                splits.upto(f.up[last] + f.lead + f.s)
                unit(last, 1, 0)
                hidden_lo(last, 1, 0)
                splits.upto(stg.end + 4 - f.rows)

            def gated_unit(stg, f):
                def unit(c, t, i):
                    dve.wait_ge(stg.gate_ready, 2 * c + t + 1 + i * 2 * f.period)
                    x = hid[:, t * N:t * N + 256]
                    nc.vector.scalar_tensor_tensor(x, mm[:, t, 256:512], st[:, RSTD + t:RSTD + t + 1], x,
                                                   ALU.mult, ALU.mult).then_inc(stg.hid_ready, 1)
                return unit

            def squared_unit(c, t, i):
                dve.wait_ge(mlp.gate_ready, 2 * c + t + 1 + i * 2 * f_mlp.period)
                x = hid[:, t * N:(t + 1) * N]
                nc.vector.scalar_tensor_tensor(x, mm[:, t, :], 0.0, x, ALU.max, ALU.mult)\
                  .then_inc(mlp.hid_ready, 1)

            def mixed_unit(c, t, i):
                if c == 0 and t == 0:
                    normalize_v(0, 0)
                    normalize_v(0, 1)
                v = 14 + 3 * (c // 2)
                vec_wait(v)
                unit_done(dve, mixb, f_mix, c, t, 0)
                if c > 0:
                    dve.wait_ge(mixb.hl_ready, 2 * c + t - 1)
                x = hid[:, t * N:(t + 1) * N]
                nc.vector.scalar_tensor_tensor(x, mm[:, 0, :], st[:, RSTD + t:RSTD + t + 1],
                                               vec_of(v, N, (c % 2) * N), ALU.mult, ALU.add)\
                  .then_inc(mixb.unit_taken, 1)
                dve.wait_ge(mixb.gate_ready, 2 * c + t + 1)
                dve.wait_ge(mixb.mix_ready, 2 * c + t + 1)
                for g, a, b in mix_pieces(c):
                    y = hid[:, t * N + a:t * N + b]
                    ins = nc.vector.scalar_tensor_tensor(y, mm[:, 1, a:b], st[:, BSP + g:BSP + g + 1], y,
                                                         ALU.add, ALU.mult)
                ins.then_inc(mixb.hid_ready, 1)
                if c + 1 < f_mix.chunks:
                    normalize_v(c + 1, t)

            def normalize_v(c, t):
                v = 12 + 3 * (c // 2)
                vec_wait(v)
                vec_wait(v + 1)
                dve.wait_ge(vln.rstd_ready, t + 1)
                x = reg[:, VB + t * HALF_B + c * N:VB + t * HALF_B + (c + 1) * N]
                step(nc.vector.scalar_tensor_tensor(x, x, st[:, MV + 2 * t:MV + 2 * t + 1],
                                                    vec_of(v, N, (c % 2) * N), ALU.subtract, ALU.mult))
                nc.vector.scalar_tensor_tensor(x, x, st[:, LRSTD + t:LRSTD + t + 1],
                                               vec_of(v + 1, N, (c % 2) * N), ALU.mult, ALU.add)\
                  .then_inc(vln.done, 1)

            def attention(a, width, tiles, base, end, post, between, filler):
                def maxima(g):
                    t, hh = GROUPS[g]
                    dve.wait_ge(a.sc_ready, g + 1)
                    s = scores_of(g)
                    post(g, s)
                    if g >= 2:
                        dve.wait_ge(a.p_ready, g - 1)
                    mx, neg = st[:, MX:MX + 4], st[:, NEG + 4 * (g % 2):NEG + 4 * (g % 2) + 4]
                    step(nc.vector.tensor_reduce(mx, s, AX_X, ALU.max))
                    if a is att1:
                        cq = st[:, CQ + 8 * t + 4 * hh:CQ + 8 * t + 4 * hh + 4]
                        step(nc.vector.tensor_tensor(mx, mx, cq, ALU.add))
                        nc.vector.tensor_tensor(neg, cq, mx, ALU.subtract).then_inc(a.bias_ready, 1)
                    else:
                        nc.vector.tensor_scalar(neg, mx, -1.0, None, ALU.mult).then_inc(a.bias_ready, 1)

                def scaled(g):
                    dve.wait_ge(a.pv_ready, g + 1)
                    r = RS + 4 * g
                    step(nc.vector.reciprocal(st[:, REC:REC + 4], st[:, r:r + 4]))
                    if g == 2:
                        dve.wait_ge(a.xtp_ready, tiles // 4)
                    hh = GROUPS[g][1]
                    nc.vector.tensor_tensor(by_head(att[:, hh * 4 * width:(hh + 1) * 4 * width]),
                                            by_head(mm[:, g % 2, 0:4 * width]),
                                            spread(st[:, REC:REC + 4], [[1, 4], [0, width]]), ALU.mult)\
                      .then_inc(a.att_ready, 1)
                    dve.wait_ge(a.att_ready, g + 1)

                def turned(t):
                    for j in range(tiles // 4):
                        tp_to_xt(a.hi_ready, tiles // 4 * t + j, base + 4 * j, t, a.xt_ready)

                maxima(0)
                maxima(1)
                splits.upto(end + 1)
                between()
                splits.upto(end + 2)
                if a is att1:
                    maxima(2)
                scaled(0)
                scaled(1)
                if a is att2:
                    maxima(2)
                turned(0)
                filler()
                maxima(3)
                splits.upto(end + 4)
                scaled(2)
                scaled(3)
                turned(1)
                splits.upto(end + RING)

            def evacuate(stg, n, u):
                dve.wait_ge(*u.wait)
                if u.kind == "wide" and stg is w_in:
                    nc.vector.tensor_scalar(reg[0:HEADS, GZ:GZ + SEQ], mm[0:HEADS, n % 2, 0:SEQ],
                                            st[0:HEADS, BF:BF + 1], None, ALU.add).then_inc(gates.z_ready, 1)
                    return
                if u.kind == "wide":
                    nc.vector.tensor_copy(reg[:, KI:KI + SEQ], mm[:, n % 2, 0:SEQ])
                    nc.vector.tensor_scalar(st[:, WI:WI + 16], mm[:, n % 2, SEQ:SEQ + 16],
                                            HEADS ** -0.5, None, ALU.mult).then_inc(stg.evac, 1)
                    return
                queries = stg is a_in and n in (QI_UNIT - 1, QI_UNIT)
                to = hid[:, u.i * N:(u.i + 1) * N] if queries else reg[:, u.to:u.to + N]
                if u.factor is None:
                    ins = nc.vector.tensor_copy(to, mm[:, n % 2, :])
                else:
                    ins = nc.vector.tensor_scalar(to, mm[:, n % 2, :], u.factor, None, ALU.mult)
                ins.then_inc(stg.evac, 1)

            for j in range(2):
                k = slice(4 * j, 4 * j + 4)
                dve.wait_ge(x_hi, j + 1)
                nc.vector.tensor_tensor(xt[:, 1, k, :].rearrange("p k n -> p (k n)"), hlf[:, j, :],
                                        xt[:, 0, k, :].rearrange("p k n -> p (k n)"), ALU.subtract)\
                  .then_inc(x_lo, 1)
                splits.upto(j + 1)
            step(nc.vector.memset(reg[0:HEADS, ONES:ONES + SEQ], 1.0))
            dve.wait_ge(small_loaded, 6 * 16)
            for n, u in enumerate(IN_UNITS[:-1]):
                splits.upto(u.m + 4)
                evacuate(w_in, n, u)
                splits.upto(u.m + RING - 1)
                if n == GATE_UNIT + 3:
                    z, e = reg[0:HEADS, GZ:GZ + SEQ], reg[0:HEADS, GE:GE + SEQ]
                    cf = reg[0:HEADS, CF:CF + SEQ]
                    dve.wait_ge(gates.ln_ready, 1)
                    step(nc.vector.scalar_tensor_tensor(z, z, 0.0, e, ALU.min, ALU.subtract))
                    step(nc.vector.tensor_tensor_scan(cf, reg[0:HEADS, ONES:ONES + SEQ], z, 0.0,
                                                      ALU.mult, ALU.add))
                    nc.vector.tensor_scalar(reg[0:HEADS, NCF:NCF + SEQ], cf, -1.0, None, ALU.mult)\
                      .then_inc(gates.cf_ready, 1)
                    dve.wait_ge(gates.nc_hi, 1)
                    nc.vector.tensor_tensor(nc_lo, reg[0:HEADS, NCF:NCF + SEQ], nc_hi, ALU.subtract)\
                      .then_inc(gates.nc_ready, 1)
                if n == len(IN_UNITS) - 2:
                    dve.wait_ge(table_ready, 1)
                    nc.vector.tensor_copy(reg[0:HEADS, TABLE:TABLE + DISTS], tp[0:HEADS, 1, 0:DISTS])\
                      .then_inc(table_copied, 1)
                    dve.wait_ge(gates.cq_ready, 1)
                    step(nc.vector.tensor_copy(st[:, CQ:CQ + 16], tp[:, 0, 0:16]))
            dve.wait_ge(const_loaded, 32)

            def mask_diagonal(g, s):
                keys = P * (GROUPS[g][0] + 1)
                d = s[:, :, keys - P:keys]
                step(nc.vector.tensor_tensor(d, d, spread(causal[:, :], [[0, 4], [1, P]]), ALU.add))

            def pooled():
                evacuate(w_in, len(IN_UNITS) - 1, IN_UNITS[-1])
                for p in range(2):
                    dve.wait_ge(pool.d_ready, p + 1)
                    nc.vector.tensor_copy(htf[:, p * N:(p + 1) * N], mm[:, p, :]).then_inc(pool.d_copied, 1)
                for p in range(2):
                    dve.wait_ge(pool.y_ready, p + 1)
                    for q in range(2):
                        g = 2 * p + q
                        nc.vector.tensor_scalar(htf[:, D + g * SEQ:D + (g + 1) * SEQ],
                                                mm[:, p, q * SEQ:(q + 1) * SEQ],
                                                st[:, PSC + g:PSC + g + 1], None, ALU.mult)\
                          .then_inc(pool.y_scaled, 1)
                dve.wait_ge(pool.hi_ready, 1)
                nc.vector.tensor_tensor(xt[:, 1, 0:4, :].rearrange("p k n -> p (k n)"), htf[:, D:2 * D],
                                        xt[:, 0, 0:4, :].rearrange("p k n -> p (k n)"), ALU.subtract)\
                  .then_inc(pool.xt_ready, 1)

            attention(att1, DH1, WIDTH // P, WIDTH // P, w_in.end, mask_diagonal, pooled,
                      lambda: None)
            dve.wait_ge(h_loaded, 16 * TT)
            for t in range(TT):
                layer(l0, w_out, t, 0, lambda j, ins: ins.then_inc(n0.xn_ready, 1))
                to_xt(n0, t)
            fused(mlp, f_mlp, squared_unit, N)

            for t in range(TT):
                layer(l1, mlp, t, 2).then_inc(n1.sum_ready, 1)
                dve.wait_ge(n1.sum_ready, n1.tiles + t + 1)
                vec_wait(4)
                for j in range(2):
                    gained(n1, t, j, 4)
                to_xt(n1, t)
            fused(ffa, f_ffa, gated_unit(ffa, f_ffa), 256)
            norm(n2, ffa, 0.5, 5, first=True)

            def index(g):
                t, hh = GROUPS[g]
                keys = P * (t + 1)
                score = reg[:, SCORE:SCORE + keys]
                dve.wait_ge(idx.relu_ready, g + 1)
                for i in range(4):
                    rel = hlf[:, g % 2, i * keys:(i + 1) * keys]
                    w = WI + 8 * t + 4 * hh + i
                    if hh == 0 and i == 0:
                        step(nc.vector.tensor_scalar(score, rel, st[:, w:w + 1], 0.0, ALU.mult, ALU.add))
                    elif i < 3:
                        step(nc.vector.scalar_tensor_tensor(score, rel, st[:, w:w + 1], score,
                                                            ALU.mult, ALU.add))
                    else:
                        nc.vector.scalar_tensor_tensor(score, rel, st[:, w:w + 1], score, ALU.mult, ALU.add)\
                          .then_inc(idx.rel_used, 1)
                        dve.wait_ge(idx.rel_used, g + 1)

            def select(t, part):
                keys = P * (t + 1)
                score, sel = reg[:, SCORE:SCORE + keys], reg[:, SEL + t * SEQ:SEL + t * SEQ + keys]
                if part == 0:
                    diagonal = reg[:, SCORE + keys - P:SCORE + keys]
                    step(nc.vector.tensor_tensor(diagonal, diagonal, causal[:, :], ALU.add))
                for r in range(TOPK // 16):
                    step(nc.vector.max(out=st[:, TOP:TOP + 8], in_=score))
                    step(nc.vector.match_replace(out=score, in_to_replace=st[:, TOP:TOP + 8],
                                                 in_values=score, imm_value=TAKEN))
                if part == 0:
                    return
                step(nc.vector.tensor_scalar(sel, score, TAKEN / 2, MASKED, ALU.is_gt, ALU.mult))
                diagonal = reg[:, SEL + t * SEQ + keys - P:SEL + t * SEQ + keys]
                step(nc.vector.tensor_tensor(diagonal, diagonal, causal[:, :], ALU.add))

            for n, u in enumerate(A_UNITS[:-2]):
                evacuate(a_in, n, u)
                splits.upto(u.m + (RING if n < LAST_A - 3 else 2))
                if n in INDEX_AFTER:
                    index(INDEX_AFTER[n])
                if n in SELECT_AFTER:
                    select(*SELECT_AFTER[n])
            dve.wait_ge(bias_loaded, 16)

            def bias_and_select(g, s):
                t, hh = GROUPS[g]
                keys = P * (t + 1)
                bias = htf[:, :].rearrange("p (i n) -> p i n", i=HEADS)[:, 4 * hh:4 * hh + 4, SEQ - keys:SEQ]
                step(nc.vector.scalar_tensor_tensor(s, s, DH2 ** -0.5, bias, ALU.mult, ALU.add))
                sel = reg[:, SEL + t * SEQ:SEL + t * SEQ + keys]
                step(nc.vector.tensor_tensor(s, s, spread(sel, [[0, 4], [1, keys]]), ALU.add))

            attention(att2, DH2, D // P, 0, a_in.end, bias_and_select,
                      lambda: evacuate(a_in, LAST_A - 1, A_UNITS[LAST_A - 1]),
                      lambda: evacuate(a_in, LAST_A, A_UNITS[LAST_A]))
            norm(n3, a_out, 1.0, 6)
            fused(ffb, f_ffb, gated_unit(ffb, f_ffb), 256)
            norm(n4, ffb, 0.5, 7)
            fused(ffc, f_ffc, gated_unit(ffc, f_ffc), 256)
            norm(n5, ffc, 0.5, 8)

            def stats(n):
                u = B_UNITS[n]
                dve.wait_ge(b_in.gelu_ready, n + 1)
                at = BN + 36 * u.i + 6 * (n // 2)
                return nc.vector.bn_stats(st[:, at:at + 6], reg[:, u.to:u.to + N])

            for n, u in enumerate(B_UNITS):
                vec_wait(9 + n // 4)
                dve.wait_ge(*u.wait)
                if n < 2:
                    dve.wait_ge(n5.rstd_ready, n5.tiles + n + 1)
                nc.vector.scalar_tensor_tensor(reg[:, u.to:u.to + N], mm[:, n % 2, :],
                                               st[:, RSTD + u.i:RSTD + u.i + 1],
                                               vec_of(9 + n // 4, N, (n // 2 % 2) * N), ALU.mult, ALU.add)\
                  .then_inc(b_in.evac, 1)
                splits.upto(u.m + RING)
                if n > 0:
                    stats(n - 1)
            step(stats(len(B_UNITS) - 1))
            for t in range(TT):
                nc.vector.bn_aggr(st[:, MV + 2 * t:MV + 2 * t + 2],
                                  st[:, BN + 36 * t:BN + 36 * t + 36].rearrange("p (c s) -> p c s", s=6))\
                  .then_inc(vln.var_ready, 1)
            fused(mixb, f_mix, mixed_unit, N)
            norm(n6, mixb, 1.0, 21)
            fused(ffd, f_ffd, gated_unit(ffd, f_ffd), 256)
            for t in range(TT):
                add_acc(n7, ffd, t, 0.5)
                rms(n7, t, 22)

        @block.tensor
        def _(pe):
            def product(out, a, b, first, last):
                nc.tensor.matmul(out, a[0], b[0], start=first, stop=False)
                nc.tensor.matmul(out, a[0], b[1], start=False, stop=False)
                return nc.tensor.matmul(out, a[1], b[0], start=False, stop=last)

            def x_tile(k, t):
                return [xt[:, i, k, t * P:(t + 1) * P] for i in range(2)]

            def x_all(k):
                return [xt[:, i, k, :] for i in range(2)]

            def col(m, k, start=0, n=N):
                return [w[:, m % RING, k * N + start:k * N + start + n] for w in (whi, wlo)]

            def row(m, k, half):
                return [w[:, m % RING, k * D + half * N:k * D + (half + 1) * N] for w in (whi, wlo)]

            def wide(m, k, start, n):
                return [w[:, m % RING, k * SEQ + start:k * SEQ + start + n] for w in (whi, wlo)]

            def token_unit(bank, m, t, last, ready, shift=0, between=None):
                for k in range(KD):
                    for at, do in between or ():
                        if k == at:
                            do()
                    if k % 4 == 0:
                        pe.wait_ge(lo_done, m + k // 4 + 1 + shift)
                    ins = product(mm[:, bank, :], x_tile(k, t), col(m + k // 4, k % 4), k == 0, k == KD - 1)
                    if last and k % 4 == 3:
                        ins.then_inc(slab_used, 1)
                if not last:
                    ins.then_inc(ready, 1)

            def project(stg, n, u, between=None):
                if n >= 2:
                    if stg is not w_in or n - 2 < GATE_UNIT:
                        pe.wait_ge(stg.evac, n - 1)
                    elif n - 2 == GATE_UNIT:
                        pe.wait_ge(gates.z_ready, 1)
                    else:
                        pe.wait_ge(stg.evac, n - 2)
                if u.kind == "tokens":
                    token_unit(n % 2, u.m, u.i, u.last, stg.unit_ready, between=between)
                elif u.kind == "turned":
                    for j in range(2):
                        for k in range(KD):
                            if k % 4 == 0:
                                pe.wait_ge(lo_done, u.m + k // 4 + 1)
                            ins = product(mm[:, n % 2, j * SEQ:(j + 1) * SEQ],
                                          col(u.m + k // 4, k % 4, (2 * u.i + j) * P, P), x_all(k),
                                          k == 0, k == KD - 1)
                            if u.last and j == 1 and k % 4 == 3:
                                ins.then_inc(slab_used, 1)
                    if not u.last:
                        ins.then_inc(stg.unit_ready, 1)
                else:
                    pe.wait_ge(lo_done, u.m + 1)
                    for k in range(KD):
                        ins = product(mm[:, n % 2, 0:SEQ], wide(u.m, k, 0, P), x_all(k), k == 0, k == KD - 1)
                    if stg is a_in:
                        for t in range(TT):
                            for k in range(KD):
                                ins = product(mm[:, n % 2, SEQ + 8 * t:SEQ + 8 * t + 8], x_tile(k, t),
                                              wide(u.m, k, P, 8), k == 0, k == KD - 1)
                    ins.then_inc(slab_used, 1)

            def out_slab(stg, t, j):
                n = stg.end - stg.first
                m = stg.first + j
                if t == 0:
                    pe.wait_ge(lo_done, m + 1)
                for k in range(2):
                    for half in range(2):
                        ins = product(acc[:, 2 * t + half, :], x_tile(2 * j + k, t), row(m, k, half),
                                      j == 0 and k == 0, j == n - 1 and k == 1)
                if t == 1:
                    ins.then_inc(slab_used, 1)
                elif j == n - 1:
                    ins.then_inc(stg.acc_ready, 1)

            def turn_norm(n, t, src=None):
                src = xn_tile(t) if src is None else src
                for j in range(2):
                    g = 2 * t + j
                    pe.wait_ge(n.xn_ready, n.halves + g + 1)
                    if g >= 2:
                        pe.wait_ge(n.xt_ready, n.halves + g - 1)
                    for k in range(4):
                        ins = nc.tensor.transpose(tp[:, g % 2, k * P:(k + 1) * P],
                                                  src[:, (4 * j + k) * P:(4 * j + k + 1) * P], idf[:, :])
                    ins.then_inc(n.tp_ready, 1)

            def tile_halves(n, t):
                return [(4 * j, lambda j=j: pe.wait_ge(n.xt_ready, n.halves + 2 * t + j + 1))
                        for j in range(2)]

            def fused(stg, f, norm, following=None, source=None, spatial=None, at=4):
                def up(c, t, i, between=None):
                    if c > 0 and spatial is None:
                        pe.wait_ge(stg.hid_ready, 2 * c + t - 1 + i * 2 * f.period)
                    if 2 * c + t > 0 and spatial is not None:
                        pe.wait_ge(stg.unit_taken, 2 * c + t)
                    token_unit(t if spatial is None else 0, f.up[c], t, t == 1, stg.unit_ready, i * f.slabs,
                               between)
                    if spatial is not None:
                        spatial(c, t)

                def turn(c, t, i):
                    pe.wait_ge(stg.hl_ready, 2 * c + t + 1 + i * 2 * f.period)
                    for j in range(f.rows):
                        g = f.rows * (2 * c + t) + j
                        if g >= 2:
                            pe.wait_ge(stg.ht_ready, g - 1 + i * 2 * f.rows * f.period)
                        for part in range(2):
                            for q in range(2):
                                ins = nc.tensor.transpose(
                                    tp[:, g % 2, (2 * part + q) * P:(2 * part + q + 1) * P].bitcast(F32R),
                                    hl[:, t, part, (2 * j + q) * P:(2 * j + q + 1) * P], idr[:, :])
                        ins.then_inc(stg.tp_ready, 1)

                def down(c, t, i, place=None):
                    place = t if place is None else place
                    pe.wait_ge(stg.ht_ready, f.rows * (2 * c + t + 1) + i * 2 * f.rows * f.period)
                    for q in range(f.tiles):
                        if following is not None and (c, t, q) == (f.chunks - 1, 1, f.tiles - 1):
                            following()
                        m = f.down[c] + q // 2
                        if q % 2 == 0:
                            pe.wait_ge(lo_done, m + 1 + i * f.slabs)
                        for half in range(2):
                            ins = product(acc[:, 2 * t + half, :], [ht[:, place, part, q, :] for part in range(2)],
                                          row(m, q % 2, half), c == 0 and q == 0,
                                          c == f.chunks - 1 and q == f.tiles - 1)
                        if t == 1 and q % 2 == 1:
                            ins.then_inc(slab_used, 1)
                    if c == f.chunks - 1 and t == 0:
                        ins.then_inc(stg.acc_ready, 1)

                def chunk(c, i):
                    up(c, 0, i)
                    turn(c - 1, 1, i)
                    down(c - 1, 0, i)
                    up(c, 1, i)
                    turn(c, 0, i)
                    down(c - 1, 1, i)

                if norm is None:
                    up(0, 0, 0)
                    up(0, 1, 0)
                else:
                    up(0, 0, 0, tile_halves(norm, 0) + [(at, lambda: turn_norm(norm, 1, source))])
                    if at == KD:
                        turn_norm(norm, 1, source)
                    up(0, 1, 0, tile_halves(norm, 1))
                turn(0, 0, 0)
                chunk(1, 0)
                last = f.chunks - 1
                if spatial is None:
                    turns(pe, f, 2, chunk)
                else:
                    for c in range(2, last):
                        chunk(c, 0)
                up(last, 0, 0)
                turn(last - 1, 1, 0)
                down(last - 1, 0, 0)
                turn(last, 0, 0)
                up(last, 1, 0)
                down(last, 0, 0)
                turn(last, 1, 0)
                down(last - 1, 1, 0)
                down(last, 1, 0, place=0)

            def attention(a, score, value, width, out, between, filler, following, v_ready):
                tiles = HEADS * width // P

                def scores(g):
                    t, hh = GROUPS[g]
                    if g >= 2:
                        pe.wait_ge(a.p_ready, g - 1)
                    for i in range(4):
                        if a is att1 and (g, i) == (3, 3):
                            turn_att(0)
                        ins = score(scores_of(g)[:, i, :], t, 4 * hh + i, P * (t + 1))
                    ins.then_inc(a.sc_ready, 1)

                def turn_probs(g):
                    t, hh = GROUPS[g]
                    pe.wait_ge(a.p_ready, g + 1)
                    for kb in range(t + 1):
                        n = key_blocks(g) + kb
                        if n >= 2:
                            pe.wait_ge(a.pt_ready, n - 1)
                        if g == 2 and kb < tiles // 4:
                            pe.wait_ge(a.xt_ready, kb + 1)
                        for i in range(4):
                            p = place_of(g) + (i * (t + 1) + kb) * P
                            ins = nc.tensor.transpose(tp[:, n % 2, i * P:(i + 1) * P], hid[:, p:p + P],
                                                      idf[:, :])
                        ins.then_inc(a.tp_ready, 1)

                def values(g):
                    t, hh = GROUPS[g]
                    pe.wait_ge(a.pt_ready, key_blocks(g) + t + 1)
                    v_ready(g)
                    if g >= 2:
                        pe.wait_ge(a.att_ready, g - 1)
                    for i in range(4):
                        for kb in range(t + 1):
                            p = place_of(g) + kb * N + i * P
                            ins = nc.tensor.matmul(mm[:, g % 2, i * width:(i + 1) * width], ptf[:, p:p + P],
                                                   value(kb, 4 * hh + i), start=kb == 0, stop=kb == t)
                    ins.then_inc(a.pv_ready, 1)

                def turn_att(t):
                    pe.wait_ge(a.att_ready, 2 * t + 2)
                    for j in range(tiles // 4):
                        g = tiles // 4 * t + j
                        if g >= 2:
                            pe.wait_ge(a.xt_ready, g - 1)
                        for k in range(4):
                            ins = nc.tensor.transpose(tp[:, g % 2, k * P:(k + 1) * P],
                                                      att[:, (4 * j + k) * P:(4 * j + k + 1) * P], idf[:, :])
                        ins.then_inc(a.xtp_ready, 1)

                scores(0)
                if a is att2:
                    pe.wait_ge(a_in.evac, LAST_A - 1)
                scores(1)
                between()
                turn_probs(0)
                turn_probs(1)
                scores(2)
                values(0)
                values(1)
                scores(3)
                filler(lambda: turn_att(0))
                if a is att1:
                    pe.wait_ge(pool.xt_ready, 1)
                turn_probs(2)
                pe.wait_ge(a.xt_ready, tiles // 4)
                out_slab(out, 0, 0)
                values(2)
                turn_probs(3)
                out_slab(out, 0, 1)
                values(3)
                out_slab(out, 0, 2)
                turn_att(1)
                out_slab(out, 0, 3)
                if a is att2:
                    pe.wait_ge(a.xt_ready, tiles // 4 + 1)
                out_slab(out, 1, 0)
                out_slab(out, 1, 1)
                pe.wait_ge(a.xt_ready, tiles // 2)
                out_slab(out, 1, 2)
                following()
                out_slab(out, 1, 3)

            for j in range(2):
                pe.wait_ge(x_lo, j + 1)
                pe.wait_ge(lo_done, j + 1)
                for t in range(TT):
                    for k in range(4 * j, 4 * j + 4):
                        ins = product(mm[:, t, :], x_tile(k, t), col(j, k % 4), k == 0, k == KD - 1)
                    if t == 1:
                        ins.then_inc(slab_used, 1)
                    elif j == 1:
                        ins.then_inc(w_in.unit_ready, 1)
            for n, u in enumerate(IN_UNITS[:-1]):
                if n >= 2:
                    project(w_in, n, u)
            pe.wait_ge(small_loaded, 6 * 16)
            nc.tensor.matmul(tp[0:HEADS, 1, 0:DISTS], reg[0:BUCKETS, REL:REL + HEADS],
                             reg[0:BUCKETS, BUCK:BUCK + DISTS], start=True, stop=True).then_inc(table_ready, 1)
            pe.wait_ge(gates.cf_ready, 1)
            pe.wait_ge(const_loaded, 32)
            for t in range(TT):
                ins = nc.tensor.transpose(tp[:, 0, 8 * t:8 * t + 8], reg[0:HEADS, CF + t * P:CF + (t + 1) * P],
                                          idf[0:HEADS, 0:HEADS])
            ins.then_inc(gates.cq_ready, 1)
            pe.wait_ge(w_in.evac, len(IN_UNITS) - 3)
            pe.wait_ge(gates.nc_ready, 1)
            pe.wait_ge(idr_ready, 1)

            def score1(out, t, head, keys):
                r, c = half_of(head)
                nc.tensor.matmul(out, reg[r:r + 64, QT1 + c + t * P:QT1 + c + (t + 1) * P],
                                 reg[r:r + 64, KT1 + c:KT1 + c + keys], start=True, stop=False)
                pick = spread(idr[0:HEADS, head:head + 1], [[0, P]])
                nc.tensor.matmul(out, pick, nc_hi[:, 0:keys], start=False, stop=False)
                return nc.tensor.matmul(out, pick, nc_lo[:, 0:keys], start=False, stop=True)

            def pooled():
                project(w_in, len(IN_UNITS) - 1, IN_UNITS[-1])
                pe.wait_ge(bands_loaded, 16)
                pe.wait_ge(w_in.evac, len(IN_UNITS) - 1)
                band = h[:, :, :].rearrange("p t d -> p (t d)")

                def banded(out, t, kind, g, first, last):
                    b = (4 * kind + g) * P
                    return nc.tensor.matmul(out, reg[:, U1 + t * N + g * P:U1 + t * N + (g + 1) * P],
                                            band[:, b:b + P], start=first, stop=last)

                for p in range(2):
                    for q in range(2):
                        g, o = 2 * p + q, q * SEQ
                        banded(mm[:, p, o:o + P], 0, 0, g, True, True)
                        banded(mm[:, p, o + P:o + SEQ], 1, 1, g, True, False)
                        ins = banded(mm[:, p, o + P:o + SEQ], 0, 2, g, False, True)
                    ins.then_inc(pool.d_ready, 1)
                for p in range(2):
                    pe.wait_ge(pool.d_copied, p + 1)
                    for q in range(2):
                        g = 2 * p + q
                        ins = nc.tensor.matmul(mm[:, p, q * SEQ:(q + 1) * SEQ],
                                               reg[:, POOLW + g * P:POOLW + (g + 1) * P],
                                               htf[:, g * SEQ:(g + 1) * SEQ], start=True, stop=True)
                    ins.then_inc(pool.y_ready, 1)
                pe.wait_ge(pool.y_scaled, 4)

            attention(att1, score1, lambda kb, head: reg[:, V1 + kb * N + head * DH1:
                                                         V1 + kb * N + (head + 1) * DH1],
                      DH1, w_out, pooled, lambda turn: None, lambda: turn_norm(n0, 0, h[:, 0, :]),
                      lambda g: None)
            pe.wait_ge(idr_ready, 1)
            fused(mlp, f_mlp, n0, lambda: turn_norm(n1, 0), h[:, 1, :], at=KD)

            fused(ffa, f_ffa, n1, at=KD)
            turn_norm(n2, 0)

            def index_scores(g):
                t, hh = GROUPS[g]
                if g == 0:
                    pe.wait_ge(a_in.evac, QI_UNIT + 1)
                if g >= 2:
                    pe.wait_ge(idx.relu_ready, g - 1)
                keys = P * (t + 1)
                for i in range(4):
                    head = 4 * hh + i
                    r, c = half_of(head)
                    ins = nc.tensor.matmul(scores_of(g)[:, i, :],
                                           hid[r:r + 64, c + t * P:c + (t + 1) * P],
                                           reg[r:r + 64, KI:KI + keys], start=True, stop=True)
                ins.then_inc(idx.rel_ready, 1)

            for n, u in enumerate(A_UNITS[:-2]):
                project(a_in, n, u, tile_halves(n2, 0) + [(6, lambda: turn_norm(n2, 1))] if n == 0
                        else tile_halves(n2, 1) if n == 1 else None)
                if n in INDEX_AFTER:
                    index_scores(INDEX_AFTER[n])
            pe.wait_ge(a_in.evac, LAST_A - 3)
            pe.wait_ge(idx.relu_ready, 4)

            def score2(out, t, head, keys):
                c = head * SEQ
                return nc.tensor.matmul(out, reg[:, QT2 + c + t * P:QT2 + c + (t + 1) * P],
                                        reg[:, KT2 + c:KT2 + c + keys], start=True, stop=True)

            def v_tile0():
                project(a_in, LAST_A - 1, A_UNITS[LAST_A - 1])

            def v_tile1(turn):
                pe.wait_ge(att2.att_ready, 1)
                project(a_in, LAST_A, A_UNITS[LAST_A], [(4, turn)])

            def v_ready(g):
                pe.wait_ge(a_in.evac, LAST_A + (g >= 2))

            attention(att2, score2, lambda kb, head: reg[:, V2 + kb * D + head * DH2:
                                                         V2 + kb * D + (head + 1) * DH2],
                      DH2, a_out, v_tile0, v_tile1, lambda: turn_norm(n3, 0), v_ready)
            fused(ffb, f_ffb, n3, lambda: turn_norm(n4, 0))
            fused(ffc, f_ffc, n4, lambda: turn_norm(n5, 0))
            for n, u in enumerate(B_UNITS):
                project(b_in, n, u, tile_halves(n5, 0) + [(4, lambda: turn_norm(n5, 1))] if n == 0
                        else tile_halves(n5, 1) if n == 1 else None)
            pe.wait_ge(b_in.evac, len(B_UNITS) - 1)
            pe.wait_ge(wsp_masked, 1)

            def spatial(c, t):
                pe.wait_ge(vln.done, 2 * c + t + 1)
                if 2 * c + t > 0:
                    pe.wait_ge(mixb.hid_ready, 2 * c + t)
                for g, a, b in mix_pieces(c):
                    v = VB + t * HALF_B + c * N
                    ins = nc.tensor.matmul(mm[:, 1, a:b], reg[:, WSP + g * P:WSP + (g + 1) * P],
                                           reg[:, v + a:v + b], start=True, stop=True)
                ins.then_inc(mixb.mix_ready, 1)

            fused(mixb, f_mix, None, lambda: turn_norm(n6, 0), spatial=spatial)
            fused(ffd, f_ffd, n6)


def mix_pieces(c):
    out, at = [], c * N
    while at < (c + 1) * N:
        g = at // GROUP_B
        end = min((g + 1) * GROUP_B, (c + 1) * N)
        out.append((g, at - c * N, end - c * N))
        at = end
    return out


def bands():
    s, to = np.arange(P)[:, None], np.arange(P)[None, :]
    out = np.zeros((P, 3, len(WINDOWS), P), np.float32)
    for g, w in enumerate(WINDOWS):
        back = to - s
        near = (back >= 0) & (back < w)
        out[:, 0, g] = near / np.minimum(to + 1, w) - (back == 0)
        out[:, 1, g] = near / w - (back == 0)
        out[:, 2, g] = (back + P < w) / w
    return out.reshape(P, -1)


def bucket_rows():
    d = np.maximum(SEQ - 1 - np.arange(DISTS), 0)
    half = BUCKETS // 2
    far = np.log(np.maximum(d, 1).astype(np.float32) / np.float32(half)) / np.float32(np.log(MAX_DIST / half))
    bucket = np.where(d < half, d, np.minimum(half + (far * np.float32(half)).astype(np.int32), BUCKETS - 1))
    return (np.arange(BUCKETS)[:, None] == bucket[None, :]).astype(np.float32)


def kernel(**inputs):
    import concourse.bacc as bacc
    from concourse.bass_utils import run_bass_kernel_spmd

    a = {k: np.asarray(v) for k, v in inputs.items()}
    x, w_in, w_mix = a["x"][0], a["w_in"][0], a["a_w_in_2"][0]
    q = WIDTH
    fout = 4 * WIDTH
    gate = np.zeros((D, P), w_in.dtype)
    gate[:, :HEADS] = w_in[:, fout:fout + HEADS]
    qi, ki = 3 * D, 3 * D + HEADS * DI
    key = w_mix[:, ki:ki + DI]
    index = np.concatenate([key, key, w_mix[:, ki + DI:ki + DI + HEADS]], 1)

    def ffn(l, i):
        up, down = a["ffn_w_in_2"][l, i], a["ffn_w_out_2"][l, i]
        return fused_slabs(up, down, 256, DFF2 // 256,
                           lambda c: np.r_[256 * c:256 * c + 256, DFF2 + 256 * c:DFF2 + 256 * c + 256])

    b_in = a["b_w_in_2"][0]

    def cols(w, start):
        return column_slabs(w, np.r_[start:start + N])

    def paired(w, start):
        heads = start + np.arange(HEADS * 64).reshape(2, 2, 2, 64)
        return column_slabs(w, heads.transpose(0, 2, 1, 3).reshape(-1))

    slabs = np.concatenate(
        [cols(w_in, 3 * q), wide_slab(gate), paired(w_in, q), paired(w_in, 2 * q), cols(w_in, 0),
         row_slabs(a["w_out"][0]),
         fused_slabs(a["w_mlp1"][0], a["w_mlp2"][0], 512, DFF1 // 512, lambda c: np.r_[512 * c:512 * c + 512]),
         ffn(0, 0),
         cols(w_mix, 2 * D), wide_slab(index), paired(w_mix, qi),
         cols(w_mix, 0), cols(w_mix, N), cols(w_mix, D), cols(w_mix, D + N), cols(w_mix, 2 * D + N),
         row_slabs(a["a_w_out_2"][0]), ffn(0, 1), ffn(1, 0)]
        + [cols(b_in, HALF_B + N * c) for c in range(HALF_B // N)]
        + [fused_slabs(b_in, a["b_w_out_2"][0], 512, HALF_B // 512, lambda c: np.r_[512 * c:512 * c + 512]),
           ffn(1, 1)])

    g2 = a["norm_g_2"]
    rows = {"ln1_g": a["ln1_g"][0], "ln1_b": a["ln1_b"][0], "ln2_g": a["ln2_g"][0], "ln2_b": a["ln2_b"][0],
            "final": a["final_g_2"]}
    for i in range(6):
        rows[f"norm{i}"] = g2[i // 3, i % 3]
    for j in range(3):
        part = slice(j * D, (j + 1) * D)
        rows[f"bias_u{j}"] = a["b_b_in_2"][0][:HALF_B][part]
        rows[f"bias_v{j}"] = a["b_b_in_2"][0][HALF_B:][part]
        rows[f"gate_g{j}"], rows[f"gate_b{j}"] = a["b_ln_g_2"][0][part], a["b_ln_b_2"][0][part]

    s, to = np.arange(P)[None, :], np.arange(P)[:, None]
    arrays = {
        "slabs": slabs,
        "vectors": np.stack([rows[v] for v in VECTORS]),
        "x": x,
        "x_turned": x.T.reshape(KD, P, SEQ).transpose(1, 0, 2).reshape(P, 2, 1024),
        "identity": np.eye(P, dtype=np.float32),
        "causal": np.where(s <= to, 0.0, MASKED).astype(np.float32),
        "bands": bands(),
        "buckets": bucket_rows(),
        "rel_table": a["rel_table_2"],
        "pool_w": a["pool_w"][0].transpose(1, 0, 2).reshape(P, -1),
        "pool_scale": a["pool_scale"][0].reshape(4, P).T,
        "b_f": a["b_f"][0].reshape(HEADS, 1),
        "w_sp": a["b_w_sp_2"][0].transpose(2, 0, 1).reshape(P, -1),
        "b_sp": a["b_b_sp_2"][0].T,
    }
    arrays = {k: np.ascontiguousarray(v) for k, v in arrays.items()}
    nc = bacc.Bacc("TRN2", target_bir_lowering=False, num_devices=1)
    dr = {k: nc.dram_tensor(f"{k}_dram", v.shape, F32, kind="ExternalInput").ap() for k, v in arrays.items()}
    dr["table"] = nc.dram_tensor("table_dram", [HEADS, DISTS], F32, kind="Internal").ap()
    dr["tables"] = nc.dram_tensor("tables_dram", [P, HEADS * DISTS], F32, kind="Internal").ap()
    dr["out"] = nc.dram_tensor("out_dram", [SEQ, D], F32, kind="ExternalOutput").ap()
    build(nc, dr)
    r = run_bass_kernel_spmd(nc, [{f"{k}_dram": v for k, v in arrays.items()}], core_ids=[0])
    return r.results[0]["out_dram"].reshape(1, SEQ, D)
```
